# Optimizing a Trainium2 kernel written in Bass

```python
import jax, jax.numpy as jnp
from jax import lax
import numpy as np

D_MODEL = 1024
BATCH = 1
SEQ = 256
DEPTH = 2
DEC_BATCH = 8
DEC_SEQ = 1
PAST_LEN = 2048
PAGE_SIZE = 128

D_MIX = D_MODEL
D_CONV = D_MIX // 2
D_LRU = D_MIX - D_CONV
N_LRU_HEADS = 8
LRU_HEAD_DIM = D_LRU // N_LRU_HEADS
SHORT_CONV_W = 3
LRU_CONV_W = 4
LRU_C = 8.0
D_IN = 3 * D_CONV + 2 * D_LRU
N_MEM = 256
N_MEM_HEADS = 4
MEM_HEAD_DIM = D_MODEL // N_MEM_HEADS
D_FF = 2816
N_EXPERTS = 8
TOP_K = 2
D_FF_EXPERT = 1408
N_DENSE = (DEPTH + 1) // 2
N_MOE = DEPTH // 2
EPS = 1e-6

kernel_name = 'hybrid_shortconv_rglru_xattn_moe_step'

def rms_norm(x, g):
    xf = x.astype(jnp.float32)
    y = xf * lax.rsqrt(jnp.mean(xf * xf, axis=-1, keepdims=True) + EPS)
    return (y * g.astype(jnp.float32)).astype(x.dtype)

def causal_dwconv(x, prev, w):
    width = w.shape[0]
    t_len = x.shape[1]
    xp = jnp.concatenate([prev.astype(x.dtype), x], axis=1)
    y = xp[:, 0:t_len] * w[0]
    for k in range(1, width):
        y = y + xp[:, k:k + t_len] * w[k]
    return y, xp[:, t_len:]

def rg_lru(x, h0, w_a, b_a, w_x, b_x, lam):
    bsz, t_len, _ = x.shape
    xh = x.reshape(bsz, t_len, N_LRU_HEADS, LRU_HEAD_DIM)
    ga = jnp.einsum('bthi,hij->bthj', xh, w_a).reshape(bsz, t_len, D_LRU) + b_a
    gx = jnp.einsum('bthi,hij->bthj', xh, w_x).reshape(bsz, t_len, D_LRU) + b_x
    r = jax.nn.sigmoid(ga.astype(jnp.float32))
    i = jax.nn.sigmoid(gx.astype(jnp.float32))
    log_a = -LRU_C * r * jax.nn.softplus(-lam.astype(jnp.float32))
    a = jnp.exp(log_a)
    u = jnp.sqrt(-jnp.expm1(2.0 * log_a)) * (i * x.astype(jnp.float32))

    def step(h, au):
        a_t, u_t = au
        h = a_t * h + u_t
        return h, h

    h_last, hs = lax.scan(step, h0.astype(jnp.float32), (jnp.swapaxes(a, 0, 1), jnp.swapaxes(u, 0, 1)))
    return jnp.swapaxes(hs, 0, 1).astype(x.dtype), h_last.astype(h0.dtype)

def mixer(h, conv_buf, lru_buf, lru_h, p, l):
    z = h @ p['w_in'][l]
    gb, gc, xa, xb, gate = jnp.split(z, [D_CONV, 2 * D_CONV, 3 * D_CONV, 3 * D_CONV + D_LRU], axis=-1)
    ya, new_conv_buf = causal_dwconv(gc * xa, conv_buf, p['w_short_conv'][l])
    ya = gb * ya
    xc, new_lru_buf = causal_dwconv(xb, lru_buf, p['w_lru_conv'][l])
    xc = xc + p['b_lru_conv'][l]
    yb, new_h = rg_lru(xc, lru_h, p['w_lru_a'][l], p['b_lru_a'][l], p['w_lru_x'][l], p['b_lru_x'][l], p['lru_lambda'][l])
    yb = yb * jax.nn.gelu(gate)
    y = jnp.concatenate([rms_norm(ya, p['norm_conv_out'][l]), rms_norm(yb, p['norm_lru_out'][l])], axis=-1)
    return y @ p['w_mix_out'][l], new_conv_buf, new_lru_buf, new_h

def memory_kv(mem, g_mem, w_k, w_v):
    bsz = mem.shape[0]
    m = rms_norm(mem, g_mem)
    k = (m @ w_k).reshape(bsz, N_MEM, N_MEM_HEADS, MEM_HEAD_DIM)
    v = (m @ w_v).reshape(bsz, N_MEM, N_MEM_HEADS, MEM_HEAD_DIM)
    return k, v

def cross_attn(h, k, v, w_q, w_o):
    bsz, t_len, _ = h.shape
    q = (h @ w_q).reshape(bsz, t_len, N_MEM_HEADS, MEM_HEAD_DIM)
    s = jnp.einsum('bthd,bmhd->bhtm', q, k.astype(q.dtype), preferred_element_type=jnp.float32) * (MEM_HEAD_DIM ** -0.5)
    pr = jax.nn.softmax(s, axis=-1).astype(h.dtype)
    o = jnp.einsum('bhtm,bmhd->bthd', pr, v.astype(h.dtype)).reshape(bsz, t_len, D_MODEL)
    return o @ w_o

def swiglu(h, w_gate, w_up, w_down):
    return (jax.nn.silu(h @ w_gate) * (h @ w_up)) @ w_down

def moe_swiglu(h, w_router, w_gate, w_up, w_down):
    logits = (h @ w_router).astype(jnp.float32)
    top_v, top_i = lax.top_k(logits, TOP_K)
    gates = jax.nn.softmax(top_v, axis=-1)
    combine = jnp.sum(jax.nn.one_hot(top_i, N_EXPERTS, dtype=jnp.float32) * gates[..., None], axis=-2)
    out = jnp.zeros_like(h)
    for e in range(N_EXPERTS):
        out = out + combine[..., e:e + 1].astype(h.dtype) * swiglu(h, w_gate[e], w_up[e], w_down[e])
    return out

def layer(l, x, k, v, conv_buf, lru_buf, lru_h, p):
    y, conv_buf, lru_buf, lru_h = mixer(rms_norm(x, p['norm_mix'][l]), conv_buf, lru_buf, lru_h, p, l)
    x = x + y
    x = x + cross_attn(rms_norm(x, p['norm_xattn'][l]), k, v, p['w_q'][l], p['w_o'][l])
    h = rms_norm(x, p['norm_ffn'][l])
    j = l // 2
    if l % 2 == 0:
        f = swiglu(h, p['w_ff_gate'][j], p['w_ff_up'][j], p['w_ff_down'][j])
    else:
        f = moe_swiglu(h, p['w_router'][j], p['w_moe_gate'][j], p['w_moe_up'][j], p['w_moe_down'][j])
    return x + f, conv_buf, lru_buf, lru_h

def setup_inputs(seed: int = 0) -> dict:
    key = jax.random.key(seed)
    ks = iter(jax.random.split(key, 64))
    f32 = jnp.float32

    def nrm(shape, scale):
        return scale * jax.random.normal(next(ks), shape, f32)

    def gain(shape):
        return 1.0 + 0.05 * jax.random.normal(next(ks), shape, f32)

    u = jax.random.uniform(next(ks), (DEPTH, D_LRU), f32, 0.9, 0.999)
    a_base = u ** (1.0 / LRU_C)
    lru_lambda = jnp.log(a_base) - jnp.log1p(-a_base)
    return {
        'x_prompt': nrm((BATCH, SEQ, D_MODEL), 1.0),
        'x_sample': nrm((DEC_BATCH, DEC_SEQ, D_MODEL), 1.0),
        'state_shortconv': nrm((DEPTH, DEC_BATCH, SHORT_CONV_W - 1, D_CONV), 1.0),
        'state_lru_conv': nrm((DEPTH, DEC_BATCH, LRU_CONV_W - 1, D_LRU), 1.0),
        'state_lru_h': nrm((DEPTH, DEC_BATCH, D_LRU), 0.5),
        'cache_mem_k': nrm((DEPTH, DEC_BATCH, N_MEM, N_MEM_HEADS, MEM_HEAD_DIM), 1.0),
        'cache_mem_v': nrm((DEPTH, DEC_BATCH, N_MEM, N_MEM_HEADS, MEM_HEAD_DIM), 1.0),
        'mem_prompt': nrm((BATCH, N_MEM, D_MODEL), 1.0),
        'norm_mix': gain((DEPTH, D_MODEL)),
        'w_in': nrm((DEPTH, D_MODEL, D_IN), D_MODEL ** -0.5),
        'w_short_conv': nrm((DEPTH, SHORT_CONV_W, D_CONV), SHORT_CONV_W ** -0.5),
        'w_lru_conv': nrm((DEPTH, LRU_CONV_W, D_LRU), LRU_CONV_W ** -0.5),
        'b_lru_conv': nrm((DEPTH, D_LRU), 0.02),
        'w_lru_a': nrm((DEPTH, N_LRU_HEADS, LRU_HEAD_DIM, LRU_HEAD_DIM), LRU_HEAD_DIM ** -0.5),
        'b_lru_a': nrm((DEPTH, D_LRU), 0.1),
        'w_lru_x': nrm((DEPTH, N_LRU_HEADS, LRU_HEAD_DIM, LRU_HEAD_DIM), LRU_HEAD_DIM ** -0.5),
        'b_lru_x': nrm((DEPTH, D_LRU), 0.1),
        'lru_lambda': lru_lambda,
        'norm_conv_out': gain((DEPTH, D_CONV)),
        'norm_lru_out': gain((DEPTH, D_LRU)),
        'w_mix_out': nrm((DEPTH, D_MIX, D_MODEL), D_MIX ** -0.5),
        'norm_xattn': gain((DEPTH, D_MODEL)),
        'norm_mem': gain((DEPTH, D_MODEL)),
        'w_q': nrm((DEPTH, D_MODEL, D_MODEL), D_MODEL ** -0.5),
        'w_k': nrm((DEPTH, D_MODEL, D_MODEL), D_MODEL ** -0.5),
        'w_v': nrm((DEPTH, D_MODEL, D_MODEL), D_MODEL ** -0.5),
        'w_o': nrm((DEPTH, D_MODEL, D_MODEL), D_MODEL ** -0.5),
        'norm_ffn': gain((DEPTH, D_MODEL)),
        'w_ff_gate': nrm((N_DENSE, D_MODEL, D_FF), D_MODEL ** -0.5),
        'w_ff_up': nrm((N_DENSE, D_MODEL, D_FF), D_MODEL ** -0.5),
        'w_ff_down': nrm((N_DENSE, D_FF, D_MODEL), D_FF ** -0.5),
        'w_router': nrm((N_MOE, D_MODEL, N_EXPERTS), D_MODEL ** -0.5),
        'w_moe_gate': nrm((N_MOE, N_EXPERTS, D_MODEL, D_FF_EXPERT), D_MODEL ** -0.5),
        'w_moe_up': nrm((N_MOE, N_EXPERTS, D_MODEL, D_FF_EXPERT), D_MODEL ** -0.5),
        'w_moe_down': nrm((N_MOE, N_EXPERTS, D_FF_EXPERT, D_MODEL), D_FF_EXPERT ** -0.5),
        'norm_final': gain((D_MODEL,)),
    }

def reference(x_prompt, x_sample, state_shortconv, state_lru_conv, state_lru_h, cache_mem_k, cache_mem_v,
              mem_prompt, norm_mix, w_in, w_short_conv, w_lru_conv, b_lru_conv, w_lru_a, b_lru_a,
              w_lru_x, b_lru_x, lru_lambda, norm_conv_out, norm_lru_out, w_mix_out, norm_xattn, norm_mem,
              w_q, w_k, w_v, w_o, norm_ffn, w_ff_gate, w_ff_up, w_ff_down, w_router, w_moe_gate,
              w_moe_up, w_moe_down, norm_final):
    p = dict(norm_mix=norm_mix, w_in=w_in, w_short_conv=w_short_conv, w_lru_conv=w_lru_conv,
             b_lru_conv=b_lru_conv, w_lru_a=w_lru_a, b_lru_a=b_lru_a, w_lru_x=w_lru_x, b_lru_x=b_lru_x,
             lru_lambda=lru_lambda, norm_conv_out=norm_conv_out, norm_lru_out=norm_lru_out,
             w_mix_out=w_mix_out, norm_xattn=norm_xattn, w_q=w_q, w_o=w_o, norm_ffn=norm_ffn,
             w_ff_gate=w_ff_gate, w_ff_up=w_ff_up, w_ff_down=w_ff_down, w_router=w_router,
             w_moe_gate=w_moe_gate, w_moe_up=w_moe_up, w_moe_down=w_moe_down)

    x = x_prompt
    bp = x.shape[0]
    pc, pl, ph, pk, pv = [], [], [], [], []
    for l in range(DEPTH):
        k, v = memory_kv(mem_prompt, norm_mem[l], w_k[l], w_v[l])
        x, cb, lb, hh = layer(l, x, k, v,
                              jnp.zeros((bp, SHORT_CONV_W - 1, D_CONV), x.dtype),
                              jnp.zeros((bp, LRU_CONV_W - 1, D_LRU), x.dtype),
                              jnp.zeros((bp, D_LRU), x.dtype), p)
        pc.append(cb); pl.append(lb); ph.append(hh); pk.append(k); pv.append(v)
    y_prompt = rms_norm(x, norm_final)

    x = x_sample
    sc, sl, sh = [], [], []
    for l in range(DEPTH):
        x, cb, lb, hh = layer(l, x, cache_mem_k[l], cache_mem_v[l],
                              state_shortconv[l], state_lru_conv[l], state_lru_h[l], p)
        sc.append(cb); sl.append(lb); sh.append(hh)
    y_sample = rms_norm(x, norm_final)

    return (y_prompt, y_sample, jnp.stack(pc), jnp.stack(pl), jnp.stack(ph), jnp.stack(pk), jnp.stack(pv),
            jnp.stack(sc), jnp.stack(sl), jnp.stack(sh))


_drawn_inputs = setup_inputs


def setup_inputs(seed=0):
    import zlib

    import numpy as np

    out = dict(_drawn_inputs(seed))
    spreads = {}
    factors = {'norm_xattn': 8.0}
    for name, (base, spread) in spreads.items():
        noise = np.random.default_rng([zlib.crc32(name.encode()), seed]).standard_normal(out[name].shape)
        drawn = base * np.exp(spread * noise) if base else spread * noise
        out[name] = __import__('jax').numpy.asarray(drawn.astype(out[name].dtype))
    for name, factor in factors.items():
        out[name] = (out[name] * factor).astype(out[name].dtype)
    return out
```

```python
import concourse.bass as bass
from concourse import mybir
from contextlib import ExitStack
import numpy as np

D = 1024
KT = D // 128
SEQ, DEC = 256, 8
T = SEQ + DEC
DEPTH = 2
G = 4
NZ = 20
MEM = 256
MT = MEM // 128
HEADS, HT = 4, 2
FF, FFT = 2816, 22
E, FE = 8, 1408
FET = FE // 128
EPS = 1e-6
RAWS = 4
CW = 2816
DW = 2048
GQ, DQ = 352, 256
TT = ((0, 128), (128, 128), (256, 8))
PAIR_CHUNKS = 24

PH = {"k": (0, 4), "v": (4, 4), "in": (8, 10), "mix": (18, 4), "q": (22, 4), "o": (26, 4)}
LAYER_CHUNKS = 30
FFN_CHUNKS = 30
LAYER0 = (0, LAYER_CHUNKS + FFN_CHUNKS)
GU0, DOWN0 = LAYER_CHUNKS, LAYER_CHUNKS + 22
MOE0 = LAYER0[1] + LAYER_CHUNKS

ZL, ZG, ZC, ZX, ZB = 0, 4, 8, 12, 16

_w = dict(g_mix=8, g_x=8, g_mem=8, g_ffn=8, g_fin=8, w_sc=12, w_lc=16, b_lc=4, b_a=4, b_x=4, lam=4,
          g_co=4, g_lo=4, st_sc=64, st_lc=96, st_h=32)
PK = {}
_at = 0
for _k, _n in _w.items():
    PK[_k] = _at
    _at += _n
NPK = _at
OC = dict(p_sc=0, p_lc=2, p_h=5, s_sc=6, s_lc=22, s_h=46)
NOC = 54


def build(nc, x_in, mem_in, pk_in, dense_in, gu_in, down_in, moe_in, lru_in, router_in, kc_in, vc_in,
          y_out, k_out, v_out, small_out):
    f32, f32r, bf16, i32, u32 = (mybir.dt.float32, mybir.dt.float32r, mybir.dt.bfloat16,
                                 mybir.dt.int32, mybir.dt.uint32)
    ALU, ACT, AX = mybir.AluOpType, mybir.ActivationFunctionType, mybir.AxisListType
    ctx = ExitStack()
    with ctx:
        def sb(name, shape, dt=f32):
            return ctx.enter_context(nc.sbuf_tensor(name, shape, dt))

        def sem(name):
            return ctx.enter_context(nc.semaphore(name))

        raw = sb("raw", [128, RAWS, CW])
        whi = [sb(f"whi{i}", [128, CW], f32r) for i in range(2)]
        wlo = [sb(f"wlo{i}", [128, CW], f32r) for i in range(2)]
        x = sb("x", [128, KT, T])
        a_hi = sb("a_hi", [128, KT, T], f32r)
        a_lo = sb("a_lo", [128, KT, T], f32r)
        pk = sb("pk", [128, DEPTH, NPK])
        ones = sb("ones", [128, 128])
        ident = sb("ident", [128, 128])
        eye8 = sb("eye8", [128, 8, 8])
        epsb = sb("epsb", [128, 1])
        sml = sb("sml", [128, G, NOC])
        nsp = sb("nsp", [128, DEPTH, 2, G])
        spt = sb("spt", [128, 4, DEPTH, G])
        rt = sb("rt", [128, T])
        rstd = sb("rstd", [128, T])
        stat = sb("stat", [128, 64])
        area = sb("area", [128, 22400])
        probe = nc.sbuf_base
        base = probe - 22400 * 4

        def at(name, offset, shape, dt=f32):
            size = int(np.prod(shape[1:])) * (2 if dt == bf16 else 4)
            assert offset + size <= 22400 * 4, name
            return nc.alloc_sbuf_tensor_at(name, shape, dt, offset=base + offset)

        m_hi = at("m_hi", 0, [128, KT, MEM], f32r)
        m_lo = at("m_lo", 8192, [128, KT, MEM], f32r)
        lru_w = at("lru_w", 0, [128, 2, G, 128])
        memn = at("memn", 16384, [128, KT, MEM])
        kt = at("kt", 24576, [128, KT, MEM])
        vt = at("vt", 32768, [128, MT, D])
        z = at("z", 40960, [128, NZ, T])
        sq = at("sq", 40960, [128, KT, T])
        tmp = [at(f"tmp{i}", 62080 + 4224 * i, [128, G, T]) for i in range(6)]
        xc, rg, ig, av, th, hs = tmp
        hf = at("hf", 71040, [128, KT, T])
        qt = at("qt", 40960, [128, KT, T])
        ring = [at(f"ring{i}", 49408 + 8192 * i, [128, DW]) for i in range(2)]
        qm = at("qm", 65792, [128, KT, DEC, 8])
        pr = [at(f"pr{i}", 67840 + 2048 * i, [128, 2, MEM]) for i in range(2)]
        ptr = [at(f"ptr{i}", 71936 + 2048 * i, [128, MT, SEQ]) for i in range(2)]
        ps_s = at("ps_s", 76032, [8, HEADS, MEM])
        ptm = at("ptm", 80128, [128, MT, HEADS, DEC, 8])
        o_s = at("o_s", 82176, [8, D])
        h_hi = at("h_hi", 24576, [128, FFT, T], f32r)
        h_lo = at("h_lo", 47808, [128, FFT, T], f32r)
        sg = [at(f"sg{i}", 71040 + 1056 * i, [128, T]) for i in range(2)]
        hff = [at(f"hff{i}", 73152 + 1056 * i, [128, T]) for i in range(2)]
        ht_hi = at("ht_hi", 0, [128, 3, D], f32r)
        ht_lo = at("ht_lo", 12288, [128, 3, D], f32r)
        wr_hi = at("wr_hi", 24576, [128, KT, 128], f32r)
        wr_lo = at("wr_lo", 28672, [128, KT, 128], f32r)
        xg_hi = at("xg_hi", 24576, [128, KT, 256], f32r)
        xg_lo = at("xg_lo", 32768, [128, KT, 256], f32r)
        oh = at("oh", 40960, [128, 3, 256], f32r)
        oht = at("oht", 44032, [128, 2, T], f32r)
        sgm = at("sgm", 46144, [128, FE])
        hm = at("hm", 51776, [128, FE])
        hx_hi = at("hx_hi", 57408, [128, FET, 128], f32r)
        hx_lo = at("hx_lo", 63040, [128, FET, 128], f32r)
        y_hi = at("y_hi", 68672, [128, 2, D], f32r)
        y_lo = at("y_lo", 76864, [128, 2, D], f32r)
        lg = at("lg", 85056, [128, T])
        rw = at("rw", 86112, [128, KT, E])
        iot = at("iot", 86368, [128, 128])
        iot_i = at("iot_i", 86880, [128, 128], i32)
        iot8 = at("iot8", 87392, [128, E])
        lt = at("lt", 87424, [128, 3, E])
        top = at("top", 87520, [128, 3, 8])
        topi = at("topi", 87616, [128, 3, 8], u32)
        topf = at("topf", 87712, [128, 3, 8])
        m1 = at("m1", 87808, [128, 3, E])
        m2 = at("m2", 87904, [128, 3, E])
        comb = at("comb", 88000, [128, 3, E])
        msk = at("msk", 88096, [128, 3, E], bf16)
        rk = at("rk", 88160, [128, 3, E])
        gt = at("gt", 88256, [128, 3, 4])
        tri = at("tri", 88320, [128, 128], bf16)
        one_b = at("one_b", 88576, [128, 128], bf16)
        cnt = at("cnt", 88832, [128, 8])
        cnt_i = at("cnt_i", 88864, [128, 8], i32)
        valid = at("valid", 88928, [128, 3, E])
        gs = at("gs", 88896, [128, 2])

        ps = ctx.enter_context(nc.psum_tensor("ps", [128, 8, 512], f32))

        raw_full = [sem(f"raw_full{i}") for i in range(RAWS)]
        hi_done, lo_done, pe_done, evac = sem("hi_done"), sem("lo_done"), sem("pe_done"), sem("evac")
        s_par, s_x, s_mem, s_lruw, s_small, s_kv, s_y, s_rw = (sem(n) for n in (
            "params_in", "x_in", "mem_in", "lru_w_in", "small_out", "kv_out", "y_out", "router_in"))
        consts, dve_c = sem("consts"), sem("dve_chain")
        n_sq, n_ss, n_rt, n_h, n_hi, n_lo = (sem(n) for n in (
            "norm_squares", "norm_sum", "norm_root", "norm_scaled", "norm_hi", "norm_lo"))
        xc_done, gates_mm, gates_act, gate_a, u_w, u_sq = (sem(n) for n in (
            "xc_done", "gates_mm", "gates_act", "lru_a_done", "lru_w_done", "lru_root"))
        gelu_done, sm_done, lruw_zero = sem("gelu_done"), sem("small_ready"), sem("lru_w_zero")
        sc_mm, sc_max, sc_exp, sc_nrm, pt_mm, pt_cp, ov_mm, at_hi, at_lo = (sem(n) for n in (
            "score_mm", "score_max", "score_exp", "probs_ready", "probs_t_mm", "probs_t_ready", "attn_mm",
            "attn_hi", "attn_lo"))
        q_ready, qm_ready, ss_mm, ss_max, ss_exp, ss_nrm, st_mm, st_cp, so_mm, so_cp, sot_mm = (sem(n) for n in (
            "q_ready", "qm_ready", "s_score_mm", "s_score_max", "s_score_exp", "s_probs_ready", "s_probs_t_mm",
            "s_probs_t_ready", "s_attn_mm", "s_attn_copied", "s_attn_t_mm"))
        ring_full = [sem(f"ring_full{i}") for i in range(2)]
        ring_used = sem("ring_used")
        silu_done, ff_h = sem("silu_done"), sem("ff_h_ready")
        tk_mm, tk_cp, wr_ready, lg_mm, lg_cp, lt_mm, rk_in, rk_mm, route = (sem(n) for n in (
            "tok_major_mm", "tok_major_copied", "router_split", "logits_mm", "logits_copied", "logits_t_mm",
            "rank_in", "rank_mm", "routed"))
        tk_cl, g_in, g_exp, sp_in, sp_exp, ya_done, gs_cp = (sem(n) for n in (
            "tok_major_copied_lo", "gate_diff", "gate_exp", "softplus_in", "softplus_exp", "ya_ready", "slot_gate_ready"))
        oh_ready, ga_mm, ga_hi, ga_lo, oht_mm, oht_cp, gs_mm = (sem(n) for n in (
            "onehot_ready", "gather_mm", "gather_hi", "gather_lo", "onehot_t_mm", "onehot_t_ready", "slot_gate_mm"))
        m_silu, m_h, hx_mm, hx_h, hx_l, y_h, y_l, scat_mm, scat_add = (sem(n) for n in (
            "moe_silu", "moe_h", "moe_ht_mm", "moe_ht_hi", "moe_ht_lo", "moe_y_hi", "moe_y_lo", "scatter_mm",
            "scatter_added"))

        class Chain:

            def __init__(self, eng, s):
                self.eng, self.sem, self.n, self.off = eng, s, 0, 0

            def __call__(self, ins):
                ins.then_inc(self.sem, 1)
                self.n += 1

            def wait(self):
                self.eng.wait_ge(self.sem, self.n + self.off)

        NORMS = ["mem", "mix0", "co0", "lo0", "xattn0", "ffn0", "mix1", "co1", "lo1", "xattn1", "ffn1", "fin"]
        order = {name: i for i, name in enumerate(NORMS)}

        block = ctx.enter_context(nc.Block())

        def nh_of(name, k):
            n = 0
            for q in ["m0", "mix0", "g0", "xattn0", "m1", "ffn0", "mix1", "g1", "xattn1", "ffn1", "fin"]:
                if q == name:
                    return n + k
                n += 8
            raise KeyError(name)

        def nhi_of(name, k):
            return 4 * SPLITS.index(name) + k

        SPLITS = ["m0", "mix0", "g0", "xattn0", "m1", "ffn0", "mix1", "g1", "xattn1", "ffn1"]
        nlo = {name: i + 1 for i, name in enumerate(SPLITS)}

        @block.sync
        def _(sp):
            def load(src, n, k, width):
                if not isinstance(n, int) or n >= RAWS:
                    sp.wait_ge(lo_done, n - (RAWS - 1))
                sp.dma_start(raw[:, k % RAWS, 0:width], src).then_inc(raw_full[k % RAWS], 16)

            def dense(l, first, count):
                n0 = LAYER0[l] + first
                for j in range(count):
                    load(dense_in[l, first + j], n0 + j, n0 + j, DW)

            def looped(src, n0, count, width):
                full = count // RAWS
                with sp.Fori(0, full) as i:
                    for u in range(RAWS):
                        load(src(i * RAWS + u), i * RAWS + (n0 + u), n0 + u, width)
                for j in range(full * RAWS, count):
                    load(src(j), n0 + j, n0 + j, width)

            sp.dma_start(pk[:], pk_in).then_inc(s_par, 16)
            sp.dma_start(memn[:], mem_in).then_inc(s_mem, 16)
            sp.dma_start(x[:], x_in).then_inc(s_x, 16)
            for l in range(DEPTH):
                if l == 0:
                    dense(0, 0, RAWS)
                    looped(lambda j: dense_in[0, j + RAWS], RAWS, LAYER_CHUNKS - RAWS, DW)
                    looped(lambda j: gu_in[j], GU0, FFN_CHUNKS - 8, DW)
                    looped(lambda j: down_in[j], DOWN0, 8, CW)
                else:
                    looped(lambda j: dense_in[1, j], LAYER0[1], LAYER_CHUNKS, DW)
            for u in range(RAWS):
                load(moe_in[u], MOE0 + u, MOE0 + u, CW)
            sp.wait_ge(route, 1)
            rounds = sp.value_load(cnt_i[0:1, 0:1], min_val=1, max_val=3)
            with sp.Fori(0, rounds) as r:
                with sp.Fori(0, 3) as p:
                    for u in range(RAWS, RAWS + PAIR_CHUNKS):
                        load(moe_in[p * PAIR_CHUNKS + u], r * 96 + p * 24 + (MOE0 + u), MOE0 + u, CW)
                for u in range(72 + RAWS, 96 + RAWS):
                    load(moe_in[u % 96], r * 96 + (MOE0 + u), MOE0 + u, CW)
            sp.wait_ge(n_h, nh_of("fin", 8))
            sp.dma_start(y_out, hf[:]).then_inc(s_y, 16)
            sp.wait_ge(s_y, 16)

        @block.gpsimd
        def _(pool):
            pool.memset(ones[:], 1.0).then_inc(consts, 1)
            pool.memset(ident[:], 0.0).then_inc(consts, 1)
            pool.memset(eye8[:], 0.0).then_inc(consts, 1)
            pool.memset(epsb[:], EPS).then_inc(consts, 1)
            pool.wait_ge(consts, 4)
            pool.affine_select(out=ident[:], in_=ident[:], compare_op=ALU.not_equal, fill=1.0, base=0,
                               pattern=[[-1, 128]], channel_multiplier=1).then_inc(consts, 1)
            pool.affine_select(out=eye8[:], in_=eye8[:], compare_op=ALU.not_equal, fill=1.0, base=0,
                               pattern=[[1, 8], [-1, 8]], channel_multiplier=0).then_inc(consts, 1)
            for l in range(DEPTH):
                pool.wait_ge(pe_done, LAYER0[l] + 8)
                pool.memset(lru_w[:], 0.0).then_inc(lruw_zero, 1)
                pool.wait_ge(lruw_zero, l + 1)
                for m in range(2):
                    for half in range(2):
                        q = slice(64 * half, 64 * half + 64)
                        pool.dma_start(lru_w[q, m, :, q], lru_in[l, m, half]).then_inc(s_lruw, 16)
                pool.wait_ge(sm_done, l + 1)
                pool.dma_start(small_out[l], sml[:]).then_inc(s_small, 16)
                pool.wait_ge(evac, LAYER0[l] + 8)
                pool.dma_start(k_out[l], kt[:]).then_inc(s_kv, 16)
                pool.dma_start(v_out[l], vt[:]).then_inc(s_kv, 16)
                pool.wait_ge(n_ss, order[f"xattn{l}"] + 1)
                for c in range(16):
                    g = 16 * l + c
                    if g >= 2:
                        pool.wait_ge(ring_used, g - 1)
                    src = kc_in[l, c] if c < 8 else vc_in[l, c - 8]
                    pool.dma_start(ring[c % 2][:], src).then_inc(ring_full[c % 2], 16)
            pool.wait_ge(n_lo, nlo["ffn1"])
            pool.iota(iot_i[:], pattern=[[1, 128]], base=0, channel_multiplier=0).then_inc(consts, 1)
            pool.memset(one_b[:], 1.0).then_inc(consts, 1)
            pool.memset(wr_hi[:].bitcast(f32), 0.0).then_inc(consts, 1)
            pool.memset(wr_lo[:].bitcast(f32), 0.0).then_inc(consts, 1)
            pool.memset(valid[:], 1.0).then_inc(consts, 1)
            pool.wait_ge(consts, 11)
            pool.affine_select(out=valid[:, 2], in_=valid[:, 2], compare_op=ALU.is_gt, fill=0.0, base=DEC,
                               pattern=[[0, E]], channel_multiplier=-1).then_inc(consts, 1)
            pool.affine_select(out=tri[:], in_=one_b[:], compare_op=ALU.is_gt, fill=0.0, base=0,
                               pattern=[[1, 128]], channel_multiplier=-1).then_inc(consts, 1)
            pool.dma_start(rw[:], router_in).then_inc(s_rw, 16)
            pool.wait_ge(s_small, 16 * DEPTH)
            pool.wait_ge(s_kv, 32 * DEPTH)

        @block.scalar
        def _(act):
            def hi(n, k, width):
                act.wait_ge(raw_full[k % RAWS], 16 * (k // RAWS + 1) if isinstance(n, int)
                            else (n - (k % RAWS)) * (16 // RAWS) + 16)
                if not isinstance(n, int) or n >= 2:
                    act.wait_ge(pe_done, n - 1)
                act.activation(whi[k % 2][:, 0:width], raw[:, k % RAWS, 0:width], ACT.Copy).then_inc(hi_done, 1)

            def width_of(k):
                return CW if DOWN0 <= k < LAYER0[1] or k >= MOE0 else DW

            def ahead(n0, count, body=None):
                full = count // RAWS
                if full > 1:
                    with act.Fori(0, full) as i:
                        for u in range(RAWS):
                            if body:
                                body(i * RAWS + u, i * RAWS + (n0 + u), u)
                            hi(i * RAWS + (n0 + u + 2), n0 + u + 2, width_of(n0 + u + 2))
                else:
                    full = 0
                for j in range(full * RAWS, count):
                    if body:
                        body(j, n0 + j, j)
                    if n0 + j + 2 < MOE0 + 2:
                        hi(n0 + j + 2, n0 + j + 2, width_of(n0 + j + 2))

            def norm_stats(name, src, tiles, scale, out=sq[:]):
                act.activation(out, src, ACT.Square).then_inc(n_sq, 1)
                norm_root(name, scale)

            def norm_root(name, scale):
                act.wait_ge(n_ss, order[name] + 1)
                act.activation(rt[:, 0:MEM if name == "mem" else T], ps[:, 4, 0:MEM if name == "mem" else T],
                               ACT.Sqrt, bias=epsb[:, 0:1], scale=scale).then_inc(n_rt, 1)

            def norm_hi(name, src, dst):
                for k in range(0, KT, 2):
                    act.wait_ge(n_h, nh_of(name, k + 2))
                    act.activation(dst[:, k:k + 2], src[:, k:k + 2], ACT.Copy).then_inc(n_hi, 1)

            def attn_hi(l, h):
                c = HEADS * l + h
                act.wait_ge(ov_mm, c + 1)
                act.activation(a_hi[:, HT * h:HT * h + 2, 0:SEQ], ps[:, 2 + h % 2, :].rearrange(
                    "p (a t) -> p a t", a=2), ACT.Copy).then_inc(at_hi, 1)

            hi(0, 0, DW)
            hi(1, 1, DW)
            act.wait_ge(sp_in, 1)
            act.activation(spt[:, 1], spt[:, 0], ACT.Exp, scale=-1.0).then_inc(sp_exp, 1)
            act.wait_ge(consts, 6)
            act.wait_ge(s_mem, 16)
            norm_stats("mem", memn[:], KT, 1.0 / D, sq[:, :, 0:MEM])
            norm_hi("m0", hf[:, :, 0:MEM], m_hi)
            act.wait_ge(s_x, 16)
            for l in range(DEPTH):
                L = LAYER0[l]
                P = pk[:, l, :]
                ahead(L, 4)
                act.wait_ge(n_lo, nlo["m0"] if l == 0 else nlo["ffn0"])
                if l == 1:
                    act.wait_ge(evac, L)
                norm_stats(f"mix{l}", x[:], KT, 1.0 / D)
                norm_hi(f"mix{l}", hf, a_hi)
                ahead(L + 4, 4)
                ahead(L + 8, 10)
                for t in range(G):
                    act.wait_ge(gates_mm, G * l + t + 1)
                    act.activation(rg[:, t], ps[:, 4 + 2 * (t % 2), 0:T], ACT.Sigmoid,
                                   bias=P[:, PK["b_a"] + t:PK["b_a"] + t + 1]).then_inc(gates_act, 1)
                    act.activation(ig[:, t], ps[:, 5 + 2 * (t % 2), 0:T], ACT.Sigmoid,
                                   bias=P[:, PK["b_x"] + t:PK["b_x"] + t + 1]).then_inc(gates_act, 1)
                act.wait_ge(gates_act, 2 * G * (l + 1))
                act.wait_ge(evac, L + 18)
                for t in range(G):
                    act.activation(av[:, t], rg[:, t], ACT.Exp, scale=nsp[:, l, 0, t:t + 1])
                    act.activation(th[:, t], rg[:, t], ACT.Tanh, scale=nsp[:, l, 1, t:t + 1]).then_inc(gate_a, 1)
                act.activation(z[:, ZG:ZG + G], z[:, ZG:ZG + G], ACT.Gelu_apprx_tanh).then_inc(gelu_done, 1)
                act.wait_ge(u_w, 2 * l + 1)
                act.activation(th[:], th[:], ACT.Sqrt).then_inc(u_sq, 1)
                act.wait_ge(ya_done, l + 1)
                act.activation(xc[:], z[:, ZX:ZX + G], ACT.Square).then_inc(n_sq, 1)
                norm_root(f"co{l}", 1.0 / 512)
                act.wait_ge(u_w, 2 * l + 2)
                act.wait_ge(n_h, nh_of(f"g{l}", 1))
                act.activation(ig[:], hs[:], ACT.Square).then_inc(n_sq, 1)
                norm_root(f"lo{l}", 1.0 / 512)
                for k in range(0, KT, 2):
                    act.wait_ge(n_h, nh_of(f"g{l}", k + 2))
                    src = z[:, ZX + k:ZX + k + 2] if k < G else hs[:, k - G:k - G + 2]
                    act.activation(a_hi[:, k:k + 2], src, ACT.Copy).then_inc(n_hi, 1)
                ahead(L + 18, 4)
                act.wait_ge(evac, L + 22)
                norm_stats(f"xattn{l}", x[:], KT, 1.0 / D)
                norm_hi(f"xattn{l}", hf, a_hi)
                ahead(L + 22, 4)
                for h in range(HEADS):
                    c = HEADS * l + h
                    act.wait_ge(sc_max, c + 1)
                    for t in range(2):
                        act.activation(pr[h % 2][:, t], ps[:, 4 + h % 2, t * MEM:(t + 1) * MEM], ACT.Exp,
                                       bias=stat[:, 2 * h + t:2 * h + t + 1],
                                       accum_out=stat[:, 16 + 2 * h + t:17 + 2 * h + t]).then_inc(sc_exp, 1)
                    if h:
                        attn_hi(l, h - 1)
                    if h == HEADS - 1:
                        attn_hi(l, h)
                act.wait_ge(ss_max, l + 1)
                for h in range(HEADS):
                    act.activation(ps_s[:, h], ps[0:8, h, 0:MEM], ACT.Exp, bias=stat[0:8, 32 + h:33 + h],
                                   accum_out=stat[0:8, 40 + h:41 + h]).then_inc(ss_exp, 1)
                act.wait_ge(sot_mm, l + 1)
                act.activation(a_hi[:, :, SEQ:T], ps[:, 5, 0:64].rearrange("p (k b) -> p k b", b=8),
                               ACT.Copy).then_inc(at_hi, 1)
                ahead(L + 26, 4)
                if l == 0:
                    norm_hi("m1", hf[:, :, 0:MEM], m_hi)
                act.wait_ge(evac, L + 30)
                norm_stats(f"ffn{l}", x[:], KT, 1.0 / D)
                norm_hi(f"ffn{l}", hf, a_hi)
                if l == 0:
                    def silu(j, n, u):
                        act.wait_ge(pe_done, n + 1)
                        act.wait_ge(evac, n - 1)
                        act.activation(sg[u % 2][:], ps[:, 2 * (u % 2), 0:T], ACT.Silu).then_inc(silu_done, 1)
                    for j in range(4):
                        silu(j, GU0 + j, j)
                        hi(GU0 + j + 2, GU0 + j + 2, DW)
                    with act.Fori(0, 4) as i:
                        for u in range(4):
                            n0 = GU0 + 4 + u
                            silu(i * 4 + (4 + u), i * 4 + n0, u)
                            hi(i * 4 + (n0 + 2), n0 + 2, DW)
                    for j in range(20, 22):
                        silu(j, GU0 + j, j)
                        hi(GU0 + j + 2, GU0 + j + 2, CW)
                    ahead(DOWN0, 8)

            for i in range(6):
                act.wait_ge(tk_mm, 2 * i + 1)
                t, half = i // 2, i % 2
                w = TT[t][1]
                act.activation(ht_hi[0:w, t, half * 512:half * 512 + 512], ps[0:w, 4 + 2 * (i % 2), :],
                               ACT.Copy).then_inc(tk_cp, 1)
            act.wait_ge(g_in, 1)
            act.activation(gt[:, :, 1], gt[:, :, 0], ACT.Exp).then_inc(g_exp, 1)
            act.wait_ge(route, 1)
            rounds = act.value_load(cnt_i[0:1, 0:1], min_val=1, max_val=3)
            with act.Fori(0, rounds) as r:
                with act.Fori(0, 4) as p:
                    it = r * 4 + p
                    n = r * 96 + p * 24
                    for g in range(4):
                        act.wait_ge(ga_mm, it * 8 + (2 * g + 1))
                        act.activation(xg_hi[:, 2 * g:2 * g + 2, :], ps[:, 4 + 2 * (g % 2), :].rearrange(
                            "p (a c) -> p a c", a=2), ACT.Copy).then_inc(ga_hi, 1)
                    for e in range(2):
                        for q in range(4):
                            k = MOE0 + 12 * e + 2 * q
                            act.wait_ge(pe_done, n + (k + 1))
                            act.activation(sgm[:, q * GQ:(q + 1) * GQ], ps[:, k % 4, 0:GQ],
                                           ACT.Silu).then_inc(m_silu, 1)
                            hi(n + (k + 2), k + 2, CW)
                            hi(n + (k + 3), k + 3, CW)
                        for b in range(3):
                            w = 512 if b < 2 else 384
                            act.wait_ge(hx_mm, it * 6 + (3 * e + b + 1))
                            act.activation(hx_hi[:, 4 * b:4 * b + w // 128].rearrange("p a c -> p (a c)"),
                                           ps[:, 4 + b, 0:w], ACT.Copy).then_inc(hx_h, 1)
                        for q in range(4):
                            k = MOE0 + 12 * e + 8 + q
                            act.wait_ge(pe_done, n + (k + 1))
                            act.activation(y_hi[:, e, q * DQ:(q + 1) * DQ], ps[:, k % 4, 0:DQ], ACT.Copy,
                                           scale=gs[:, e:e + 1]).then_inc(y_h, 1)
                            hi(n + (k + 2), k + 2, CW)
            act.wait_ge(s_x, 16)
            act.wait_ge(scat_add, rounds * 32)
            norm_stats("fin", x[:], KT, 1.0 / D)

        @block.vector
        def _(dve):
            chain = Chain(dve, dve_c)

            def col(l, name, i):
                c = PK[name] + i
                return pk[:, l, c:c + 1]

            def lo(n, k, width):
                dve.wait_ge(hi_done, n + 1)
                dve.tensor_tensor(wlo[k % 2][:, 0:width], raw[:, k % RAWS, 0:width],
                                  whi[k % 2][:, 0:width].bitcast(f32), ALU.subtract).then_inc(lo_done, 1)

            def width_of(k):
                return CW if DOWN0 <= k < LAYER0[1] or k >= MOE0 else DW

            def banks(k, w):
                b = 2 * (k % 2)
                return ps[:, b:b + 2, 0:w]

            def evacs(n0, count, body):
                def one(j, n, k):
                    dve.wait_ge(pe_done, n + 1)
                    body(j, k).then_inc(evac, 1)
                    if k + 2 < MOE0 + 2:
                        lo(n + 2, k + 2, width_of(k + 2))
                full = count // RAWS
                if full > 1:
                    with dve.Fori(0, full) as i:
                        for u in range(RAWS):
                            one(i * RAWS + u, i * RAWS + (n0 + u), n0 + u)
                else:
                    full = 0
                for j in range(full * RAWS, count):
                    one(j, n0 + j, n0 + j)

            def root_reciprocal(name, w=T):
                dve.wait_ge(n_rt, order[name] + 1)
                chain(dve.reciprocal(rstd[:, 0:w], rt[:, 0:w]))
                chain.wait()

            def split_lo(name, src, dst_hi, dst_lo):
                for k in range(0, KT, 2):
                    dve.wait_ge(n_hi, nhi_of(name, k // 2 + 1))
                    ins = dve.tensor_tensor(dst_lo[:, k:k + 2], src(k), dst_hi[:, k:k + 2].bitcast(f32), ALU.subtract)
                ins.then_inc(n_lo, 1)

            def norm(name, gain, l):
                root_reciprocal(name)
                for k in range(KT):
                    dve.scalar_tensor_tensor(out=hf[:, k], in0=x[:, k], scalar=col(l, gain, k), in1=rstd[:],
                                             op0=ALU.mult, op1=ALU.mult).then_inc(n_h, 1)

            def mem_operand(l):
                for k in range(KT):
                    dve.tensor_scalar(hf[:, k, 0:MEM], memn[:, k], col(l, "g_mem", k), None, ALU.mult).then_inc(n_h, 1)
                split_lo(f"m{l}", lambda k: hf[:, k:k + 2, 0:MEM], m_hi, m_lo)

            dve.wait_ge(s_par, 16)
            lam = pk[:, :, PK["lam"]:PK["lam"] + G]
            dve.scalar_tensor_tensor(out=spt[:, 0], in0=lam, scalar=-1.0, in1=lam, op0=ALU.mult,
                                     op1=ALU.max).then_inc(sp_in, 1)
            lo(0, 0, DW)
            lo(1, 1, DW)
            dve.wait_ge(sp_exp, 1)
            chain(dve.tensor_scalar(spt[:, 2], spt[:, 1], 2.0, None, ALU.add))
            chain.wait()
            chain(dve.reciprocal(spt[:, 3], spt[:, 2]))
            chain.wait()
            chain(dve.tensor_tensor(spt[:, 0], spt[:, 1], spt[:, 3], ALU.mult))
            chain.wait()
            chain(dve.tensor_tensor(spt[:, 1], spt[:, 0], spt[:, 0], ALU.mult))
            chain.wait()
            chain(dve.tensor_scalar(spt[:, 2], spt[:, 1], 1.0 / 19, None, ALU.mult))
            for c in range(17, 1, -2):
                chain.wait()
                chain(dve.scalar_tensor_tensor(out=spt[:, 2], in0=spt[:, 2], scalar=1.0 / c, in1=spt[:, 1],
                                               op0=ALU.add, op1=ALU.mult))
            chain.wait()
            chain(dve.scalar_tensor_tensor(out=spt[:, 2], in0=spt[:, 2], scalar=1.0, in1=spt[:, 0],
                                           op0=ALU.add, op1=ALU.mult))
            chain(dve.tensor_scalar(spt[:, 3], lam, -1.0, 0.0, ALU.mult, ALU.max))
            chain.wait()
            chain(dve.scalar_tensor_tensor(out=spt[:, 2], in0=spt[:, 2], scalar=2.0, in1=spt[:, 3],
                                           op0=ALU.mult, op1=ALU.add))
            chain.wait()
            for i, c in enumerate((-8.0, 8.0)):
                chain(dve.tensor_scalar(nsp[:, :, i, :], spt[:, 2], c, None, ALU.mult))

            root_reciprocal("mem", MEM)
            chain(dve.tensor_tensor(memn[:], memn[:], rstd[:, 0:MEM].unsqueeze(1).to_broadcast([128, KT, MEM]),
                                    ALU.mult))
            chain.wait()
            mem_operand(0)

            for l in range(DEPTH):
                L = LAYER0[l]
                evacs(L, 4, lambda j, k: dve.tensor_copy(kt[:, 2 * j:2 * j + 2], banks(k, MEM)))
                norm(f"mix{l}", "g_mix", l)
                split_lo(f"mix{l}", lambda k: hf[:, k:k + 2], a_hi, a_lo)
                evacs(L + 4, 4, lambda j, k: dve.tensor_copy(vt[:, :, j * 256:j * 256 + 256], banks(k, 256)))
                evacs(L + 8, 10, lambda j, k: dve.tensor_copy(z[:, bass.ds(j * 2, 2), :], banks(k, T)))

                for t in range(G):
                    chain(dve.tensor_scalar(xc[:, t], z[:, ZL + t], col(l, "w_lc", 12 + t), col(l, "b_lc", t),
                                            ALU.mult, ALU.add))
                if l:
                    dve.wait_ge(s_small, 16)
                for tap in (2, 1, 0):
                    chain.wait()
                    s = 3 - tap
                    for t in range(G):
                        w = col(l, "w_lc", 4 * tap + t)
                        chain(dve.scalar_tensor_tensor(out=xc[:, t, s:SEQ], in0=z[:, ZL + t, 0:SEQ - s], scalar=w,
                                                       in1=xc[:, t, s:SEQ], op0=ALU.mult, op1=ALU.add))
                        c = PK["st_lc"] + 24 * t + 8 * tap
                        ins = dve.scalar_tensor_tensor(out=xc[:, t, SEQ:T], in0=pk[:, l, c:c + 8], scalar=w,
                                                       in1=xc[:, t, SEQ:T], op0=ALU.mult, op1=ALU.add)
                        if tap or t < G - 1:
                            chain(ins)
                ins.then_inc(xc_done, 1)

                st_lc = pk[:, l, PK["st_lc"]:PK["st_lc"] + 96].rearrange("p (t k) -> p t k", t=G)
                st_sc = pk[:, l, PK["st_sc"]:PK["st_sc"] + 64].rearrange("p (t k) -> p t k", t=G)
                st_h = pk[:, l, PK["st_h"]:PK["st_h"] + 32].rearrange("p (t k) -> p t k", t=G)

                def small(name, w, src, shift=0):
                    c = OC[name] + shift
                    return dve.tensor_copy(sml[:, :, c:c + w], src)

                chain(dve.tensor_tensor(z[:, ZC:ZC + G], z[:, ZC:ZC + G], z[:, ZX:ZX + G], ALU.mult))
                small("p_lc", 3, z[:, ZL:ZL + G, SEQ - 3:SEQ])
                small("s_lc", 16, st_lc[:, :, 8:24])
                small("s_lc", 8, z[:, ZL:ZL + G, SEQ:T], 16)
                small("s_sc", 8, st_sc[:, :, 8:16])
                chain.wait()
                small("p_sc", 2, z[:, ZC:ZC + G, SEQ - 2:SEQ])
                small("s_sc", 8, z[:, ZC:ZC + G, SEQ:T], 8)
                for t in range(G):
                    chain(dve.tensor_scalar(z[:, ZX + t], z[:, ZC + t], col(l, "w_sc", 8 + t), None, ALU.mult))
                for tap in (1, 0):
                    chain.wait()
                    s = 2 - tap
                    for t in range(G):
                        w = col(l, "w_sc", 4 * tap + t)
                        chain(dve.scalar_tensor_tensor(out=z[:, ZX + t, s:SEQ], in0=z[:, ZC + t, 0:SEQ - s], scalar=w,
                                                       in1=z[:, ZX + t, s:SEQ], op0=ALU.mult, op1=ALU.add))
                        c = PK["st_sc"] + 16 * t + 8 * tap
                        chain(dve.scalar_tensor_tensor(out=z[:, ZX + t, SEQ:T], in0=pk[:, l, c:c + 8], scalar=w,
                                                       in1=z[:, ZX + t, SEQ:T], op0=ALU.mult, op1=ALU.add))
                chain.wait()
                dve.tensor_tensor(z[:, ZX:ZX + G], z[:, ZX:ZX + G], z[:, ZB:ZB + G], ALU.mult).then_inc(ya_done, 1)

                dve.wait_ge(gate_a, G * (l + 1))
                chain(dve.tensor_tensor(rg[:], av[:], av[:], ALU.mult))
                chain(dve.tensor_tensor(ig[:], ig[:], xc[:], ALU.mult))
                chain.wait()
                dve.scalar_tensor_tensor(out=th[:], in0=rg[:], scalar=1.0, in1=th[:], op0=ALU.add,
                                         op1=ALU.mult).then_inc(u_w, 1)
                dve.wait_ge(u_sq, l + 1)
                chain(dve.tensor_tensor(ig[:], ig[:], th[:], ALU.mult))
                chain(dve.tensor_tensor(hs[:, :, SEQ:T], av[:, :, SEQ:T], st_h, ALU.mult))
                chain.wait()
                for t in range(G):
                    chain(dve.tensor_tensor_scan(hs[:, t, 0:SEQ], av[:, t, 0:SEQ], ig[:, t, 0:SEQ], 0.0,
                                                 ALU.mult, ALU.add))
                chain(dve.tensor_tensor(hs[:, :, SEQ:T], hs[:, :, SEQ:T], ig[:, :, SEQ:T], ALU.add))
                chain.wait()
                small("p_h", 1, hs[:, :, SEQ - 1:SEQ])
                small("s_h", 8, hs[:, :, SEQ:T]).then_inc(sm_done, 1)
                dve.wait_ge(gelu_done, l + 1)
                dve.wait_ge(sm_done, l + 1)
                dve.tensor_tensor(hs[:], hs[:], z[:, ZG:ZG + G], ALU.mult).then_inc(u_w, 1)

                for name, src, gain in ((f"co{l}", z[:, ZX:ZX + G], "g_co"), (f"lo{l}", hs, "g_lo")):
                    if gain == "g_lo":
                        dve.wait_ge(n_h, nh_of(f"g{l}", G))
                    root_reciprocal(name)
                    for k in range(G):
                        dve.scalar_tensor_tensor(out=src[:, k], in0=src[:, k], scalar=col(l, gain, k), in1=rstd[:],
                                                 op0=ALU.mult, op1=ALU.mult).then_inc(n_h, 1)
                split_lo(f"g{l}", lambda k: z[:, ZX + k:ZX + k + 2] if k < G else hs[:, k - G:k - G + 2], a_hi, a_lo)

                def add_x(j, k):
                    return dve.tensor_tensor(x[:, 2 * j:2 * j + 2], x[:, 2 * j:2 * j + 2], banks(k, T), ALU.add)

                evacs(L + 18, 4, add_x)
                norm(f"xattn{l}", "g_x", l)
                split_lo(f"xattn{l}", lambda k: hf[:, k:k + 2], a_hi, a_lo)
                evacs(L + 22, 4, lambda j, k: dve.tensor_scalar(qt[:, 2 * j:2 * j + 2], banks(k, T), 1.0 / 16, None,
                                                                ALU.mult))

                dve.wait_ge(evac, L + 26)
                dve.tensor_tensor(qm[:], qt[:, :, SEQ:T].unsqueeze(3).to_broadcast([128, KT, DEC, 8]),
                                  eye8[:].unsqueeze(1).to_broadcast([128, KT, DEC, 8]), ALU.mult).then_inc(qm_ready, 1)

                def score_max(h):
                    dve.wait_ge(sc_mm, HEADS * l + h + 1)
                    chain(dve.tensor_reduce(stat[:, 8 + 2 * (h % 2):10 + 2 * (h % 2)],
                                            ps[:, 4 + h % 2, :].rearrange("p (t m) -> p t m", t=2), AX.X, ALU.max))
                    chain.wait()
                    dve.tensor_scalar(stat[:, 2 * h:2 * h + 2], stat[:, 8 + 2 * (h % 2):10 + 2 * (h % 2)], -1.0, None,
                                      ALU.mult).then_inc(sc_max, 1)

                score_max(0)
                score_max(1)
                for h in range(HEADS):
                    c = HEADS * l + h
                    dve.wait_ge(sc_exp, 2 * c + 2)
                    chain(dve.reciprocal(stat[:, 24 + 2 * h:26 + 2 * h], stat[:, 16 + 2 * h:18 + 2 * h]))
                    chain.wait()
                    for t in range(2):
                        ins = dve.tensor_scalar(pr[h % 2][:, t], pr[h % 2][:, t], stat[:, 24 + 2 * h + t:25 + 2 * h + t],
                                                None, ALU.mult)
                    ins.then_inc(sc_nrm, 1)
                    dve.wait_ge(pt_mm, c + 1)
                    dve.tensor_copy(ptr[h % 2][:], ps[:, 6 + h % 2, :].rearrange("p (m t) -> p m t", m=2))\
                       .then_inc(pt_cp, 1)
                    if h + 2 < HEADS:
                        score_max(h + 2)
                    dve.wait_ge(at_hi, 5 * l + h + 1)
                    dve.tensor_tensor(a_lo[:, HT * h:HT * h + 2, 0:SEQ],
                                      ps[:, 2 + h % 2, :].rearrange("p (a t) -> p a t", a=2),
                                      a_hi[:, HT * h:HT * h + 2, 0:SEQ].bitcast(f32), ALU.subtract).then_inc(at_lo, 1)

                dve.wait_ge(ss_mm, l + 1)
                chain(dve.tensor_reduce(stat[0:8, 36:40], ps[0:8, 0:HEADS, 0:MEM], AX.X, ALU.max))
                chain.wait()
                dve.tensor_scalar(stat[0:8, 32:36], stat[0:8, 36:40], -1.0, None, ALU.mult).then_inc(ss_max, 1)
                dve.wait_ge(ss_exp, HEADS * (l + 1))
                chain(dve.reciprocal(stat[0:8, 44:48], stat[0:8, 40:44]))
                chain.wait()
                dve.tensor_tensor(ps_s[:], ps_s[:], stat[0:8, 44:48].unsqueeze(2).to_broadcast([8, HEADS, MEM]),
                                  ALU.mult).then_inc(ss_nrm, 1)
                dve.wait_ge(st_mm, l + 1)
                dve.tensor_tensor(ptm[:].rearrange("p m h b c -> p (m h) b c"),
                                  ps[:, 4, 0:64].rearrange("p (a b) -> p a b", b=8).unsqueeze(3)
                                  .to_broadcast([128, 8, 8, 8]),
                                  eye8[:].unsqueeze(1).to_broadcast([128, 8, 8, 8]), ALU.mult).then_inc(st_cp, 1)
                dve.wait_ge(so_mm, l + 1)
                dve.tensor_copy(o_s[:].rearrange("p (h d) -> p h d", h=HEADS), ps[0:8, 0:HEADS, 0:MEM])\
                   .then_inc(so_cp, 1)
                dve.wait_ge(at_hi, 5 * l + 5)
                dve.tensor_tensor(a_lo[:, :, SEQ:T], ps[:, 5, 0:64].rearrange("p (k b) -> p k b", b=8),
                                  a_hi[:, :, SEQ:T].bitcast(f32), ALU.subtract).then_inc(at_lo, 1)

                evacs(L + 26, 4, add_x)
                if l == 0:
                    mem_operand(1)
                norm(f"ffn{l}", "g_ffn", l)
                split_lo(f"ffn{l}", lambda k: hf[:, k:k + 2], a_hi, a_lo)
                if l == 0:
                    dve.wait_ge(s_kv, 32)

                    def gated(j, n, k, last=False):
                        dve.wait_ge(silu_done, j + 1)
                        dve.tensor_tensor(hff[k % 2][:], sg[k % 2][:], ps[:, 2 * (k % 2) + 1, 0:T],
                                          ALU.mult).then_inc(evac, 1)
                        lo(n + 2, k + 2, width_of(k + 2))
                        dve.wait_ge(evac, n + 1)
                        chain(dve.tensor_copy(h_hi[:, j, :], hff[k % 2][:]))
                        chain.wait()
                        ins = dve.tensor_tensor(h_lo[:, j, :], hff[k % 2][:], h_hi[:, j, :].bitcast(f32),
                                                ALU.subtract)
                        if last:
                            ins.then_inc(ff_h, 1)

                    with dve.Fori(0, 5) as i:
                        chain.off = i * RAWS
                        for u in range(RAWS):
                            gated(i * RAWS + u, i * RAWS + (GU0 + u), GU0 + u)
                    chain.off, chain.n = 0, chain.n + 4 * RAWS
                    gated(20, GU0 + 20, GU0 + 20)
                    gated(21, GU0 + 21, GU0 + 21, True)
                    evacs(DOWN0, 8, lambda j, k: dve.tensor_tensor(x[:, j, :], x[:, j, :], ps[:, 2 * (k % 2), 0:T],
                                                                   ALU.add))

            dve.wait_ge(consts, 13)
            dve.wait_ge(s_rw, 16)
            dve.wait_ge(n_lo, nlo["ffn1"])
            chain(dve.memset(ht_hi[:, 2].bitcast(f32), 0.0))
            chain(dve.memset(ht_lo[:, 2].bitcast(f32), 0.0))
            chain(dve.tensor_copy(wr_hi[:, :, 0:E], rw[:]))
            chain.wait()
            dve.tensor_tensor(wr_lo[:, :, 0:E], rw[:], wr_hi[:, :, 0:E].bitcast(f32), ALU.subtract).then_inc(wr_ready, 1)
            chain(dve.tensor_copy(iot[:], iot_i[:]))
            chain(dve.memset(lt[:], 0.0))
            for i in range(6):
                dve.wait_ge(tk_mm, 2 * i + 2)
                t, half = i // 2, i % 2
                w = TT[t][1]
                dve.tensor_copy(ht_lo[0:w, t, half * 512:half * 512 + 512], ps[0:w, 5 + 2 * (i % 2), :])\
                   .then_inc(tk_cl, 1)
            dve.wait_ge(lg_mm, 1)
            dve.tensor_copy(lg[0:E], ps[0:E, 0, 0:T]).then_inc(lg_cp, 1)
            dve.wait_ge(lt_mm, 1)
            chain.wait()
            for i, (c0, w) in enumerate(TT):
                chain(dve.tensor_copy(lt[0:w, i], ps[0:w, 1, i * E:(i + 1) * E]))
            chain.wait()
            for i in range(3):
                chain(dve.max(top[:, i], lt[:, i]))
            chain.wait()
            for i in range(3):
                chain(dve.max_index(topi[:, i], top[:, i], lt[:, i]))
            dve.tensor_tensor(gt[:, :, 0], top[:, :, 1], top[:, :, 0], ALU.subtract).then_inc(g_in, 1)
            chain.wait()
            chain(dve.tensor_copy(topf[:], topi[:]))
            chain.wait()
            numbers = iot[:, 0:E].unsqueeze(1).to_broadcast([128, 3, E])
            for c, m in ((0, m1), (1, m2)):
                chain(dve.tensor_tensor(m[:], numbers, topf[:, :, c:c + 1].to_broadcast([128, 3, E]), ALU.is_equal))
            chain.wait()
            for m in (m1, m2):
                chain(dve.tensor_tensor(m[:], m[:], valid[:], ALU.mult))
            chain.wait()
            dve.tensor_tensor(msk[:], m1[:], m2[:], ALU.add).then_inc(rk_in, 1)
            dve.wait_ge(g_exp, 1)
            chain(dve.tensor_scalar(gt[:, :, 2], gt[:, :, 1], 1.0, None, ALU.add))
            chain.wait()
            chain(dve.reciprocal(gt[:, :, 3], gt[:, :, 2]))
            chain.wait()
            chain(dve.tensor_tensor(gt[:, :, 2], gt[:, :, 1], gt[:, :, 3], ALU.mult))
            chain.wait()
            chain(dve.tensor_tensor(m1[:], m1[:], gt[:, :, 3:4].to_broadcast([128, 3, E]), ALU.mult))
            chain(dve.tensor_tensor(m2[:], m2[:], gt[:, :, 2:3].to_broadcast([128, 3, E]), ALU.mult))
            chain.wait()
            chain(dve.tensor_tensor(comb[:], m1[:], m2[:], ALU.add))
            dve.wait_ge(rk_mm, 1)
            chain(dve.scalar_tensor_tensor(out=rk[:], in0=ps[:, 2, 0:3 * E].rearrange("p (i e) -> p i e", i=3),
                                           scalar=1.0, in1=msk[:], op0=ALU.add, op1=ALU.mult))
            chain.wait()
            chain(dve.tensor_scalar(rk[:], rk[:], -1.0, None, ALU.add))
            chain(dve.tensor_reduce(cnt[:, 0:1], ps[:, 3, 0:E], AX.X, ALU.max))
            chain.wait()
            chain(dve.tensor_scalar(cnt[:, 1:2], cnt[:, 0:1], 128.5, 1.0, ALU.is_gt, ALU.add))
            chain(dve.tensor_scalar(cnt[:, 2:3], cnt[:, 0:1], 256.5, None, ALU.is_gt))
            chain.wait()
            dve.tensor_tensor(cnt_i[:, 0:1], cnt[:, 1:2], cnt[:, 2:3], ALU.add).then_inc(route, 1)
            dve.wait_ge(route, 1)

            rounds = dve.value_load(cnt_i[0:1, 0:1], min_val=1, max_val=3)
            with dve.Fori(0, rounds) as r:
                with dve.Fori(0, 4) as p:
                    it = r * 4 + p
                    n = r * 96 + p * 24
                    for i in range(3):
                        for e in range(2):
                            ins = dve.tensor_scalar(oh[:, i, 128 * e:128 * e + 128], iot[:],
                                                    rk[:, i, bass.ds(p * 2 + e, 1)], None, ALU.is_equal)
                    ins.then_inc(oh_ready, 1)
                    for g in range(4):
                        dve.wait_ge(ga_mm, it * 8 + (2 * g + 2))
                        dve.tensor_copy(xg_lo[:, 2 * g:2 * g + 2, :],
                                        ps[:, 5 + 2 * (g % 2), :].rearrange("p (a c) -> p a c", a=2)).then_inc(ga_lo, 1)
                    for e in range(2):
                        dve.wait_ge(oht_mm, it * 2 + (e + 1))
                        dve.tensor_copy(oht[:, e], ps[:, 6 + e, 0:T]).then_inc(oht_cp, 1)
                    dve.wait_ge(gs_mm, it + 1)
                    for e in range(2):
                        ins = dve.tensor_copy(gs[:, e:e + 1], ps[:, 4, bass.ds(p * 2 + (E * e + e), 1)])
                    ins.then_inc(gs_cp, 1)
                    for e in range(2):
                        for q in range(4):
                            k = MOE0 + 12 * e + 2 * q
                            dve.wait_ge(m_silu, it * 8 + (4 * e + q + 1))
                            dve.wait_ge(pe_done, n + (k + 2))
                            dve.tensor_tensor(hm[:, q * GQ:(q + 1) * GQ], sgm[:, q * GQ:(q + 1) * GQ],
                                              ps[:, (k + 1) % 4, 0:GQ], ALU.mult).then_inc(evac, 2)
                            lo(n + (k + 2), k + 2, CW)
                            lo(n + (k + 3), k + 3, CW)
                        for b in range(3):
                            w = 512 if b < 2 else 384
                            dve.wait_ge(hx_h, it * 6 + (3 * e + b + 1))
                            dve.tensor_tensor(hx_lo[:, 4 * b:4 * b + w // 128].rearrange("p a c -> p (a c)"),
                                              ps[:, 4 + b, 0:w],
                                              hx_hi[:, 4 * b:4 * b + w // 128].rearrange("p a c -> p (a c)").bitcast(f32),
                                              ALU.subtract).then_inc(hx_l, 1)
                        for q in range(4):
                            k = MOE0 + 12 * e + 8 + q
                            dve.wait_ge(y_h, it * 8 + (4 * e + q + 1))
                            dve.scalar_tensor_tensor(out=y_lo[:, e, q * DQ:(q + 1) * DQ], in0=ps[:, k % 4, 0:DQ],
                                                     scalar=gs[:, e:e + 1],
                                                     in1=y_hi[:, e, q * DQ:(q + 1) * DQ].bitcast(f32),
                                                     op0=ALU.mult, op1=ALU.subtract).then_inc(evac, 1)
                            lo(n + (k + 2), k + 2, CW)
                    for f in range(KT):
                        dve.wait_ge(scat_mm, it * 8 + (f + 1))
                        dve.tensor_tensor(x[:, f], x[:, f], ps[:, 4 + f % 4, 0:T], ALU.add).then_inc(scat_add, 1)
                dve.tensor_scalar(iot[:], iot[:], 128.0, None, ALU.add).then_inc(route, 1)
                dve.wait_ge(route, r + 2)
            norm("fin", "g_fin", 0)

        @block.tensor
        def _(pe):
            def mm3(out, w_hi, w_lo, m_hi_, m_lo_, first, last):
                pe.matmul(out, w_hi, m_hi_, start=first, stop=False)
                pe.matmul(out, w_hi, m_lo_, start=False, stop=False)
                return pe.matmul(out, w_lo, m_hi_, start=False, stop=last)

            def chunk(n, body, k):
                pe.wait_ge(lo_done, n + 1)
                if not isinstance(n, int) or n >= 2:
                    pe.wait_ge(evac, n - 1)
                body(k).then_inc(pe_done, 1)

            def chunks(n0, count, body):
                first = 2 if n0 == 0 else 0
                for j in range(first):
                    chunk(j, body, j)
                with pe.Fori(0, (count - first) // 2) as i:
                    for u in range(2):
                        chunk(i * 2 + (n0 + first + u), body, n0 + u)

            def proj(m_h, m_l, w):
                def body(k):
                    for s in range(2):
                        for i in range(KT):
                            c = i * 256 + s * 128
                            last = mm3(ps[:, 2 * (k % 2) + s, 0:w], whi[k % 2][:, c:c + 128], wlo[k % 2][:, c:c + 128],
                                       m_h[:, i, :], m_l[:, i, :], i == 0, i == KT - 1)
                    return last
                return body

            def values(k):
                for t in range(MT):
                    for i in range(KT):
                        m = slice(t * 128, t * 128 + 128)
                        w = slice(i * 256, i * 256 + 256)
                        last = mm3(ps[:, 2 * (k % 2) + t, 0:256], m_hi[:, i, m], m_lo[:, i, m],
                                   whi[k % 2][:, w], wlo[k % 2][:, w], i == 0, i == KT - 1)
                return last

            def down(k):
                for i in range(FFT):
                    c = i * 128
                    last = mm3(ps[:, 2 * (k % 2), 0:T], whi[k % 2][:, c:c + 128], wlo[k % 2][:, c:c + 128],
                               h_hi[:, i, :], h_lo[:, i, :], i == 0, i == FFT - 1)
                return last

            def norm_sum(name, src, tiles, w=T):
                pe.wait_ge(n_sq, order[name] + 1)
                if order[name]:
                    pe.wait_ge(n_rt, order[name])
                for i in range(tiles):
                    last = pe.matmul(ps[:, 4, 0:w], ones[:], src[:, i, 0:w], start=i == 0, stop=i == tiles - 1)
                last.then_inc(n_ss, 1)

            pe.wait_ge(consts, 6)
            norm_sum("mem", sq, KT, MEM)
            for l in range(DEPTH):
                L = LAYER0[l]
                pe.wait_ge(n_lo, nlo[f"m{l}"])
                chunks(L, 4, proj(m_hi, m_lo, MEM))
                norm_sum(f"mix{l}", sq, KT)
                chunks(L + 4, 4, values)
                pe.wait_ge(n_lo, nlo[f"mix{l}"])
                chunks(L + 8, 10, proj(a_hi, a_lo, T))
                pe.wait_ge(s_lruw, 64 * (l + 1))
                pe.wait_ge(xc_done, l + 1)
                for t in range(G):
                    if t >= 2:
                        pe.wait_ge(gates_act, 2 * G * l + 2 * t - 2)
                    for m in range(2):
                        last = pe.matmul(ps[:, 4 + 2 * (t % 2) + m, 0:T], lru_w[:, m, t], xc[:, t], start=True, stop=True)
                    last.then_inc(gates_mm, 1)
                norm_sum(f"co{l}", xc, G)
                norm_sum(f"lo{l}", ig, G)
                pe.wait_ge(n_lo, nlo[f"g{l}"])
                chunks(L + 18, 4, proj(a_hi, a_lo, T))
                norm_sum(f"xattn{l}", sq, KT)
                pe.wait_ge(n_lo, nlo[f"xattn{l}"])
                chunks(L + 22, 4, proj(a_hi, a_lo, T))

                def scores(h):
                    for t in range(2):
                        for d in range(HT):
                            last = pe.matmul(ps[:, 4 + h % 2, t * MEM:(t + 1) * MEM], qt[:, HT * h + d, t * 128:t * 128 + 128],
                                             kt[:, HT * h + d, :], start=d == 0, stop=d == HT - 1)
                    last.then_inc(sc_mm, 1)

                pe.wait_ge(evac, L + 26)
                scores(0)
                scores(1)
                for h in range(HEADS):
                    c = HEADS * l + h
                    pe.wait_ge(sc_nrm, c + 1)
                    for m in range(MT):
                        for t in range(2):
                            last = pe.transpose(ps[:, 6 + h % 2, m * SEQ + t * 128:m * SEQ + t * 128 + 128],
                                                pr[h % 2][:, t, m * 128:m * 128 + 128], ident[:])
                    last.then_inc(pt_mm, 1)
                    if h + 2 < HEADS:
                        scores(h + 2)
                    pe.wait_ge(pt_cp, c + 1)
                    if h >= 2:
                        pe.wait_ge(at_lo, 5 * l + h - 1)
                    for d in range(HT):
                        for m in range(MT):
                            last = pe.matmul(ps[:, 2 + h % 2, d * SEQ:(d + 1) * SEQ],
                                             vt[:, m, h * 256 + d * 128:h * 256 + d * 128 + 128], ptr[h % 2][:, m],
                                             start=m == 0, stop=m == MT - 1)
                    last.then_inc(ov_mm, 1)

                pe.wait_ge(qm_ready, l + 1)
                pe.wait_ge(at_lo, 5 * l + 4)
                for c in range(8):
                    pe.wait_ge(ring_full[c % 2], 16 * (8 * l + c // 2 + 1))
                    for h in range(HEADS):
                        for d in range(HT):
                            j = HT * h + d
                            last = pe.matmul(ps[0:8, h, 0:MEM], qm[:, j, c, :], ring[c % 2][:, j * MEM:(j + 1) * MEM],
                                             start=c == 0 and d == 0, stop=c == 7 and d == HT - 1)
                    last.then_inc(ring_used, 1)
                pe.wait_ge(ring_used, 16 * l + 8)
                pe.matmul(ps[0:8, 6, 0:8], ident[:, 0:8], ident[:, 0:8], start=True, stop=True).then_inc(ss_mm, 1)
                pe.wait_ge(ss_nrm, l + 1)
                for m in range(MT):
                    for h in range(HEADS):
                        c = (m * HEADS + h) * 8
                        last = pe.transpose(ps[:, 4, c:c + 8], ps_s[:, h, m * 128:m * 128 + 128], ident[0:8, 0:8])
                last.then_inc(st_mm, 1)
                pe.wait_ge(st_cp, l + 1)
                for c in range(8):
                    pe.wait_ge(ring_full[c % 2], 16 * (8 * l + 4 + c // 2 + 1))
                    for h in range(HEADS):
                        for m in range(MT):
                            o = m * D + h * 256
                            last = pe.matmul(ps[0:8, h, 0:256], ptm[:, m, h, c, :], ring[c % 2][:, o:o + 256],
                                             start=c == 0 and m == 0, stop=c == 7 and m == MT - 1)
                    last.then_inc(ring_used, 1)
                pe.matmul(ps[0:8, 6, 0:8], ident[:, 0:8], ident[:, 0:8], start=True, stop=True).then_inc(so_mm, 1)
                pe.wait_ge(so_cp, l + 1)
                for j in range(KT):
                    last = pe.transpose(ps[:, 5, j * 8:j * 8 + 8], o_s[:, j * 128:j * 128 + 128], ident[0:8, 0:8])
                last.then_inc(sot_mm, 1)
                pe.wait_ge(at_lo, 5 * l + 5)
                chunks(L + 26, 4, proj(a_hi, a_lo, T))
                norm_sum(f"ffn{l}", sq, KT)
                pe.wait_ge(n_lo, nlo[f"ffn{l}"])
                if l == 0:
                    chunks(GU0, 22, proj(a_hi, a_lo, T))
                    pe.wait_ge(ff_h, 1)
                    chunks(DOWN0, 8, down)

            for i in range(6):
                t, half = i // 2, i % 2
                c0, w = TT[t]
                if i >= 2:
                    pe.wait_ge(tk_cp, i - 1)
                    pe.wait_ge(tk_cl, i - 1)
                for part, src in enumerate((a_hi, a_lo)):
                    for f in range(4):
                        last = pe.transpose(ps[0:w, 4 + 2 * (i % 2) + part, f * 128:f * 128 + 128],
                                            src[:, 4 * half + f, c0:c0 + w].bitcast(f32), ident[:])
                    last.then_inc(tk_mm, 1)
            pe.wait_ge(wr_ready, 1)
            pe.wait_ge(evac, MOE0)
            for i in range(KT):
                last = mm3(ps[:, 0, 0:T], wr_hi[:, i], wr_lo[:, i], a_hi[:, i], a_lo[:, i], i == 0, i == KT - 1)
            last.then_inc(lg_mm, 1)
            pe.wait_ge(lg_cp, 1)
            for i, (c0, w) in enumerate(TT):
                last = pe.transpose(ps[0:w, 1, i * E:(i + 1) * E], lg[0:E, c0:c0 + w], ident[0:E, 0:E])
            last.then_inc(lt_mm, 1)
            pe.wait_ge(rk_in, 1)
            for i in range(3):
                for j in range(i + 1):
                    pe.matmul(ps[:, 2, i * E:(i + 1) * E], tri[:] if j == i else one_b[:], msk[:, j],
                              start=j == 0, stop=j == i)
            for j in range(3):
                last = pe.matmul(ps[:, 3, 0:E], one_b[:], msk[:, j], start=j == 0, stop=j == 2)
            last.then_inc(rk_mm, 1)

            pe.wait_ge(tk_cp, 6)
            pe.wait_ge(tk_cl, 6)
            pe.wait_ge(route, 1)
            rounds = pe.value_load(cnt_i[0:1, 0:1], min_val=1, max_val=3)
            ohf = oh[:].bitcast(f32)
            with pe.Fori(0, rounds) as r:
                with pe.Fori(0, 4) as p:
                    it = r * 4 + p
                    n = r * 96 + p * 24
                    pe.wait_ge(oh_ready, it + 1)
                    pe.wait_ge(scat_add, it * 8)
                    for g in range(4):
                        if g >= 2:
                            pe.wait_ge(ga_hi, it * 4 + (g - 1))
                            pe.wait_ge(ga_lo, it * 4 + (g - 1))
                        for part, src in enumerate((ht_hi, ht_lo)):
                            for a in range(2):
                                f = 2 * g + a
                                for i in range(3):
                                    last = pe.matmul(ps[:, 4 + 2 * (g % 2) + part, a * 256:a * 256 + 256],
                                                     src[:, i, f * 128:f * 128 + 128], oh[:, i, :],
                                                     start=i == 0, stop=i == 2)
                            last.then_inc(ga_mm, 1)
                    pe.wait_ge(ga_hi, it * 4 + 4)
                    pe.wait_ge(ga_lo, it * 4 + 4)
                    for e in range(2):
                        for i in range(3):
                            last = pe.transpose(ps[:, 6 + e, i * 128:i * 128 + 128], ohf[:, i, 128 * e:128 * e + 128],
                                                ident[:])
                        last.then_inc(oht_mm, 1)
                    for e in range(2):
                        for i in range(3):
                            last = pe.matmul(ps[:, 4, E * e:E * e + E], ohf[:, i, 128 * e:128 * e + 128], comb[:, i],
                                             start=i == 0, stop=i == 2)
                    last.then_inc(gs_mm, 1)

                    def expert_chunk(k, body):
                        pe.wait_ge(lo_done, n + (k + 1))
                        pe.wait_ge(evac, n + (k - 3))
                        body(k).then_inc(pe_done, 1)

                    for e in range(2):
                        def gate_up(k):
                            for i in range(KT):
                                w = slice(i * GQ, (i + 1) * GQ)
                                s = slice(128 * e, 128 * e + 128)
                                last = mm3(ps[:, k % 4, 0:GQ], xg_hi[:, i, s], xg_lo[:, i, s], whi[k % 2][:, w],
                                           wlo[k % 2][:, w], i == 0, i == KT - 1)
                            return last

                        def down_q(k):
                            for i in range(FET):
                                w = slice(i * DQ, (i + 1) * DQ)
                                last = mm3(ps[:, k % 4, 0:DQ], hx_hi[:, i], hx_lo[:, i], whi[k % 2][:, w],
                                           wlo[k % 2][:, w], i == 0, i == FET - 1)
                            return last

                        def turn(b):
                            if e:
                                pe.wait_ge(hx_l, it * 6 + (b + 1))
                            for a in range(4 if b < 2 else 3):
                                f = 4 * b + a
                                last = pe.transpose(ps[:, 4 + b, a * 128:a * 128 + 128], hm[:, f * 128:f * 128 + 128],
                                                    ident[:])
                            last.then_inc(hx_mm, 1)

                        K = MOE0 + 12 * e
                        for c in range(7):
                            expert_chunk(K + c, gate_up)
                        if e == 0:
                            pe.wait_ge(gs_cp, it + 1)
                            pe.wait_ge(oht_cp, it * 2 + 2)
                        pe.wait_ge(evac, n + (K + 4))
                        turn(0)
                        expert_chunk(K + 7, gate_up)
                        pe.wait_ge(evac, n + (K + 6))
                        turn(1)
                        pe.wait_ge(evac, n + (K + 8))
                        turn(2)
                        pe.wait_ge(hx_l, it * 6 + (3 * e + 3))
                        for c in range(8, 12):
                            expert_chunk(K + c, down_q)
                    pe.wait_ge(evac, n + (MOE0 + 24))
                    for f in range(KT):
                        if f >= 4:
                            pe.wait_ge(scat_add, it * 8 + (f - 3))
                        for e in range(2):
                            for part, y in enumerate((y_hi, y_lo)):
                                last = pe.matmul(ps[:, 4 + f % 4, 0:T], y[:, e, f * 128:f * 128 + 128], oht[:, e],
                                                 start=e == 0 and part == 0, stop=e == 1 and part == 1)
                        last.then_inc(scat_mm, 1)
            norm_sum("fin", sq, KT)


def kernel(**inputs):
    import concourse.bacc as bacc
    from concourse.bass_utils import run_bass_kernel_spmd as run

    a = {k: np.asarray(v) for k, v in inputs.items()}
    c = np.ascontiguousarray

    def rows(w, k):
        return w.reshape(*w.shape[:-2], k, 128, w.shape[-1]).swapaxes(-3, -2)

    def dense(w):
        n = w.shape[1] // 256
        return rows(w, KT).reshape(128, KT, n, 256).transpose(2, 0, 1, 3).reshape(n, 128, DW)

    def vec(v):
        v = v.reshape(*v.shape[:-1], v.shape[-1] // 128, 128)
        return np.moveaxis(v, -1, 0)

    x = np.concatenate([a["x_prompt"][0], a["x_sample"][:, 0]], axis=0)
    x_in = c(rows(x.T, KT))
    mem_in = c(rows(a["mem_prompt"][0].T, KT))
    layers, packs = [], []
    for l in range(DEPTH):
        B, C, X, XL, GA = np.split(a["w_in"][l], 5, axis=1)
        w_in = np.concatenate([XL, GA, C, X, B], axis=1)
        layers.append(np.concatenate([dense(w) for w in (a["w_k"][l], a["w_v"][l], w_in, a["w_mix_out"][l],
                                                         a["w_q"][l], a["w_o"][l])]))
        p = [vec(a["norm_mix"][l]), vec(a["norm_xattn"][l]), vec(a["norm_mem"][l]), vec(a["norm_ffn"][l]),
             vec(a["norm_final"]), vec(a["w_short_conv"][l]), vec(a["w_lru_conv"][l]), vec(a["b_lru_conv"][l]),
             vec(a["b_lru_a"][l]), vec(a["b_lru_x"][l]), vec(a["lru_lambda"][l]), vec(a["norm_conv_out"][l]),
             vec(a["norm_lru_out"][l]),
             vec(a["state_shortconv"][l]).transpose(0, 3, 2, 1), vec(a["state_lru_conv"][l]).transpose(0, 3, 2, 1),
             vec(a["state_lru_h"][l]).transpose(0, 2, 1)]
        packs.append(np.concatenate([q.reshape(128, -1) for q in p], axis=1))
    gate, up = (rows(a[k][0], KT).reshape(128, KT, FFT, 128) for k in ("w_ff_gate", "w_ff_up"))
    gu = np.stack([gate, up], axis=3).transpose(2, 0, 1, 3, 4).reshape(FFT, 128, DW)
    down = rows(a["w_ff_down"][0], FFT).reshape(128, FFT, KT, 128).transpose(2, 0, 1, 3).reshape(KT, 128, CW)
    mg, mu = (rows(a[k][0], KT).reshape(E, 128, KT, 4, GQ).transpose(0, 3, 1, 2, 4).reshape(E, 4, 1, 128, CW)
              for k in ("w_moe_gate", "w_moe_up"))
    md = rows(a["w_moe_down"][0], FET).reshape(E, 128, FET, 4, DQ).transpose(0, 3, 1, 2, 4).reshape(E, 4, 128, CW)
    moe = np.concatenate([np.concatenate([mg, mu], axis=2).reshape(E, 8, 128, CW), md], axis=1).reshape(E * 12, 128, CW)
    lru = np.stack([a["w_lru_a"], a["w_lru_x"]], axis=1).reshape(DEPTH, 2, G, 2, 64, 64).transpose(0, 1, 3, 4, 2, 5)
    router = rows(a["w_router"][0], KT)
    kc = a["cache_mem_k"].reshape(DEPTH, DEC, MEM, KT, 128).transpose(0, 1, 4, 3, 2).reshape(DEPTH, DEC, 128, DW)
    vc = a["cache_mem_v"].reshape(DEPTH, DEC, MT, 128, D).transpose(0, 1, 3, 2, 4).reshape(DEPTH, DEC, 128, DW)

    ins = dict(x_in=x_in, mem_in=mem_in, pk_in=np.stack(packs, axis=1), dense_in=np.stack(layers), gu_in=gu,
               down_in=down, moe_in=moe, lru_in=lru, router_in=router, kc_in=kc, vc_in=vc)
    outs = dict(y_out=(128, KT, T), k_out=(DEPTH, 128, KT, MEM), v_out=(DEPTH, 128, MT, D),
                small_out=(DEPTH, 128, G, NOC))
    nc = bacc.Bacc("TRN2", target_bir_lowering=False, num_devices=1)
    ins = {f"{k}_dram": c(v) for k, v in ins.items()}
    aps = [nc.dram_tensor(k, v.shape, mybir.dt.from_np(v.dtype), kind="ExternalInput").ap() for k, v in ins.items()]
    aps += [nc.dram_tensor(k, s, mybir.dt.float32, kind="ExternalOutput").ap() for k, s in outs.items()]
    build(nc, *aps)
    r = run(nc, [ins], core_ids=[0]).results[0]
    y = r["y_out"].transpose(1, 0, 2).reshape(D, T).T
    k_mem = r["k_out"].transpose(0, 3, 2, 1).reshape(DEPTH, 1, MEM, HEADS, 256)
    v_mem = r["v_out"].transpose(0, 2, 1, 3).reshape(DEPTH, 1, MEM, HEADS, 256)
    s = r["small_out"].transpose(0, 3, 2, 1).reshape(DEPTH, NOC, 512)

    def part(name, n):
        return s[:, OC[name]:OC[name] + n]

    return (c(y[None, 0:SEQ]), c(y[SEQ:T, None]), c(part("p_sc", 2)[:, None]), c(part("p_lc", 3)[:, None]),
            c(part("p_h", 1)), c(k_mem), c(v_mem),
            c(part("s_sc", 16).reshape(DEPTH, 2, DEC, 512).swapaxes(1, 2)),
            c(part("s_lc", 24).reshape(DEPTH, 3, DEC, 512).swapaxes(1, 2)), c(part("s_h", 8)))
```

```python
import concourse.bass as bass
from concourse import mybir
from contextlib import ExitStack
import numpy as np

D = 1024
KT = D // 128
SEQ, DEC = 256, 8
T = SEQ + DEC
DEPTH = 2
G = 4
NZ = 20
MEM = 256
MT = MEM // 128
HEADS, HT = 4, 2
FF, FFT = 2816, 22
E, FE = 8, 1408
FET = FE // 128
EPS = 1e-6
AREA = 20800
RAWS = 4
CW = 2816
DW = 2048
GQ, DQ = 352, 256
TT = ((0, 128), (128, 128), (256, 8))
PAIR_CHUNKS = 24
CACHES = 16
HW = 1536

PH = {"k": (0, 4), "in": (4, 10), "v": (14, 4), "mix": (18, 4), "q": (22, 4), "o": (26, 4)}
LAYER_CHUNKS = 30
FFN_CHUNKS = 30
LAYER0 = (0, LAYER_CHUNKS + FFN_CHUNKS)
GU0, DOWN0 = LAYER_CHUNKS, LAYER_CHUNKS + 22
MOE0 = LAYER0[1] + LAYER_CHUNKS



def halves(k):
    if k >= MOE0 and (k - MOE0) % 12 >= 8:
        return (0, 6 * DQ), (6 * DQ, 5 * DQ)
    w = (CW if k >= MOE0 or DOWN0 <= k < LAYER0[1] else DW) // 2
    return (0, w), (w, w)


def fills(k):
    return k // RAWS + 1 + (CACHES // RAWS) * sum(k >= LAYER0[l] + PH["o"][0] for l in range(DEPTH))


ZL, ZG, ZC, ZX, ZB = 0, 4, 8, 12, 16

_w = dict(g_mix=8, g_x=8, g_mem=8, g_ffn=8, g_fin=8, w_sc=12, w_lc=16, b_lc=4, b_a=4, b_x=4, lam=4,
          g_co=4, g_lo=4, st_sc=64, st_lc=96, st_h=32)
PK = {}
_at = 0
for _k, _n in _w.items():
    PK[_k] = _at
    _at += _n
NPK = _at
OC = dict(p_sc=0, p_lc=2, p_h=5, s_sc=6, s_lc=22, s_h=46)
NOC = 54


def build(nc, x_in, mem_in, pk_in, dense_in, gu_in, down_in, moe_in, lru_in, router_in, cache_in,
          y_out, k_out, v_out, small_out):
    f32, f32r, bf16, i32, u32 = (mybir.dt.float32, mybir.dt.float32r, mybir.dt.bfloat16,
                                 mybir.dt.int32, mybir.dt.uint32)
    ALU, ACT, AX = mybir.AluOpType, mybir.ActivationFunctionType, mybir.AxisListType
    ctx = ExitStack()
    with ctx:
        def sb(name, shape, dt=f32):
            return ctx.enter_context(nc.sbuf_tensor(name, shape, dt))

        def sem(name):
            return ctx.enter_context(nc.semaphore(name))

        raw = sb("raw", [128, RAWS, CW])
        whi = [sb(f"whi{i}", [128, HW], f32r) for i in range(4)]
        wlo = [sb(f"wlo{i}", [128, HW], f32r) for i in range(4)]
        x = sb("x", [128, KT, T])
        a_hi = sb("a_hi", [128, KT, T], f32r)
        a_lo = sb("a_lo", [128, KT, T], f32r)
        pk = sb("pk", [128, DEPTH, NPK])
        ones = sb("ones", [128, 128])
        ident = sb("ident", [128, 128])
        epsb = sb("epsb", [128, 1])
        sml = sb("sml", [128, G, NOC])
        nsp = sb("nsp", [128, DEPTH, 2, G])
        spt = sb("spt", [128, 4, DEPTH, G])
        rt = sb("rt", [128, T])
        rstd = sb("rstd", [128, T])
        stat = sb("stat", [128, 64])
        area = sb("area", [128, AREA])
        probe = nc.sbuf_base
        base = probe - AREA * 4

        def at(name, offset, shape, dt=f32):
            size = int(np.prod(shape[1:])) * (2 if dt == bf16 else 4)
            assert offset + size <= AREA * 4, name
            return nc.alloc_sbuf_tensor_at(name, shape, dt, offset=base + offset)

        m_hi = at("m_hi", 0, [128, KT, MEM], f32r)
        m_lo = at("m_lo", 8192, [128, KT, MEM], f32r)
        lru_w = at("lru_w", 32768, [128, 2, G, 128])
        memn = at("memn", 16384, [128, KT, MEM])
        kt = at("kt", 24576, [128, KT, MEM])
        vt = at("vt", 32768, [128, MT, D])
        z = at("z", 40960, [128, NZ, T])
        sq = at("sq", 40960, [128, KT, T])
        xc, rg, ig, av = (at(nm, 62080 + 4224 * i, [128, G, T]) for i, nm in enumerate(("xc", "rg", "ig", "av")))
        th = at("th", 40960, [128, G, T])
        hs = at("hs", 49408, [128, G, T])
        hf = at("hf", 71040, [128, KT, T])
        qt = at("qt", 40960, [128, KT, T])
        sq_d = at("sq_d", 71040, [128, KT, T])
        qm = at("qm", 49408, [128, KT, DEC, 32])
        pr = [at(f"pr{i}", 57600 + 2048 * i, [128, 2, MEM]) for i in range(2)]
        ptr = [at(f"ptr{i}", 61696 + 2048 * i, [128, MT, SEQ]) for i in range(2)]
        ptm = at("ptm", 65792, [128, MT, HEADS, DEC, 32])
        ps_s = at("ps_s", 73984, [128, MEM])
        o_s = at("o_s", 75008, [128, D])
        h_hi = at("h_hi", 24576, [128, FFT, T], f32r)
        h_lo = at("h_lo", 47808, [128, FFT, T], f32r)
        sg = [at(f"sg{i}", 71040 + 1056 * i, [128, T]) for i in range(2)]
        hff = [at(f"hff{i}", 73152 + 1056 * i, [128, T]) for i in range(2)]
        ht_hi = at("ht_hi", 0, [128, 3, D], f32r)
        ht_lo = at("ht_lo", 12288, [128, 3, D], f32r)
        wr_hi = at("wr_hi", 24576, [128, KT, 128], f32r)
        wr_lo = at("wr_lo", 28672, [128, KT, 128], f32r)
        xg_hi = at("xg_hi", 24576, [128, KT, 256], f32r)
        xg_lo = at("xg_lo", 32768, [128, KT, 256], f32r)
        oh = at("oh", 40960, [128, 3, 256], f32r)
        oht = at("oht", 44032, [128, 2, T], f32r)
        sgm = at("sgm", 46144, [128, 2, GQ])
        hm = at("hm", 48960, [128, FE])
        hx_hi = at("hx_hi", 54592, [128, FET, 128], f32r)
        hx_lo = at("hx_lo", 60224, [128, FET, 128], f32r)
        y_hi = at("y_hi", 65856, [128, 2, D], f32r)
        y_lo = at("y_lo", 74048, [128, 2, D], f32r)
        lg = at("lg", 32768, [128, T])
        rw = at("rw", 33824, [128, KT, E])
        iot_i = at("iot_i", 34080, [128, 128], i32)
        lt = at("lt", 34592, [128, 3, E])
        top = at("top", 34688, [128, 3, 8])
        topi = at("topi", 34784, [128, 3, 8], u32)
        topf = at("topf", 34880, [128, 3, 8])
        m1 = at("m1", 34976, [128, 3, E])
        m2 = at("m2", 35072, [128, 3, E])
        msk = at("msk", 35168, [128, 3, E], bf16)
        gt = at("gt", 35232, [128, 3, 4])
        tri = at("tri", 35296, [128, 128], bf16)
        one_b = at("one_b", 35552, [128, 128], bf16)
        cnt = at("cnt", 35808, [128, 8])
        valid = at("valid", 35840, [128, 3, E])
        iot = at("iot", 82240, [128, 128])
        comb = at("comb", 82752, [128, 3, E])
        rk = at("rk", 82848, [128, 3, E])
        cnt_i = at("cnt_i", 82944, [128, 8], i32)
        gs = at("gs", 82976, [128, 2])

        ps = ctx.enter_context(nc.psum_tensor("ps", [128, 8, 512], f32))

        raw_full = [sem(f"raw_full{i}") for i in range(RAWS)]
        hi_done, lo_done, pe_done, evac = sem("hi_done"), sem("lo_done"), sem("pe_done"), sem("evac")
        s_par, s_x, s_mem, s_lruw, s_small, s_kv, s_y, s_rw = (sem(n) for n in (
            "params_in", "x_in", "mem_in", "lru_w_in", "small_out", "kv_out", "y_out", "router_in"))
        consts, dve_c = sem("consts"), sem("dve_chain")
        n_sq, n_ss, n_rt, n_h, n_hi, n_lo = (sem(n) for n in (
            "norm_squares", "norm_sum", "norm_root", "norm_scaled", "norm_hi", "norm_lo"))
        xc_done, gates_mm, gates_act, gate_a, u_w, u_sq = (sem(n) for n in (
            "xc_done", "gates_mm", "gates_act", "lru_a_done", "lru_w_done", "lru_root"))
        gelu_done, sm_done, lruw_zero = sem("gelu_done"), sem("small_ready"), sem("lru_w_zero")
        sc_mm, sc_max, sc_exp, sc_nrm, pt_mm, pt_cp, ov_mm, at_hi, at_lo = (sem(n) for n in (
            "score_mm", "score_max", "score_exp", "probs_ready", "probs_t_mm", "probs_t_ready", "attn_mm",
            "attn_hi", "attn_lo"))
        q_ready, qm_ready, ss_mm, ss_max, ss_exp, ss_nrm, st_mm, st_cp, so_mm, so_cp, sot_mm = (sem(n) for n in (
            "q_ready", "qm_ready", "s_score_mm", "s_score_max", "s_score_exp", "s_probs_ready", "s_probs_t_mm",
            "s_probs_t_ready", "s_attn_mm", "s_attn_copied", "s_attn_t_mm"))
        cache_used, zeros, cx_done = sem("cache_used"), sem("masks_zeroed"), sem("short_conv_input")
        silu_done, ff_h = sem("silu_done"), sem("ff_h_ready")
        tk_mm, tk_cp, wr_ready, lg_mm, lg_cp, lt_mm, rk_in, rk_mm, route = (sem(n) for n in (
            "tok_major_mm", "tok_major_copied", "router_split", "logits_mm", "logits_copied", "logits_t_mm",
            "rank_in", "rank_mm", "routed"))
        tk_cl, g_in, g_exp, sp_in, sp_exp, ya_done, gs_cp = (sem(n) for n in (
            "tok_major_copied_lo", "gate_diff", "gate_exp", "softplus_in", "softplus_exp", "ya_ready", "slot_gate_ready"))
        oh_ready, ga_mm, ga_hi, ga_lo, oht_mm, oht_cp, gs_mm = (sem(n) for n in (
            "onehot_ready", "gather_mm", "gather_hi", "gather_lo", "onehot_t_mm", "onehot_t_ready", "slot_gate_mm"))
        m_silu, m_h, hx_mm, hx_h, hx_l, y_h, y_l, scat_mm, scat_add = (sem(n) for n in (
            "moe_silu", "moe_h", "moe_ht_mm", "moe_ht_hi", "moe_ht_lo", "moe_y_hi", "moe_y_lo", "scatter_mm",
            "scatter_added"))

        class Chain:

            def __init__(self, eng, s):
                self.eng, self.sem, self.n, self.off = eng, s, 0, 0

            def __call__(self, ins):
                ins.then_inc(self.sem, 1)
                self.n += 1

            def wait(self):
                self.eng.wait_ge(self.sem, self.n + self.off)

        NORMS = ["mem", "mix0", "co0", "lo0", "xattn0", "ffn0", "mix1", "co1", "lo1", "xattn1", "ffn1", "fin"]
        order = {name: i for i, name in enumerate(NORMS)}

        def sample_out(g):
            return ps[:, 4:6, :].rearrange("p a (k c) -> p (a k) c", c=128)[:, :, 4 * g:4 * g + 100:33]

        block = ctx.enter_context(nc.Block())

        SPLITS = ["m0", "mix0", "g0", "xattn0", "ffn0", "m1", "mix1", "g1", "xattn1", "ffn1", "fin"]

        def nh_of(name, k):
            return KT * SPLITS.index(name) + k

        def pair_of(name, k):
            return 4 * SPLITS.index(name) + k

        def sq_of(name, k):
            n = 0
            for q in NORMS:
                if q == name:
                    return n + k
                n += 1 if q[:2] in ("co", "lo") or q == "mem" else 4

        @block.sync
        def _(sp):
            def load(src, off, k, width):
                if k >= RAWS:
                    sp.wait_ge(lo_done, off * 2 + (2 * k - 6))
                sp.dma_start(raw[:, k % RAWS, 0:width], src).then_inc(raw_full[k % RAWS], 16)

            def looped(src, k0, count, width):
                full = count // RAWS
                with sp.Fori(0, full) as i:
                    for u in range(RAWS):
                        load(src(i * RAWS + u), i * RAWS, k0 + u, width)
                for j in range(full * RAWS, count):
                    load(src(j), 0, k0 + j, width)

            sp.dma_start(pk[:], pk_in).then_inc(s_par, 16)
            sp.dma_start(memn[:], mem_in).then_inc(s_mem, 16)
            sp.dma_start(x[:], x_in).then_inc(s_x, 16)
            for l in range(DEPTH):
                L = LAYER0[l]
                first = 0 if l else RAWS
                for j in range(first):
                    load(dense_in[l, j], 0, L + j, DW)
                looped(lambda j: dense_in[l, j + first], L + first, 26 - first, DW)
                for c in range(RAWS):
                    sp.wait_ge(lo_done, 2 * (L + 22 + c) + 2)
                    k = (L + 26 + c) % RAWS
                    sp.dma_start(raw[:, k, 0:DW], cache_in[l, c]).then_inc(raw_full[k], 16)
                with sp.Fori(0, CACHES // RAWS - 1) as i:
                    for u in range(RAWS):
                        sp.wait_ge(cache_used, i * RAWS + (CACHES * l + u + 1))
                        k = (L + 26 + u) % RAWS
                        sp.dma_start(raw[:, k, 0:DW], cache_in[l, i * RAWS + (RAWS + u)]).then_inc(raw_full[k], 16)
                for j in range(4):
                    sp.wait_ge(cache_used, CACHES * l + 13 + j)
                    k = (L + 26 + j) % RAWS
                    sp.dma_start(raw[:, k, 0:DW], dense_in[l, 26 + j]).then_inc(raw_full[k], 16)
                if l == 0:
                    looped(lambda j: gu_in[j], GU0, 22, DW)
                    looped(lambda j: down_in[j], DOWN0, 8, CW)
            for u in range(RAWS):
                load(moe_in[u], 0, MOE0 + u, CW)
            sp.wait_ge(route, 1)
            rounds = sp.value_load(cnt_i[0:1, 0:1], min_val=1, max_val=3)
            with sp.Fori(0, rounds) as r:
                with sp.Fori(0, 3) as p:
                    for u in range(RAWS, RAWS + PAIR_CHUNKS):
                        load(moe_in[p * PAIR_CHUNKS + u], r * 96 + p * 24, MOE0 + u, CW)
                for u in range(72 + RAWS, 96 + RAWS):
                    load(moe_in[u % 96], r * 96, MOE0 + u, CW)
            sp.wait_ge(n_h, nh_of("fin", 8))
            sp.dma_start(y_out, hf[:]).then_inc(s_y, 16)
            sp.wait_ge(s_y, 16)

        @block.gpsimd
        def _(pool):
            pool.memset(ones[:], 1.0).then_inc(consts, 1)
            pool.memset(ident[:], 0.0).then_inc(consts, 1)
            pool.memset(epsb[:], EPS).then_inc(consts, 1)
            pool.wait_ge(consts, 3)
            pool.affine_select(out=ident[:], in_=ident[:], compare_op=ALU.not_equal, fill=1.0, base=0,
                               pattern=[[-1, 128]], channel_multiplier=1).then_inc(consts, 1)
            for l in range(DEPTH):
                L = LAYER0[l]
                if l:
                    pool.wait_ge(pe_done, 2 * L)
                pool.memset(lru_w[:], 0.0).then_inc(lruw_zero, 1)
                pool.wait_ge(lruw_zero, l + 1)
                for m in range(2):
                    for half in range(2):
                        q = slice(64 * half, 64 * half + 64)
                        pool.dma_start(lru_w[q, m, :, q], lru_in[l, m, half]).then_inc(s_lruw, 16)
                pool.wait_ge(evac, L + 4)
                pool.dma_start(k_out[l], kt[:]).then_inc(s_kv, 16)
                pool.wait_ge(evac, L + 12)
                pool.tensor_tensor(z[:, ZC:ZC + G], z[:, ZC:ZC + G], z[:, ZX:ZX + G], ALU.mult).then_inc(cx_done, 1)
                pool.wait_ge(evac, L + 18)
                pool.dma_start(v_out[l], vt[:]).then_inc(s_kv, 16)
                pool.wait_ge(sm_done, l + 1)
                pool.dma_start(small_out[l], sml[:]).then_inc(s_small, 16)
                pool.wait_ge(n_lo, pair_of(f"xattn{l}", 4))
                pool.memset(qm[:], 0.0).then_inc(zeros, 1)
                pool.memset(ptm[:], 0.0).then_inc(zeros, 1)
            pool.wait_ge(s_small, 16 * DEPTH)
            pool.wait_ge(s_kv, 32 * DEPTH)
            pool.wait_ge(n_lo, pair_of("ffn1", 4))
            pool.dma_start(rw[:], router_in).then_inc(s_rw, 16)
            pool.memset(wr_hi[:].bitcast(f32), 0.0).then_inc(consts, 1)
            pool.memset(wr_lo[:].bitcast(f32), 0.0).then_inc(consts, 1)
            pool.iota(iot_i[:], pattern=[[1, 128]], base=0, channel_multiplier=0).then_inc(consts, 1)
            pool.memset(one_b[:], 1.0).then_inc(consts, 1)
            pool.memset(valid[:], 1.0).then_inc(consts, 1)
            pool.wait_ge(consts, 9)
            pool.affine_select(out=valid[:, 2], in_=valid[:, 2], compare_op=ALU.is_gt, fill=0.0, base=DEC,
                               pattern=[[0, E]], channel_multiplier=-1).then_inc(consts, 1)
            pool.affine_select(out=tri[:], in_=one_b[:], compare_op=ALU.is_gt, fill=0.0, base=0,
                               pattern=[[1, 128]], channel_multiplier=-1).then_inc(consts, 1)

        @block.scalar
        def _(act):
            def hi(off, k, s):
                c, w = halves(k)[s]
                m = 2 * k + s
                if s == 0:
                    act.wait_ge(raw_full[k % RAWS], off * (16 // RAWS) + 16 * fills(k))
                if m >= 4:
                    act.wait_ge(pe_done, off * 2 + (m - 3))
                act.activation(whi[m % 4][:, 0:w], raw[:, k % RAWS, c:c + w], ACT.Copy).then_inc(hi_done, 1)

            def step(off, k, body=None, first=False):
                if not first:
                    hi(off, k + 2, 0)
                if body:
                    body()
                if first:
                    hi(off, k + 2, 0)
                hi(off, k + 2, 1)

            def square(dst, src):
                act.activation(dst, src, ACT.Square).then_inc(n_sq, 1)

            def root(name, scale):
                w = MEM if name == "mem" else T
                act.wait_ge(n_ss, order[name] + 1)
                act.activation(rt[:, 0:w], ps[:, 4, 0:w], ACT.Sqrt, bias=epsb[:, 0:1], scale=scale).then_inc(n_rt, 1)

            def norm_hi(name, src, dst, ks=range(0, KT, 2)):
                for k in ks:
                    act.wait_ge(n_h, nh_of(name, k + 2))
                    act.activation(dst[:, k:k + 2], src(k), ACT.Copy).then_inc(n_hi, 1)

            def of(buf):
                return lambda k: buf[:, k:k + 2]

            def x_square(k, j, buf):
                def body():
                    act.wait_ge(evac, k + 1)
                    square(buf[:, 2 * j:2 * j + 2], x[:, 2 * j:2 * j + 2])
                return body

            def attn_hi(l, h):
                act.wait_ge(ov_mm, HEADS * l + h + 1)
                act.activation(a_hi[:, HT * h:HT * h + 2, 0:SEQ], ps[:, 2 + h % 2, :].rearrange(
                    "p (a t) -> p a t", a=2), ACT.Copy).then_inc(at_hi, 1)

            act.wait_ge(consts, 4)
            act.wait_ge(s_mem, 16)
            square(sq[:, :, 0:MEM], memn[:])
            act.wait_ge(s_x, 16)
            for j in range(4):
                square(sq_d[:, 2 * j:2 * j + 2], x[:, 2 * j:2 * j + 2])
            act.wait_ge(sp_in, 1)
            act.activation(spt[:, 1], spt[:, 0], ACT.Exp, scale=-1.0).then_inc(sp_exp, 1)
            root("mem", 1.0 / D)
            for k in range(2):
                hi(0, k, 0)
                hi(0, k, 1)
            norm_hi("m0", lambda k: hf[:, k:k + 2, 0:MEM], m_hi)
            for l in range(DEPTH):
                L = LAYER0[l]
                P = pk[:, l, :]
                step(0, L)
                root(f"mix{l}", 1.0 / D)
                step(0, L + 1)
                norm_hi(f"mix{l}", of(hf), a_hi)
                step(0, L + 2)
                step(0, L + 3)

                def sigmoids(t0):
                    def body():
                        for t in (t0, t0 + 1):
                            act.wait_ge(gates_mm, G * l + t + 1)
                            act.activation(rg[:, t], ps[:, 4 + 2 * (t % 2), 0:T], ACT.Sigmoid,
                                           bias=P[:, PK["b_a"] + t:PK["b_a"] + t + 1]).then_inc(gates_act, 1)
                            act.activation(ig[:, t], ps[:, 5 + 2 * (t % 2), 0:T], ACT.Sigmoid,
                                           bias=P[:, PK["b_x"] + t:PK["b_x"] + t + 1]).then_inc(gates_act, 1)
                    return body

                def decay():
                    act.wait_ge(gates_act, 2 * G * (l + 1))
                    for t in range(G):
                        act.activation(av[:, t], rg[:, t], ACT.Exp, scale=nsp[:, l, 0, t:t + 1])
                        act.activation(th[:, t], rg[:, t], ACT.Tanh, scale=nsp[:, l, 1, t:t + 1]).then_inc(gate_a, 1)

                def lru_root():
                    act.wait_ge(u_w, 2 * l + 1)
                    act.activation(th[:], th[:], ACT.Sqrt).then_inc(u_sq, 1)

                def gelu():
                    act.activation(z[:, ZG:ZG + G], z[:, ZG:ZG + G], ACT.Gelu_apprx_tanh).then_inc(gelu_done, 1)

                do = {5: sigmoids(0), 6: sigmoids(2), 7: decay, 8: gelu, 9: lru_root}
                for j in range(10):
                    step(0, L + 4 + j, do.get(j))

                def ya_square():
                    act.wait_ge(ya_done, l + 1)
                    square(xc[:], z[:, ZX:ZX + G])

                def yb_square():
                    root(f"co{l}", 1.0 / 512)
                    act.wait_ge(u_w, 2 * l + 2)
                    square(ig[:], hs[:])

                def group_roots():
                    norm_hi(f"g{l}", lambda k: z[:, ZX + k:ZX + k + 2], a_hi, (0, 2))
                    root(f"lo{l}", 1.0 / 512)

                step(0, L + 14)
                step(0, L + 15, ya_square, True)
                step(0, L + 16, yb_square)
                step(0, L + 17, group_roots, True)
                norm_hi(f"g{l}", lambda k: hs[:, k - G:k - G + 2], a_hi, (4, 6))
                for j in range(4):
                    step(0, L + 18 + j, x_square(L + 18 + j, j, sq))
                root(f"xattn{l}", 1.0 / D)
                norm_hi(f"xattn{l}", of(hf), a_hi)
                step(0, L + 22)
                step(0, L + 23)
                for h in range(HEADS):
                    c = HEADS * l + h
                    act.wait_ge(sc_max, c + 1)
                    for t in range(2):
                        act.activation(pr[h % 2][:, t], ps[:, 4 + h % 2, t * MEM:(t + 1) * MEM], ACT.Exp,
                                       bias=stat[:, 2 * h + t:2 * h + t + 1],
                                       accum_out=stat[:, 16 + 2 * h + t:17 + 2 * h + t]).then_inc(sc_exp, 1)
                    if h:
                        attn_hi(l, h - 1)
                attn_hi(l, HEADS - 1)
                act.wait_ge(ss_max, l + 1)
                act.activation(ps_s[:], ps[:, 0, 0:MEM], ACT.Exp, bias=stat[:, 32:33],
                               accum_out=stat[:, 34:35]).then_inc(ss_exp, 1)
                for k in (L + 26, L + 27):
                    hi(0, k, 0)
                    hi(0, k, 1)
                act.wait_ge(sot_mm, 2 * l + 2)
                for g in range(2):
                    act.activation(a_hi[:, :, SEQ + 4 * g:SEQ + 4 * g + 4], sample_out(g), ACT.Copy).then_inc(at_hi, 1)
                for j in range(4):
                    step(0, L + 26 + j, x_square(L + 26 + j, j, sq))
                root(f"ffn{l}", 1.0 / D)
                norm_hi(f"ffn{l}", of(hf), a_hi)
                if l == 0:
                    norm_hi("m1", lambda k: hf[:, k:k + 2, 0:MEM], m_hi)
                    act.wait_ge(n_lo, pair_of("m1", 4))

                    def silu(off, k):
                        def body():
                            act.wait_ge(pe_done, off * 2 + (2 * k + 2))
                            act.wait_ge(evac, off + (k - 1))
                            act.activation(sg[k % 2][:], ps[:, 2 * (k % 2), 0:T], ACT.Silu).then_inc(silu_done, 1)
                        return body

                    with act.Fori(0, 5) as i:
                        for u in range(RAWS):
                            step(i * RAWS, GU0 + u, silu(i * RAWS, GU0 + u))
                    for k in range(GU0 + 20, GU0 + 22):
                        step(0, k, silu(0, k))
                    for j in range(8):
                        step(0, DOWN0 + j, x_square(DOWN0 + j, j // 2, sq_d) if j % 2 else None)

            for i in range(6):
                act.wait_ge(tk_mm, 2 * i + 1)
                t, half = i // 2, i % 2
                w = TT[t][1]
                act.activation(ht_hi[0:w, t, half * 512:half * 512 + 512], ps[0:w, 4 + 2 * (i % 2), :],
                               ACT.Copy).then_inc(tk_cp, 1)
            act.wait_ge(g_in, 1)
            act.activation(gt[:, :, 1], gt[:, :, 0], ACT.Exp).then_inc(g_exp, 1)
            act.wait_ge(route, 1)
            rounds = act.value_load(cnt_i[0:1, 0:1], min_val=1, max_val=3)
            with act.Fori(0, rounds) as r:
                with act.Fori(0, 4) as p:
                    it = r * 4 + p
                    off = r * 96 + p * 24
                    for g in range(4):
                        act.wait_ge(ga_mm, it * 8 + (2 * g + 1))
                        act.activation(xg_hi[:, 2 * g:2 * g + 2, :], ps[:, 4 + 2 * (g % 2), :].rearrange(
                            "p (a c) -> p a c", a=2), ACT.Copy).then_inc(ga_hi, 1)
                    for e in range(2):
                        for q in range(4):
                            k = MOE0 + 12 * e + 2 * q

                            def silu_q():
                                act.wait_ge(pe_done, off * 2 + (2 * k + 2))
                                act.wait_ge(evac, off + (MOE0 + 12 * e + 2 * q - 2))
                                act.activation(sgm[:, q % 2], ps[:, k % 4, 0:GQ], ACT.Silu).then_inc(m_silu, 1)

                            step(off, k, silu_q)
                            step(off, k + 1)
                        for b in range(3):
                            w = 512 if b < 2 else 384
                            act.wait_ge(hx_mm, it * 6 + (3 * e + b + 1))
                            act.activation(hx_hi[:, 4 * b:4 * b + w // 128].rearrange("p a c -> p (a c)"),
                                           ps[:, 4 + b, 0:w], ACT.Copy).then_inc(hx_h, 1)
                        for q in range(4):
                            k = MOE0 + 12 * e + 8 + q

                            def y_part():
                                act.wait_ge(pe_done, off * 2 + (2 * k + 2))
                                act.activation(y_hi[:, e, q * DQ:(q + 1) * DQ], ps[:, k % 4, 0:DQ], ACT.Copy,
                                               scale=gs[:, e:e + 1]).then_inc(y_h, 1)

                            step(off, k, y_part)
            act.wait_ge(scat_add, rounds * 32 + 1)
            for j in range(4):
                square(sq[:, 2 * j:2 * j + 2], x[:, 2 * j:2 * j + 2])
            root("fin", 1.0 / D)

        @block.vector
        def _(dve):
            chain = Chain(dve, dve_c)

            def col(l, name, i):
                c = PK[name] + i
                return pk[:, l, c:c + 1]

            def lo(off, k, s):
                c, w = halves(k)[s]
                m = 2 * k + s
                dve.wait_ge(hi_done, off * 2 + (m + 1))
                dve.tensor_tensor(wlo[m % 4][:, 0:w], raw[:, k % RAWS, c:c + w], whi[m % 4][:, 0:w].bitcast(f32),
                                  ALU.subtract).then_inc(lo_done, 1)

            def banks(k, w):
                b = 2 * (k % 2)
                return ps[:, b:b + 2, 0:w]

            def step(off, k, read, extra=None, first=None, split=True):
                if first:
                    first()
                if split:
                    lo(off, k + 2, 0)
                dve.wait_ge(pe_done, off * 2 + (2 * k + 2))
                read().then_inc(evac, 1)
                if extra:
                    dve.wait_ge(evac, off + (k + 1))
                    extra()
                if split:
                    lo(off, k + 2, 1)

            def root_reciprocal(name, w=T):
                dve.wait_ge(n_rt, order[name] + 1)
                chain.wait()
                chain(dve.reciprocal(rstd[:, 0:w], rt[:, 0:w]))
                chain.wait()

            def lo_pair(name, j, src, dst_hi, dst_lo):
                dve.wait_ge(n_hi, pair_of(name, j + 1))
                dve.tensor_tensor(dst_lo[:, 2 * j:2 * j + 2], src, dst_hi[:, 2 * j:2 * j + 2].bitcast(f32),
                                  ALU.subtract).then_inc(n_lo, 1)

            def norm(name, gain, l):
                root_reciprocal(name)
                if name != "fin":
                    dve.wait_ge(n_lo, pair_of(name, 0))
                for k in range(KT):
                    dve.scalar_tensor_tensor(out=hf[:, k], in0=x[:, k], scalar=col(l, gain, k), in1=rstd[:],
                                             op0=ALU.mult, op1=ALU.mult).then_inc(n_h, 1)
                    if k in (3, 5, 7) and name != "fin":
                        j = (k - 3) // 2
                        lo_pair(name, j, hf[:, 2 * j:2 * j + 2], a_hi, a_lo)
                if name != "fin":
                    lo_pair(name, 3, hf[:, 6:8], a_hi, a_lo)

            def mem_operand(l):
                if l:
                    dve.wait_ge(n_lo, pair_of("m1", 0))
                for k in range(KT):
                    dve.tensor_scalar(hf[:, k, 0:MEM], memn[:, k], col(l, "g_mem", k), None, ALU.mult).then_inc(n_h, 1)
                for j in range(4):
                    lo_pair(f"m{l}", j, hf[:, 2 * j:2 * j + 2, 0:MEM], m_hi, m_lo)

            dve.wait_ge(s_par, 16)
            lam = pk[:, :, PK["lam"]:PK["lam"] + G]
            dve.scalar_tensor_tensor(out=spt[:, 0], in0=lam, scalar=-1.0, in1=lam, op0=ALU.mult,
                                     op1=ALU.max).then_inc(sp_in, 1)

            root_reciprocal("mem", MEM)
            for k in range(KT):
                ins = dve.tensor_tensor(memn[:, k], memn[:, k], rstd[:, 0:MEM], ALU.mult)
                chain(ins)
            chain.wait()
            dve.wait_ge(n_ss, order["mix0"] + 1)
            mem_operand(0)
            for k in range(2):
                lo(0, k, 0)
                lo(0, k, 1)

            dve.wait_ge(sp_exp, 1)
            chain(dve.tensor_scalar(spt[:, 2], spt[:, 1], 2.0, None, ALU.add))
            chain.wait()
            chain(dve.reciprocal(spt[:, 3], spt[:, 2]))
            chain.wait()
            chain(dve.tensor_tensor(spt[:, 0], spt[:, 1], spt[:, 3], ALU.mult))
            chain.wait()
            chain(dve.tensor_tensor(spt[:, 1], spt[:, 0], spt[:, 0], ALU.mult))
            chain.wait()
            chain(dve.tensor_scalar(spt[:, 2], spt[:, 1], 1.0 / 19, None, ALU.mult))
            for c in range(17, 1, -2):
                chain.wait()
                chain(dve.scalar_tensor_tensor(out=spt[:, 2], in0=spt[:, 2], scalar=1.0 / c, in1=spt[:, 1],
                                               op0=ALU.add, op1=ALU.mult))
            chain.wait()
            chain(dve.scalar_tensor_tensor(out=spt[:, 2], in0=spt[:, 2], scalar=1.0, in1=spt[:, 0],
                                           op0=ALU.add, op1=ALU.mult))
            chain(dve.tensor_scalar(spt[:, 3], lam, -1.0, 0.0, ALU.mult, ALU.max))
            chain.wait()
            chain(dve.scalar_tensor_tensor(out=spt[:, 2], in0=spt[:, 2], scalar=2.0, in1=spt[:, 3],
                                           op0=ALU.mult, op1=ALU.add))
            chain.wait()
            for i, c in enumerate((-8.0, 8.0)):
                ins = dve.tensor_scalar(nsp[:, :, i, :], spt[:, 2], c, None, ALU.mult)
                chain(ins)

            for l in range(DEPTH):
                L = LAYER0[l]
                st_lc = pk[:, l, PK["st_lc"]:PK["st_lc"] + 96].rearrange("p (t k) -> p t k", t=G)
                st_sc = pk[:, l, PK["st_sc"]:PK["st_sc"] + 64].rearrange("p (t k) -> p t k", t=G)
                st_h = pk[:, l, PK["st_h"]:PK["st_h"] + 32].rearrange("p (t k) -> p t k", t=G)

                for j in range(4):
                    step(0, L + j, lambda: dve.tensor_copy(kt[:, 2 * j:2 * j + 2], banks(L + j, MEM)))
                    if j == 1:
                        norm(f"mix{l}", "g_mix", l)

                def small(name, w, src, shift=0):
                    c = OC[name] + shift
                    return dve.tensor_copy(sml[:, :, c:c + w], src)

                def conv_tap(dst, src, name, state, taps, tap):
                    chain.wait()
                    s = taps - 1 - tap
                    for t in range(G):
                        w = col(l, name, 4 * tap + t)
                        chain(dve.scalar_tensor_tensor(out=dst[:, t, s:SEQ], in0=src[:, t, 0:SEQ - s], scalar=w,
                                                       in1=dst[:, t, s:SEQ], op0=ALU.mult, op1=ALU.add))
                        c = 8 * tap
                        chain(dve.scalar_tensor_tensor(out=dst[:, t, SEQ:T], in0=state[:, t, c:c + 8], scalar=w,
                                                       in1=dst[:, t, SEQ:T], op0=ALU.mult, op1=ALU.add))

                xl, cx, sc = z[:, ZL:ZL + G], z[:, ZC:ZC + G], z[:, ZX:ZX + G]

                def lru_conv_base():
                    for t in range(G):
                        chain(dve.tensor_scalar(xc[:, t], xl[:, t], col(l, "w_lc", 12 + t), col(l, "b_lc", t),
                                                ALU.mult, ALU.add))
                    conv_tap(xc, xl, "w_lc", st_lc, 4, 2)

                def lru_conv_end():
                    conv_tap(xc, xl, "w_lc", st_lc, 4, 0)
                    chain.wait()
                    if l:
                        dve.wait_ge(s_small, 16)
                    small("p_lc", 3, z[:, ZL:ZL + G, SEQ - 3:SEQ]).then_inc(xc_done, 1)

                def lru_states():
                    chain(small("s_lc", 16, st_lc[:, :, 8:24]))
                    chain(small("s_lc", 8, z[:, ZL:ZL + G, SEQ:T], 16))
                    chain(small("s_sc", 8, st_sc[:, :, 8:16]))

                def lru_input():
                    dve.wait_ge(gate_a, G * (l + 1))
                    chain(dve.tensor_tensor(rg[:], av[:], av[:], ALU.mult))
                    chain(dve.tensor_tensor(ig[:], ig[:], xc[:], ALU.mult))
                    chain.wait()
                    dve.scalar_tensor_tensor(out=th[:], in0=rg[:], scalar=1.0, in1=th[:], op0=ALU.add,
                                             op1=ALU.mult).then_inc(u_w, 1)

                def short_conv():
                    dve.wait_ge(cx_done, l + 1)
                    chain(small("p_sc", 2, z[:, ZC:ZC + G, SEQ - 2:SEQ]))
                    chain(small("s_sc", 8, z[:, ZC:ZC + G, SEQ:T], 8))
                    for t in range(G):
                        chain(dve.tensor_scalar(sc[:, t], cx[:, t], col(l, "w_sc", 8 + t), None, ALU.mult))
                    conv_tap(sc, cx, "w_sc", st_sc, 3, 1)

                def short_conv_end():
                    conv_tap(sc, cx, "w_sc", st_sc, 3, 0)
                    chain.wait()
                    dve.wait_ge(evac, L + 14)
                    dve.tensor_tensor(sc, sc, z[:, ZB:ZB + G], ALU.mult).then_inc(ya_done, 1)

                def recurrence():
                    dve.wait_ge(u_sq, l + 1)
                    chain(dve.tensor_tensor(ig[:], ig[:], th[:], ALU.mult))
                    chain(dve.tensor_tensor(hs[:, :, SEQ:T], av[:, :, SEQ:T], st_h, ALU.mult))
                    chain.wait()
                    for t in range(G):
                        chain(dve.tensor_tensor_scan(hs[:, t, 0:SEQ], av[:, t, 0:SEQ], ig[:, t, 0:SEQ], 0.0,
                                                     ALU.mult, ALU.add))
                    chain(dve.tensor_tensor(hs[:, :, SEQ:T], hs[:, :, SEQ:T], ig[:, :, SEQ:T], ALU.add))
                    chain.wait()
                    chain(small("p_h", 1, hs[:, :, SEQ - 1:SEQ]))
                    small("s_h", 8, hs[:, :, SEQ:T]).then_inc(sm_done, 1)
                    dve.wait_ge(gelu_done, l + 1)
                    dve.wait_ge(sm_done, l + 1)
                    chain.wait()
                    dve.tensor_tensor(hs[:], hs[:], z[:, ZG:ZG + G], ALU.mult).then_inc(u_w, 1)

                def group_norm(name, src, gain, after=None):
                    root_reciprocal(name)
                    for k in range(G):
                        dve.scalar_tensor_tensor(out=src[:, k], in0=src[:, k], scalar=col(l, gain, k), in1=rstd[:],
                                                 op0=ALU.mult, op1=ALU.mult).then_inc(n_h, 1)

                extras = {1: lru_conv_base, 2: lambda: conv_tap(xc, xl, "w_lc", st_lc, 4, 1), 3: lru_conv_end,
                          4: lru_states, 8: lru_input, 9: short_conv}
                for j in range(10):
                    step(0, L + 4 + j, lambda: dve.tensor_copy(z[:, 2 * j:2 * j + 2, :], banks(L + 4 + j, T)),
                         extras.get(j))

                def value(j, **kw):
                    step(0, L + 14 + j, lambda: dve.tensor_copy(vt[:, :, j * 256:j * 256 + 256],
                                                                banks(L + 14 + j, 256)), **kw)

                def lru_norm():
                    for j in range(2):
                        lo_pair(f"g{l}", j, z[:, ZX + 2 * j:ZX + 2 * j + 2], a_hi, a_lo)
                    group_norm(f"lo{l}", hs, "g_lo")

                value(0, first=short_conv_end)
                value(1, first=recurrence)
                value(2)
                group_norm(f"co{l}", sc, "g_co")
                value(3, first=lru_norm)
                for j in range(2):
                    lo_pair(f"g{l}", 2 + j, hs[:, 2 * j:2 * j + 2], a_hi, a_lo)

                def add_x(k, j):
                    return dve.tensor_tensor(x[:, 2 * j:2 * j + 2], x[:, 2 * j:2 * j + 2], banks(k, T), ALU.add)

                for j in range(4):
                    step(0, L + 18 + j, lambda: add_x(L + 18 + j, j))
                norm(f"xattn{l}", "g_x", l)
                for j in range(4):
                    step(0, L + 22 + j, lambda: dve.tensor_scalar(qt[:, 2 * j:2 * j + 2], banks(L + 22 + j, T),
                                                                  1.0 / 16, None, ALU.mult), split=j < 2)

                dve.wait_ge(evac, L + 26)
                dve.wait_ge(zeros, 2 * l + 1)
                for h in range(HEADS):
                    ins = dve.tensor_copy(
                        qm[:].rearrange("p j b c -> p j (b c)")[:, HT * h:HT * h + HT, 8 * h:8 * h + 232:33],
                        qt[:, HT * h:HT * h + HT, SEQ:T])
                    if h < HEADS - 1:
                        chain(ins)
                ins.then_inc(qm_ready, 1)

                def score_max(h):
                    dve.wait_ge(sc_mm, HEADS * l + h + 1)
                    chain(dve.tensor_reduce(stat[:, 8 + 2 * (h % 2):10 + 2 * (h % 2)],
                                            ps[:, 4 + h % 2, :].rearrange("p (t m) -> p t m", t=2), AX.X, ALU.max))
                    chain.wait()
                    dve.tensor_scalar(stat[:, 2 * h:2 * h + 2], stat[:, 8 + 2 * (h % 2):10 + 2 * (h % 2)], -1.0, None,
                                      ALU.mult).then_inc(sc_max, 1)

                score_max(0)
                score_max(1)
                for h in range(HEADS):
                    c = HEADS * l + h
                    dve.wait_ge(sc_exp, 2 * c + 2)
                    chain(dve.reciprocal(stat[:, 24 + 2 * h:26 + 2 * h], stat[:, 16 + 2 * h:18 + 2 * h]))
                    chain.wait()
                    for t in range(2):
                        ins = dve.tensor_scalar(pr[h % 2][:, t], pr[h % 2][:, t], stat[:, 24 + 2 * h + t:25 + 2 * h + t],
                                                None, ALU.mult)
                    ins.then_inc(sc_nrm, 1)
                    dve.wait_ge(pt_mm, c + 1)
                    dve.tensor_copy(ptr[h % 2][:], ps[:, 6 + h % 2, :].rearrange("p (m t) -> p m t", m=2))\
                       .then_inc(pt_cp, 1)
                    if h + 2 < HEADS:
                        score_max(h + 2)
                    dve.wait_ge(at_hi, 6 * l + h + 1)
                    dve.tensor_tensor(a_lo[:, HT * h:HT * h + 2, 0:SEQ],
                                      ps[:, 2 + h % 2, :].rearrange("p (a t) -> p a t", a=2),
                                      a_hi[:, HT * h:HT * h + 2, 0:SEQ].bitcast(f32), ALU.subtract).then_inc(at_lo, 1)

                dve.wait_ge(ss_mm, l + 1)
                chain(dve.tensor_reduce(stat[:, 33:34], ps[:, 0, 0:MEM], AX.X, ALU.max))
                chain.wait()
                dve.tensor_scalar(stat[:, 32:33], stat[:, 33:34], -1.0, None, ALU.mult).then_inc(ss_max, 1)
                dve.wait_ge(ss_exp, l + 1)
                chain(dve.reciprocal(stat[:, 35:36], stat[:, 34:35]))
                chain.wait()
                dve.tensor_scalar(ps_s[:], ps_s[:], stat[:, 35:36], None, ALU.mult).then_inc(ss_nrm, 1)
                dve.wait_ge(zeros, 2 * l + 2)
                dve.wait_ge(st_mm, l + 1)
                for r in range(4):
                    dve.tensor_copy(
                        ptm[:].rearrange("p m h b c -> p (m h) (b c)")[:, :, 33 * r:33 * r + 133:132],
                        ps[:, 6, 0:MEM].rearrange("p (m c) -> p m c", m=MT)[:, :, 33 * r:33 * r + 29:4]
                        .rearrange("p m (h q) -> p m h q", q=2)).then_inc(st_cp, 1)
                lo(0, L + 26, 0)
                lo(0, L + 26, 1)
                dve.wait_ge(so_mm, l + 1)
                dve.tensor_copy(o_s[:].rearrange("p (h d) -> p h d", h=HEADS), ps[:, 0:HEADS, 0:256])\
                   .then_inc(so_cp, 1)
                lo(0, L + 27, 0)
                lo(0, L + 27, 1)
                dve.wait_ge(at_hi, 6 * l + 6)
                for g in range(2):
                    c = SEQ + 4 * g
                    dve.tensor_tensor(a_lo[:, :, c:c + 4], sample_out(g), a_hi[:, :, c:c + 4].bitcast(f32),
                                      ALU.subtract).then_inc(at_lo, 1)

                for j in range(4):
                    step(0, L + 26 + j, lambda: add_x(L + 26 + j, j))
                norm(f"ffn{l}", "g_ffn", l)
                if l == 0:
                    mem_operand(1)
                    dve.wait_ge(s_kv, 32)
                    dve.wait_ge(n_lo, pair_of("m1", 4))

                    def gated(off, j, last=False):
                        k = GU0 + j
                        lo(off, k + 2, 0)
                        dve.wait_ge(silu_done, off + (j + 1))
                        dve.tensor_tensor(hff[k % 2][:], sg[k % 2][:], ps[:, 2 * (k % 2) + 1, 0:T],
                                          ALU.mult).then_inc(evac, 1)
                        lo(off, k + 2, 1)
                        dve.wait_ge(evac, off + (k + 1))
                        chain(dve.tensor_copy(h_hi[:, off + j, :], hff[k % 2][:]))
                        chain.wait()
                        ins = dve.tensor_tensor(h_lo[:, off + j, :], hff[k % 2][:], h_hi[:, off + j, :].bitcast(f32),
                                                ALU.subtract)
                        if last:
                            ins.then_inc(ff_h, 1)

                    with dve.Fori(0, 5) as i:
                        chain.off = i * RAWS
                        for u in range(RAWS):
                            gated(i * RAWS, u)
                    chain.off, chain.n = 0, chain.n + 4 * RAWS
                    gated(0, 20)
                    gated(0, 21, True)
                    for j in range(8):
                        k = DOWN0 + j
                        step(0, k, lambda: dve.tensor_tensor(x[:, j, :], x[:, j, :], ps[:, 2 * (k % 2), 0:T], ALU.add))

            dve.wait_ge(consts, 11)
            dve.wait_ge(s_rw, 16)
            dve.wait_ge(n_lo, pair_of("ffn1", 4))
            chain(dve.memset(ht_hi[:, 2].bitcast(f32), 0.0))
            chain(dve.memset(ht_lo[:, 2].bitcast(f32), 0.0))
            chain(dve.tensor_copy(wr_hi[:, :, 0:E], rw[:]))
            chain.wait()
            dve.tensor_tensor(wr_lo[:, :, 0:E], rw[:], wr_hi[:, :, 0:E].bitcast(f32), ALU.subtract).then_inc(wr_ready, 1)
            chain(dve.tensor_copy(iot[:], iot_i[:]))
            dve.memset(lt[:], 0.0).then_inc(scat_add, 1)
            dve.wait_ge(scat_add, 1)
            for i in range(6):
                dve.wait_ge(tk_mm, 2 * i + 2)
                t, half = i // 2, i % 2
                w = TT[t][1]
                dve.tensor_copy(ht_lo[0:w, t, half * 512:half * 512 + 512], ps[0:w, 5 + 2 * (i % 2), :])\
                   .then_inc(tk_cl, 1)
            dve.wait_ge(lg_mm, 1)
            dve.tensor_copy(lg[0:E], ps[0:E, 0, 0:T]).then_inc(lg_cp, 1)
            dve.wait_ge(lt_mm, 1)
            chain.wait()
            for i, (c0, w) in enumerate(TT):
                chain(dve.tensor_copy(lt[0:w, i], ps[0:w, 1, i * E:(i + 1) * E]))
            chain.wait()
            for i in range(3):
                chain(dve.max(top[:, i], lt[:, i]))
            chain.wait()
            for i in range(3):
                chain(dve.max_index(topi[:, i], top[:, i], lt[:, i]))
            dve.tensor_tensor(gt[:, :, 0], top[:, :, 1], top[:, :, 0], ALU.subtract).then_inc(g_in, 1)
            chain.wait()
            chain(dve.tensor_copy(topf[:], topi[:]))
            chain.wait()
            numbers = iot[:, 0:E].unsqueeze(1).to_broadcast([128, 3, E])
            for c, m in ((0, m1), (1, m2)):
                chain(dve.tensor_tensor(m[:], numbers, topf[:, :, c:c + 1].to_broadcast([128, 3, E]), ALU.is_equal))
            chain.wait()
            for m in (m1, m2):
                chain(dve.tensor_tensor(m[:], m[:], valid[:], ALU.mult))
            chain.wait()
            dve.tensor_tensor(msk[:], m1[:], m2[:], ALU.add).then_inc(rk_in, 1)
            dve.wait_ge(g_exp, 1)
            chain(dve.tensor_scalar(gt[:, :, 2], gt[:, :, 1], 1.0, None, ALU.add))
            chain.wait()
            chain(dve.reciprocal(gt[:, :, 3], gt[:, :, 2]))
            chain.wait()
            chain(dve.tensor_tensor(gt[:, :, 2], gt[:, :, 1], gt[:, :, 3], ALU.mult))
            chain.wait()
            chain(dve.tensor_tensor(m1[:], m1[:], gt[:, :, 3:4].to_broadcast([128, 3, E]), ALU.mult))
            chain(dve.tensor_tensor(m2[:], m2[:], gt[:, :, 2:3].to_broadcast([128, 3, E]), ALU.mult))
            chain.wait()
            chain(dve.tensor_tensor(comb[:], m1[:], m2[:], ALU.add))
            dve.wait_ge(rk_mm, 1)
            chain(dve.scalar_tensor_tensor(out=rk[:], in0=ps[:, 2, 0:3 * E].rearrange("p (i e) -> p i e", i=3),
                                           scalar=1.0, in1=msk[:], op0=ALU.add, op1=ALU.mult))
            chain.wait()
            chain(dve.tensor_scalar(rk[:], rk[:], -1.0, None, ALU.add))
            chain(dve.tensor_reduce(cnt[:, 0:1], ps[:, 3, 0:E], AX.X, ALU.max))
            chain.wait()
            chain(dve.tensor_scalar(cnt[:, 1:2], cnt[:, 0:1], 128.5, 1.0, ALU.is_gt, ALU.add))
            chain(dve.tensor_scalar(cnt[:, 2:3], cnt[:, 0:1], 256.5, None, ALU.is_gt))
            chain.wait()
            dve.tensor_tensor(cnt_i[:, 0:1], cnt[:, 1:2], cnt[:, 2:3], ALU.add).then_inc(route, 1)
            dve.wait_ge(route, 1)

            rounds = dve.value_load(cnt_i[0:1, 0:1], min_val=1, max_val=3)
            with dve.Fori(0, rounds) as r:
                with dve.Fori(0, 4) as p:
                    it = r * 4 + p
                    off = r * 96 + p * 24
                    for i in range(3):
                        for e in range(2):
                            ins = dve.tensor_scalar(oh[:, i, 128 * e:128 * e + 128], iot[:],
                                                    rk[:, i, bass.ds(p * 2 + e, 1)], None, ALU.is_equal)
                    ins.then_inc(oh_ready, 1)
                    for g in range(4):
                        dve.wait_ge(ga_mm, it * 8 + (2 * g + 2))
                        dve.tensor_copy(xg_lo[:, 2 * g:2 * g + 2, :],
                                        ps[:, 5 + 2 * (g % 2), :].rearrange("p (a c) -> p a c", a=2)).then_inc(ga_lo, 1)
                    for e in range(2):
                        dve.wait_ge(oht_mm, it * 2 + (e + 1))
                        dve.tensor_copy(oht[:, e], ps[:, 6 + e, 0:T]).then_inc(oht_cp, 1)
                    dve.wait_ge(gs_mm, it + 1)
                    for e in range(2):
                        ins = dve.tensor_copy(gs[:, e:e + 1], ps[:, 4, bass.ds(p * 2 + (E * e + e), 1)])
                    ins.then_inc(gs_cp, 1)
                    for e in range(2):
                        for q in range(4):
                            k = MOE0 + 12 * e + 2 * q
                            lo(off, k + 2, 0)
                            lo(off, k + 2, 1)
                            lo(off, k + 3, 0)
                            dve.wait_ge(m_silu, it * 8 + (4 * e + q + 1))
                            dve.wait_ge(pe_done, off * 2 + (2 * k + 4))
                            dve.tensor_tensor(hm[:, q * GQ:(q + 1) * GQ], sgm[:, q % 2], ps[:, (k + 1) % 4, 0:GQ],
                                              ALU.mult).then_inc(evac, 2)
                            lo(off, k + 3, 1)
                        for b in range(3):
                            w = 512 if b < 2 else 384
                            dve.wait_ge(hx_h, it * 6 + (3 * e + b + 1))
                            dve.tensor_tensor(hx_lo[:, 4 * b:4 * b + w // 128].rearrange("p a c -> p (a c)"),
                                              ps[:, 4 + b, 0:w],
                                              hx_hi[:, 4 * b:4 * b + w // 128].rearrange("p a c -> p (a c)").bitcast(f32),
                                              ALU.subtract).then_inc(hx_l, 1)
                        for q in range(4):
                            k = MOE0 + 12 * e + 8 + q
                            lo(off, k + 2, 0)
                            dve.wait_ge(y_h, it * 8 + (4 * e + q + 1))
                            dve.scalar_tensor_tensor(out=y_lo[:, e, q * DQ:(q + 1) * DQ], in0=ps[:, k % 4, 0:DQ],
                                                     scalar=gs[:, e:e + 1],
                                                     in1=y_hi[:, e, q * DQ:(q + 1) * DQ].bitcast(f32),
                                                     op0=ALU.mult, op1=ALU.subtract).then_inc(evac, 1)
                            lo(off, k + 2, 1)
                    for f in range(KT):
                        dve.wait_ge(scat_mm, it * 8 + (f + 1))
                        dve.tensor_tensor(x[:, f], x[:, f], ps[:, 4 + f % 4, 0:T], ALU.add).then_inc(scat_add, 1)
                dve.tensor_scalar(iot[:], iot[:], 128.0, None, ALU.add).then_inc(route, 1)
                dve.wait_ge(route, r + 2)
            norm("fin", "g_fin", 0)

        @block.tensor
        def _(pe):
            def mm3(out, w_hi, w_lo, m_hi_, m_lo_, first, last):
                pe.matmul(out, w_hi, m_hi_, start=first, stop=False)
                pe.matmul(out, w_hi, m_lo_, start=False, stop=False)
                return pe.matmul(out, w_lo, m_hi_, start=False, stop=last)

            def chunk(off, k, body):
                if not isinstance(off, int) or k >= 2:
                    pe.wait_ge(evac, off + (k - 1))
                for s in range(2):
                    pe.wait_ge(lo_done, off * 2 + (2 * k + s + 1))
                    body(k, s).then_inc(pe_done, 1)

            def chunks(k0, count, body):
                with pe.Fori(0, count // 2) as i:
                    for u in range(2):
                        chunk(i * 2, k0 + u, body)

            def slab(k, s, i, m_h, m_l, w):
                h = (2 * k + s) % 4
                c = i * 128
                return mm3(ps[:, 2 * (k % 2) + s, 0:w], whi[h][:, c:c + 128], wlo[h][:, c:c + 128],
                           m_h[:, i, :], m_l[:, i, :], i == 0, i == KT - 1)

            def proj(m_h, m_l, w):
                def body(k, s):
                    for i in range(KT):
                        last = slab(k, s, i, m_h, m_l, w)
                    return last
                return body

            def first_chunk(k, name, m_h, m_l, w):
                pe.wait_ge(lo_done, 2 * k + 2)
                if k >= 2:
                    pe.wait_ge(evac, k - 1)
                for p in range(4):
                    pe.wait_ge(n_lo, pair_of(name, p + 1))
                    for s in range(2):
                        for i in (2 * p, 2 * p + 1):
                            last = slab(k, s, i, m_h, m_l, w)
                        if p == 3:
                            last.then_inc(pe_done, 1)

            def values(k, s):
                h = (2 * k + s) % 4
                for t in range(MT):
                    for i in range(4 * s, 4 * s + 4):
                        m = slice(t * 128, t * 128 + 128)
                        w = slice((i - 4 * s) * 256, (i - 4 * s) * 256 + 256)
                        last = mm3(ps[:, 2 * (k % 2) + t, 0:256], m_hi[:, i, m], m_lo[:, i, m],
                                   whi[h][:, w], wlo[h][:, w], i == 0, i == KT - 1)
                return last

            def down(k, s):
                h = (2 * k + s) % 4
                for i in range(11 * s, 11 * s + 11):
                    c = (i - 11 * s) * 128
                    last = mm3(ps[:, 2 * (k % 2), 0:T], whi[h][:, c:c + 128], wlo[h][:, c:c + 128],
                               h_hi[:, i, :], h_lo[:, i, :], i == 0, i == FFT - 1)
                return last

            def sum_pair(name, src, j, pairs=4, w=T):
                pe.wait_ge(n_sq, sq_of(name, j + 1))
                if j == 0 and order[name]:
                    pe.wait_ge(n_rt, order[name])
                for i in (2 * j, 2 * j + 1):
                    last = pe.matmul(ps[:, 4, 0:w], ones[:], src[:, i, 0:w], start=i == 0, stop=i == 2 * pairs - 1)
                if j == pairs - 1:
                    last.then_inc(n_ss, 1)

            def whole_sum(name, src, pairs, w=T):
                pe.wait_ge(n_sq, sq_of(name, 1))
                if order[name]:
                    pe.wait_ge(n_rt, order[name])
                for i in range(2 * pairs):
                    last = pe.matmul(ps[:, 4, 0:w], ones[:], src[:, i, 0:w], start=i == 0, stop=i == 2 * pairs - 1)
                last.then_inc(n_ss, 1)

            pe.wait_ge(consts, 4)
            whole_sum("mem", sq, 4, MEM)
            for j in range(4):
                sum_pair("mix0", sq_d, j)
            for l in range(DEPTH):
                L = LAYER0[l]
                by_a = proj(a_hi, a_lo, T)
                by_m = proj(m_hi, m_lo, MEM)
                first_chunk(L, f"m{l}", m_hi, m_lo, MEM)
                if l:
                    sum_pair("mix1", sq_d, 3)
                for j in range(1, 4):
                    chunk(0, L + j, by_m)
                def gates(t):
                    if t >= 2:
                        pe.wait_ge(gates_act, 2 * G * l + 2 * t - 2)
                    for m in range(2):
                        last = pe.matmul(ps[:, 4 + 2 * (t % 2) + m, 0:T], lru_w[:, m, t], xc[:, t], start=True, stop=True)
                    last.then_inc(gates_mm, 1)

                first_chunk(L + 4, f"mix{l}", a_hi, a_lo, T)
                chunks(L + 5, 4, by_a)
                pe.wait_ge(s_lruw, 64 * (l + 1))
                pe.wait_ge(xc_done, l + 1)
                gates(0)
                gates(1)
                chunk(0, L + 9, by_a)
                gates(2)
                gates(3)
                chunks(L + 10, 4, by_a)
                chunk(0, L + 14, values)
                chunk(0, L + 15, values)
                whole_sum(f"co{l}", xc, 2)
                chunk(0, L + 16, values)
                whole_sum(f"lo{l}", ig, 2)
                chunk(0, L + 17, values)
                first_chunk(L + 18, f"g{l}", a_hi, a_lo, T)
                for j in range(1, 4):
                    chunk(0, L + 18 + j, by_a)
                    sum_pair(f"xattn{l}", sq, j - 1)
                sum_pair(f"xattn{l}", sq, 3)
                first_chunk(L + 22, f"xattn{l}", a_hi, a_lo, T)
                for j in range(1, 4):
                    chunk(0, L + 22 + j, by_a)

                def scores(h):
                    for t in range(2):
                        for d in range(HT):
                            last = pe.matmul(ps[:, 4 + h % 2, t * MEM:(t + 1) * MEM], qt[:, HT * h + d, t * 128:t * 128 + 128],
                                             kt[:, HT * h + d, :], start=d == 0, stop=d == HT - 1)
                    last.then_inc(sc_mm, 1)

                def cached(c):
                    slot = (L + 26 + c) % RAWS
                    pe.wait_ge(raw_full[slot], 16 * ((L + 26 + CACHES * l + c) // RAWS + 1))
                    return slot

                def sample_scores(b0):
                    slots = [cached(b0), cached(b0 + 1)]
                    for j in range(KT):
                        for u in range(2):
                            b = b0 + u
                            g = 32 * (b % 4)
                            last = pe.matmul(ps[g:g + 32, 0, 0:MEM], qm[:, j, b, :],
                                             raw[:, slots[u], j * MEM:(j + 1) * MEM],
                                             start=b < 4 and j == 0, stop=b >= 4 and j == KT - 1)
                            if j == KT - 1:
                                last.then_inc(cache_used, 1)

                pe.wait_ge(evac, L + 26)
                scores(0)
                scores(1)
                pe.wait_ge(qm_ready, l + 1)
                sample_scores(0)
                for h in range(HEADS):
                    c = HEADS * l + h
                    pe.wait_ge(sc_nrm, c + 1)
                    for m in range(MT):
                        for t in range(2):
                            last = pe.transpose(ps[:, 6 + h % 2, m * SEQ + t * 128:m * SEQ + t * 128 + 128],
                                                pr[h % 2][:, t, m * 128:m * 128 + 128], ident[:])
                    last.then_inc(pt_mm, 1)
                    if h + 2 < HEADS:
                        scores(h + 2)
                    if h < 3:
                        sample_scores(2 * h + 2)
                    if h == 2:
                        pe.wait_ge(cache_used, CACHES * l + 8)
                        pe.matmul(ps[0:8, 1, 0:8], ident[:, 0:8], ident[:, 0:8], start=True, stop=True).then_inc(ss_mm, 1)
                    pe.wait_ge(pt_cp, c + 1)
                    if h >= 2:
                        pe.wait_ge(at_lo, 6 * l + h - 1)
                    for d in range(HT):
                        for m in range(MT):
                            last = pe.matmul(ps[:, 2 + h % 2, d * SEQ:(d + 1) * SEQ],
                                             vt[:, m, h * 256 + d * 128:h * 256 + d * 128 + 128], ptr[h % 2][:, m],
                                             start=m == 0, stop=m == MT - 1)
                    last.then_inc(ov_mm, 1)

                pe.wait_ge(ss_nrm, l + 1)
                pe.wait_ge(pt_cp, HEADS * l + 4)
                for m in range(MT):
                    last = pe.transpose(ps[:, 6, m * 128:m * 128 + 128], ps_s[:, m * 128:m * 128 + 128], ident[:])
                last.then_inc(st_mm, 1)
                pe.wait_ge(st_cp, 4 * l + 4)
                pe.wait_ge(at_lo, 6 * l + 4)
                for b0 in range(0, DEC, 2):
                    slots = [cached(DEC + b0), cached(DEC + b0 + 1)]
                    for h in range(HEADS):
                        for m in range(MT):
                            for u in range(2):
                                b = b0 + u
                                g = 32 * (b % 4)
                                o = m * D + h * 256
                                last = pe.matmul(ps[g:g + 32, h, 0:256], ptm[:, m, h, b, :], raw[:, slots[u], o:o + 256],
                                                 start=b < 4 and m == 0, stop=b >= 4 and m == MT - 1)
                                if h == HEADS - 1 and m == MT - 1:
                                    last.then_inc(cache_used, 1)
                pe.wait_ge(cache_used, CACHES * l + 16)
                pe.matmul(ps[0:8, 7, 0:8], ident[:, 0:8], ident[:, 0:8], start=True, stop=True).then_inc(so_mm, 1)
                pe.wait_ge(so_cp, l + 1)
                for j in range(KT):
                    last = pe.transpose(ps[:, 4 + j // 4, (j % 4) * 128:(j % 4) * 128 + 128],
                                        o_s[:, j * 128:j * 128 + 128], ident[:])
                    if j % 4 == 3:
                        last.then_inc(sot_mm, 1)
                pe.wait_ge(at_lo, 6 * l + 6)
                chunk(0, L + 26, by_a)
                for j in range(1, 4):
                    chunk(0, L + 26 + j, by_a)
                    sum_pair(f"ffn{l}", sq, j - 1)
                sum_pair(f"ffn{l}", sq, 3)
                if l == 0:
                    first_chunk(GU0, "ffn0", a_hi, a_lo, T)
                    chunks(GU0 + 1, 20, by_a)
                    chunk(0, GU0 + 21, by_a)
                    pe.wait_ge(ff_h, 1)
                    for j in range(8):
                        chunk(0, DOWN0 + j, down)
                        if j in (2, 4, 6):
                            sum_pair("mix1", sq_d, j // 2 - 1)

            pe.wait_ge(n_lo, pair_of("ffn1", 4))
            for i in range(6):
                t, half = i // 2, i % 2
                c0, w = TT[t]
                if i >= 2:
                    pe.wait_ge(tk_cp, i - 1)
                    pe.wait_ge(tk_cl, i - 1)
                for part, src in enumerate((a_hi, a_lo)):
                    for f in range(4):
                        last = pe.transpose(ps[0:w, 4 + 2 * (i % 2) + part, f * 128:f * 128 + 128],
                                            src[:, 4 * half + f, c0:c0 + w].bitcast(f32), ident[:])
                    last.then_inc(tk_mm, 1)
            pe.wait_ge(wr_ready, 1)
            pe.wait_ge(evac, MOE0)
            for i in range(KT):
                last = mm3(ps[:, 0, 0:T], wr_hi[:, i], wr_lo[:, i], a_hi[:, i], a_lo[:, i], i == 0, i == KT - 1)
            last.then_inc(lg_mm, 1)
            pe.wait_ge(lg_cp, 1)
            for i, (c0, w) in enumerate(TT):
                last = pe.transpose(ps[0:w, 1, i * E:(i + 1) * E], lg[0:E, c0:c0 + w], ident[0:E, 0:E])
            last.then_inc(lt_mm, 1)
            pe.wait_ge(rk_in, 1)
            for i in range(3):
                for j in range(i + 1):
                    pe.matmul(ps[:, 2, i * E:(i + 1) * E], tri[:] if j == i else one_b[:], msk[:, j],
                              start=j == 0, stop=j == i)
            for j in range(3):
                last = pe.matmul(ps[:, 3, 0:E], one_b[:], msk[:, j], start=j == 0, stop=j == 2)
            last.then_inc(rk_mm, 1)

            pe.wait_ge(tk_cp, 6)
            pe.wait_ge(tk_cl, 6)
            pe.wait_ge(route, 1)
            rounds = pe.value_load(cnt_i[0:1, 0:1], min_val=1, max_val=3)
            ohf = oh[:].bitcast(f32)
            with pe.Fori(0, rounds) as r:
                with pe.Fori(0, 4) as p:
                    it = r * 4 + p
                    off = r * 96 + p * 24
                    pe.wait_ge(oh_ready, it + 1)
                    pe.wait_ge(scat_add, it * 8 + 1)
                    for g in range(4):
                        if g >= 2:
                            pe.wait_ge(ga_hi, it * 4 + (g - 1))
                            pe.wait_ge(ga_lo, it * 4 + (g - 1))
                        for part, src in enumerate((ht_hi, ht_lo)):
                            for a in range(2):
                                f = 2 * g + a
                                for i in range(3):
                                    last = pe.matmul(ps[:, 4 + 2 * (g % 2) + part, a * 256:a * 256 + 256],
                                                     src[:, i, f * 128:f * 128 + 128], oh[:, i, :],
                                                     start=i == 0, stop=i == 2)
                            last.then_inc(ga_mm, 1)
                    pe.wait_ge(ga_hi, it * 4 + 4)
                    pe.wait_ge(ga_lo, it * 4 + 4)
                    for e in range(2):
                        for i in range(3):
                            last = pe.transpose(ps[:, 6 + e, i * 128:i * 128 + 128], ohf[:, i, 128 * e:128 * e + 128],
                                                ident[:])
                        last.then_inc(oht_mm, 1)
                    for e in range(2):
                        for i in range(3):
                            last = pe.matmul(ps[:, 4, E * e:E * e + E], ohf[:, i, 128 * e:128 * e + 128], comb[:, i],
                                             start=i == 0, stop=i == 2)
                    last.then_inc(gs_mm, 1)

                    def expert_chunk(k, body):
                        pe.wait_ge(evac, off + (k - 3))
                        for s in range(2):
                            pe.wait_ge(lo_done, off * 2 + (2 * k + s + 1))
                            body(k, s).then_inc(pe_done, 1)

                    for e in range(2):
                        def gate_up(k, s):
                            h = (2 * k + s) % 4
                            for i in range(4 * s, 4 * s + 4):
                                w = slice((i - 4 * s) * GQ, (i - 4 * s + 1) * GQ)
                                t = slice(128 * e, 128 * e + 128)
                                last = mm3(ps[:, k % 4, 0:GQ], xg_hi[:, i, t], xg_lo[:, i, t], whi[h][:, w],
                                           wlo[h][:, w], i == 0, i == KT - 1)
                            return last

                        def down_q(k, s):
                            h = (2 * k + s) % 4
                            for i in range(6 * s, 6 + 5 * s):
                                w = slice((i - 6 * s) * DQ, (i - 6 * s + 1) * DQ)
                                last = mm3(ps[:, k % 4, 0:DQ], hx_hi[:, i], hx_lo[:, i], whi[h][:, w],
                                           wlo[h][:, w], i == 0, i == FET - 1)
                            return last

                        def turn(b):
                            if e:
                                pe.wait_ge(hx_l, it * 6 + (b + 1))
                            for a in range(4 if b < 2 else 3):
                                f = 4 * b + a
                                last = pe.transpose(ps[:, 4 + b, a * 128:a * 128 + 128], hm[:, f * 128:f * 128 + 128],
                                                    ident[:])
                            last.then_inc(hx_mm, 1)

                        K = MOE0 + 12 * e
                        for c in range(7):
                            expert_chunk(K + c, gate_up)
                        if e == 0:
                            pe.wait_ge(gs_cp, it + 1)
                            pe.wait_ge(oht_cp, it * 2 + 2)
                        pe.wait_ge(evac, off + (K + 4))
                        turn(0)
                        expert_chunk(K + 7, gate_up)
                        pe.wait_ge(evac, off + (K + 6))
                        turn(1)
                        pe.wait_ge(evac, off + (K + 8))
                        turn(2)
                        pe.wait_ge(hx_l, it * 6 + (3 * e + 3))
                        for c in range(8, 12):
                            expert_chunk(K + c, down_q)
                    pe.wait_ge(evac, off + (MOE0 + 24))
                    for f in range(KT):
                        if f >= 4:
                            pe.wait_ge(scat_add, it * 8 + (f - 2))
                        for e in range(2):
                            for part, y in enumerate((y_hi, y_lo)):
                                last = pe.matmul(ps[:, 4 + f % 4, 0:T], y[:, e, f * 128:f * 128 + 128], oht[:, e],
                                                 start=e == 0 and part == 0, stop=e == 1 and part == 1)
                        last.then_inc(scat_mm, 1)
            for j in range(4):
                sum_pair("fin", sq, j)


def kernel(**inputs):
    import concourse.bacc as bacc
    from concourse.bass_utils import run_bass_kernel_spmd as run

    a = {k: np.asarray(v) for k, v in inputs.items()}
    c = np.ascontiguousarray

    def rows(w, k):
        return w.reshape(*w.shape[:-2], k, 128, w.shape[-1]).swapaxes(-3, -2)

    def dense(w):
        n = w.shape[1] // 256
        return rows(w, KT).reshape(128, KT, n, 256).transpose(2, 0, 1, 3).reshape(n, 128, DW)

    def slabs(w):
        return dense(w).reshape(-1, 128, KT, 2, 128).swapaxes(2, 3).reshape(-1, 128, DW)

    def vec(v):
        v = v.reshape(*v.shape[:-1], v.shape[-1] // 128, 128)
        return np.moveaxis(v, -1, 0)

    x = np.concatenate([a["x_prompt"][0], a["x_sample"][:, 0]], axis=0)
    x_in = c(rows(x.T, KT))
    mem_in = c(rows(a["mem_prompt"][0].T, KT))
    layers, packs = [], []
    for l in range(DEPTH):
        B, C, X, XL, GA = np.split(a["w_in"][l], 5, axis=1)
        w_in = np.concatenate([XL, GA, C, X, B], axis=1)
        layers.append(np.concatenate([slabs(a["w_k"][l]), slabs(w_in), dense(a["w_v"][l]), slabs(a["w_mix_out"][l]),
                                      slabs(a["w_q"][l]), slabs(a["w_o"][l])]))
        p = [vec(a["norm_mix"][l]), vec(a["norm_xattn"][l]), vec(a["norm_mem"][l]), vec(a["norm_ffn"][l]),
             vec(a["norm_final"]), vec(a["w_short_conv"][l]), vec(a["w_lru_conv"][l]), vec(a["b_lru_conv"][l]),
             vec(a["b_lru_a"][l]), vec(a["b_lru_x"][l]), vec(a["lru_lambda"][l]), vec(a["norm_conv_out"][l]),
             vec(a["norm_lru_out"][l]),
             vec(a["state_shortconv"][l]).transpose(0, 3, 2, 1), vec(a["state_lru_conv"][l]).transpose(0, 3, 2, 1),
             vec(a["state_lru_h"][l]).transpose(0, 2, 1)]
        packs.append(np.concatenate([q.reshape(128, -1) for q in p], axis=1))
    gate, up = (rows(a[k][0], KT).reshape(128, KT, FFT, 128) for k in ("w_ff_gate", "w_ff_up"))
    gu = np.stack([gate, up], axis=0).transpose(3, 1, 0, 2, 4).reshape(FFT, 128, DW)
    down = rows(a["w_ff_down"][0], FFT).reshape(128, FFT, KT, 128).transpose(2, 0, 1, 3).reshape(KT, 128, CW)
    mg, mu = (rows(a[k][0], KT).reshape(E, 128, KT, 4, GQ).transpose(0, 3, 1, 2, 4).reshape(E, 4, 1, 128, CW)
              for k in ("w_moe_gate", "w_moe_up"))
    md = rows(a["w_moe_down"][0], FET).reshape(E, 128, FET, 4, DQ).transpose(0, 3, 1, 2, 4).reshape(E, 4, 128, CW)
    moe = np.concatenate([np.concatenate([mg, mu], axis=2).reshape(E, 8, 128, CW), md], axis=1).reshape(E * 12, 128, CW)
    lru = np.stack([a["w_lru_a"], a["w_lru_x"]], axis=1).reshape(DEPTH, 2, G, 2, 64, 64).transpose(0, 1, 3, 4, 2, 5)
    router = rows(a["w_router"][0], KT)
    kc = a["cache_mem_k"].reshape(DEPTH, DEC, MEM, KT, 128).transpose(0, 1, 4, 3, 2).reshape(DEPTH, DEC, 128, DW)
    vc = a["cache_mem_v"].reshape(DEPTH, DEC, MT, 128, D).transpose(0, 1, 3, 2, 4).reshape(DEPTH, DEC, 128, DW)

    ins = dict(x_in=x_in, mem_in=mem_in, pk_in=np.stack(packs, axis=1), dense_in=np.stack(layers), gu_in=gu,
               down_in=down, moe_in=moe, lru_in=lru, router_in=router, cache_in=np.concatenate([kc, vc], axis=1))
    outs = dict(y_out=(128, KT, T), k_out=(DEPTH, 128, KT, MEM), v_out=(DEPTH, 128, MT, D),
                small_out=(DEPTH, 128, G, NOC))
    nc = bacc.Bacc("TRN2", target_bir_lowering=False, num_devices=1)
    ins = {f"{k}_dram": c(v) for k, v in ins.items()}
    aps = [nc.dram_tensor(k, v.shape, mybir.dt.from_np(v.dtype), kind="ExternalInput").ap() for k, v in ins.items()]
    aps += [nc.dram_tensor(k, s, mybir.dt.float32, kind="ExternalOutput").ap() for k, s in outs.items()]
    build(nc, *aps)
    r = run(nc, [ins], core_ids=[0]).results[0]
    y = r["y_out"].transpose(1, 0, 2).reshape(D, T).T
    k_mem = r["k_out"].transpose(0, 3, 2, 1).reshape(DEPTH, 1, MEM, HEADS, 256)
    v_mem = r["v_out"].transpose(0, 2, 1, 3).reshape(DEPTH, 1, MEM, HEADS, 256)
    s = r["small_out"].transpose(0, 3, 2, 1).reshape(DEPTH, NOC, 512)

    def part(name, n):
        return s[:, OC[name]:OC[name] + n]

    return (c(y[None, 0:SEQ]), c(y[SEQ:T, None]), c(part("p_sc", 2)[:, None]), c(part("p_lc", 3)[:, None]),
            c(part("p_h", 1)), c(k_mem), c(v_mem),
            c(part("s_sc", 16).reshape(DEPTH, 2, DEC, 512).swapaxes(1, 2)),
            c(part("s_lc", 24).reshape(DEPTH, 3, DEC, 512).swapaxes(1, 2)), c(part("s_h", 8)))
```

```python
import concourse.bass as bass
from concourse import mybir
from contextlib import ExitStack
import numpy as np

D = 1024
KT = D // 128
SEQ, DEC = 256, 8
T = SEQ + DEC
DEPTH = 2
G = 4
NZ = 20
MEM = 256
MT = MEM // 128
HEADS, HT = 4, 2
FF, FFT = 2816, 22
E, FE = 8, 1408
FET = FE // 128
EPS = 1e-6
AREA = 20800
RAWS = 4
CW = 2816
DW = 2048
GQ, DQ = 352, 256
TT = ((0, 128), (128, 128), (256, 8))
PAIR_CHUNKS = 24
CACHES = 16
RING_CACHES = 12
HW = 1536

K_A, IN, V, K_B, MIX, K_C, Q, O = 0, 2, 12, 16, 17, 21, 22, 26
LAYER_CHUNKS = 30
FFN_CHUNKS = 30
LAYER0 = (0, LAYER_CHUNKS + FFN_CHUNKS)
GU0, DOWN0 = LAYER_CHUNKS, LAYER_CHUNKS + 22
MOE0 = LAYER0[1] + LAYER_CHUNKS



def halves(k):
    if k >= MOE0 and (k - MOE0) % PAIR_CHUNKS >= 16:
        return (0, 6 * DQ), (6 * DQ, 5 * DQ)
    w = (CW if k >= MOE0 or DOWN0 <= k < LAYER0[1] else DW) // 2
    return (0, w), (w, w)


def fills(k):
    return (k + RING_CACHES * sum(k >= LAYER0[l] + O for l in range(DEPTH))) // RAWS + 1


def cache_place(l, c):
    return LAYER0[l] + O + RING_CACHES * l + (c - 2 if c < 8 else c - 4)


ZL, ZC, ZX, ZG, ZB = 0, 4, 8, 12, 16

_w = dict(g_mix=8, g_x=8, g_mem=8, g_ffn=8, g_fin=8, w_sc=12, w_lc=16, b_lc=4, b_a=4, b_x=4, lam=4,
          g_co=4, g_lo=4, st_sc=64, st_lc=96, st_h=32)
PK = {}
_at = 0
for _k, _n in _w.items():
    PK[_k] = _at
    _at += _n
NPK = _at
OC = dict(p_sc=0, p_lc=2, p_h=5, s_sc=6, s_lc=22, s_h=46)
NOC = 54


def build(nc, x_in, mem_in, pk_in, dense_in, gu_in, down_in, moe_in, lru_in, router_in, cache_in,
          y_out, k_out, v_out, small_out):
    f32, f32r, bf16, i32, u32 = (mybir.dt.float32, mybir.dt.float32r, mybir.dt.bfloat16,
                                 mybir.dt.int32, mybir.dt.uint32)
    ALU, ACT, AX = mybir.AluOpType, mybir.ActivationFunctionType, mybir.AxisListType
    ctx = ExitStack()
    with ctx:
        def sb(name, shape, dt=f32):
            return ctx.enter_context(nc.sbuf_tensor(name, shape, dt))

        def sem(name):
            return ctx.enter_context(nc.semaphore(name))

        raw = sb("raw", [128, RAWS, CW])
        whi = [sb(f"whi{i}", [128, HW], f32r) for i in range(4)]
        wlo = [sb(f"wlo{i}", [128, HW], f32r) for i in range(4)]
        x = sb("x", [128, KT, T])
        a_hi = sb("a_hi", [128, KT, T], f32r)
        a_lo = sb("a_lo", [128, KT, T], f32r)
        pk = sb("pk", [128, DEPTH, NPK])
        ones = sb("ones", [128, 128])
        ident = sb("ident", [128, 128])
        epsb = sb("epsb", [128, 1])
        warm = sb("warm", [128, 1])
        sml = sb("sml", [128, G, NOC])
        nsp = sb("nsp", [128, DEPTH, 2, G])
        spt = sb("spt", [128, 4, DEPTH, G])
        rt = sb("rt", [128, T])
        rstd = sb("rstd", [128, T])
        stat = sb("stat", [128, 64])
        area = sb("area", [128, AREA])
        probe = nc.sbuf_base
        base = probe - AREA * 4

        def at(name, offset, shape, dt=f32):
            size = int(np.prod(shape[1:])) * (2 if dt == bf16 else 4)
            assert offset + size <= AREA * 4, name
            return nc.alloc_sbuf_tensor_at(name, shape, dt, offset=base + offset)

        m_hi = at("m_hi", 0, [128, KT, MEM], f32r)
        m_lo = at("m_lo", 8192, [128, KT, MEM], f32r)
        lru_w = at("lru_w", 32768, [128, 2, G, 128])
        memn = at("memn", 16384, [128, KT, MEM])
        spare = at("spare", 0, [128, 2, DW])
        rstm = at("rstm", 79488, [128, MEM])
        sq_x = at("sq_x", 62080, [128, KT, T])
        kt = at("kt", 24576, [128, KT, MEM])
        vt = at("vt", 32768, [128, MT, D])
        z = at("z", 40960, [128, NZ, T])
        sq = at("sq", 40960, [128, KT, T])
        xc, rg, ig, av = (at(nm, 62080 + 4224 * i, [128, G, T]) for i, nm in enumerate(("xc", "rg", "ig", "av")))
        th = at("th", 40960, [128, G, T])
        hs = at("hs", 45184, [128, G, T])
        hf = at("hf", 71040, [128, KT, T])
        qt = at("qt", 40960, [128, KT, T])
        sq_d = at("sq_d", 71040, [128, KT, T])
        qm = at("qm", 49408, [128, KT, DEC, 32])
        pr = [at(f"pr{i}", 57600 + 2048 * i, [128, 2, MEM]) for i in range(2)]
        ptr = [at(f"ptr{i}", 61696 + 2048 * i, [128, MT, SEQ]) for i in range(2)]
        ptm = at("ptm", 65792, [128, MT, HEADS, DEC, 32])
        ps_s = at("ps_s", 73984, [128, MEM])
        o_s = at("o_s", 75008, [128, D])
        h_hi = at("h_hi", 24576, [128, FFT, T], f32r)
        h_lo = at("h_lo", 47808, [128, FFT, T], f32r)
        sg = [at(f"sg{i}", 71040 + 1056 * i, [128, T]) for i in range(2)]
        hff = [at(f"hff{i}", 73152 + 1056 * i, [128, T]) for i in range(2)]
        ht_hi = at("ht_hi", 0, [128, 3, D], f32r)
        ht_lo = at("ht_lo", 12288, [128, 3, D], f32r)
        wr_hi = at("wr_hi", 24576, [128, KT, 128], f32r)
        wr_lo = at("wr_lo", 28672, [128, KT, 128], f32r)
        xg_hi = at("xg_hi", 24576, [128, KT, 256], f32r)
        xg_lo = at("xg_lo", 32768, [128, KT, 256], f32r)
        oh = at("oh", 40960, [128, 3, 256], f32r)
        oht = at("oht", 44032, [128, 2, T], f32r)
        sgm = at("sgm", 46144, [128, 2, GQ])
        hm = at("hm", 48960, [128, FE])
        hx_hi, hx_lo = ([at(f"{nm}{e}", 54592 + 5632 * (2 * e + part), [128, FET, 128], f32r) for e in range(2)]
                        for part, nm in enumerate(("hx_hi", "hx_lo")))
        lg = at("lg", 32768, [128, T])
        rw = at("rw", 33824, [128, KT, E])
        iot_i = at("iot_i", 34080, [128, 128], i32)
        lt = at("lt", 34592, [128, 3, E])
        top = at("top", 34688, [128, 3, 8])
        topi = at("topi", 34784, [128, 3, 8], u32)
        topf = at("topf", 34880, [128, 3, 8])
        m1 = at("m1", 80576, [128, 3, E])
        m2 = at("m2", 80672, [128, 3, E])
        msk = at("msk", 35168, [128, 3, E], bf16)
        gt = at("gt", 80768, [128, 3, 4])
        tri = at("tri", 35296, [128, 128], bf16)
        one_b = at("one_b", 35552, [128, 128], bf16)
        cnt = at("cnt", 80832, [128, 8])
        valid = at("valid", 35840, [128, 3, E])
        iot = at("iot", 79488, [128, 128])
        comb = at("comb", 80000, [128, 3, E + 2])
        rk = at("rk", 80128, [128, 3, 4, E])
        cnt_i = at("cnt_i", 80512, [128, 8], i32)
        gs = at("gs", 80544, [128, 2])

        ps = ctx.enter_context(nc.psum_tensor("ps", [128, 8, 512], f32))

        raw_full = [sem(f"raw_full{i}") for i in range(RAWS)]
        spare_full = [sem(f"spare_full{i}") for i in range(2)]
        hi_done, lo_done, pe_done, evac = sem("hi_done"), sem("lo_done"), sem("pe_done"), sem("evac")
        s_mem = [sem(f"mem_in{i}") for i in range(2)]
        s_par, s_x, s_lruw, s_small, s_kv, s_y, s_rw = (sem(n) for n in (
            "params_in", "x_in", "lru_w_in", "small_out", "kv_out", "y_out", "router_in"))
        consts, dve_c = sem("consts"), sem("dve_chain")
        n_sq, n_ss, n_rt, n_h, n_hi, n_lo = (sem(n) for n in (
            "norm_squares", "norm_sum", "norm_root", "norm_scaled", "norm_hi", "norm_lo"))
        xc_done, gates_mm, gates_act, gate_a, u_w, u_sq = (sem(n) for n in (
            "xc_done", "gates_mm", "gates_act", "lru_a_done", "lru_w_done", "lru_root"))
        gelu_done, sm_done, lruw_zero = sem("gelu_done"), sem("small_ready"), sem("lru_w_zero")
        sc_mm, sc_max, sc_exp, sc_nrm, pt_mm, pt_cp, ov_mm, at_hi, at_lo = (sem(n) for n in (
            "score_mm", "score_max", "score_exp", "probs_ready", "probs_t_mm", "probs_t_ready", "attn_mm",
            "attn_hi", "attn_lo"))
        qm_ready, ss_max, ss_exp, ss_nrm, st_mm, st_cp, so_cp, sot_mm = (sem(n) for n in (
            "qm_ready", "s_score_max", "s_score_exp", "s_probs_ready", "s_probs_t_mm", "s_probs_t_ready",
            "s_attn_copied", "s_attn_t_mm"))
        comb_ready, sp_ready = sem("combine_weights"), sem("softplus_ready")
        n_fold, pool_c, iu_done, sc_done = (sem(n) for n in (
            "norm_squares_folded", "pool_chain", "lru_gated_input", "short_conv_done"))
        cache_used, zeros, cx_done = sem("cache_used"), sem("masks_zeroed"), sem("short_conv_input")
        silu_done, ff_h = sem("silu_done"), sem("ff_h_ready")
        tk_mm, tk_cp, wr_ready, lg_mm, lg_cp, lt_mm, rk_in, rk_mm, route = (sem(n) for n in (
            "tok_major_mm", "tok_major_copied", "router_split", "logits_mm", "logits_copied", "logits_t_mm",
            "rank_in", "rank_mm", "routed"))
        g_in, g_exp, sp_in, sp_exp, ya_done, gs_cp = (sem(n) for n in (
            "gate_diff", "gate_exp", "softplus_in", "softplus_exp", "ya_ready", "slot_gate_ready"))
        oh_ready, ga_mm, ga_hi, ga_lo, oht_mm, oht_cp, gs_mm = (sem(n) for n in (
            "onehot_ready", "gather_mm", "gather_hi", "gather_lo", "onehot_t_mm", "onehot_t_ready", "slot_gate_mm"))
        m_silu, hx_mm, hx_h, hx_l, y_h, scat_mm, scat_add = (sem(n) for n in (
            "moe_silu", "moe_ht_mm", "moe_ht_hi", "moe_ht_lo", "moe_y_hi", "scatter_mm",
            "scatter_added"))

        class Chain:

            def __init__(self, eng, s):
                self.eng, self.sem, self.n, self.off = eng, s, 0, 0

            def __call__(self, ins):
                ins.then_inc(self.sem, 1)
                self.n += 1

            def wait(self):
                self.eng.wait_ge(self.sem, self.n + self.off)

        NORMS = ["mem", "mix0", "co0", "lo0", "xattn0", "ffn0", "mix1", "co1", "lo1", "xattn1", "ffn1", "fin"]
        order = {name: i for i, name in enumerate(NORMS)}
        FOLDED = ["co0", "lo0", "xattn0", "ffn0", "mix1", "co1", "lo1", "xattn1", "ffn1"]

        def y_part(buf, e, q):
            return buf[:, 4 * e + q, 0:DQ]

        def sample_out(g):
            return ps[:, 0:2, :].rearrange("p a (k c) -> p (a k) c", c=128)[:, :, 4 * g:4 * g + 100:33]

        block = ctx.enter_context(nc.Block())

        SPLITS = ["m0", "mix0", "g0", "xattn0", "ffn0", "m1", "mix1", "g1", "xattn1", "ffn1", "fin"]

        def nh_of(name, k):
            return KT * SPLITS.index(name) + k

        def pair_of(name, k):
            return 4 * SPLITS.index(name) + k

        def sq_of(name, k):
            n = 0
            for q in NORMS:
                if q == name:
                    return n + k
                n += 1 if q[:2] in ("co", "lo") else 4

        @block.sync
        def _(sp):
            def load(src, off, k, width):
                if k >= RAWS:
                    sp.wait_ge(lo_done, off * 2 + (2 * k - 6))
                sp.dma_start(raw[:, k % RAWS, 0:width], src).then_inc(raw_full[k % RAWS], 16)

            def looped(src, k0, count, width):
                full = count // RAWS
                with sp.Fori(0, full) as i:
                    for u in range(RAWS):
                        load(src(i * RAWS + u), i * RAWS, k0 + u, width)
                for j in range(full * RAWS, count):
                    load(src(j), 0, k0 + j, width)

            def cache(l, c):
                k = cache_place(l, c) % RAWS
                sp.dma_start(raw[:, k, 0:DW], cache_in[l, c]).then_inc(raw_full[k], 16)

            for j in range(2):
                sp.dma_start(memn[:, 4 * j:4 * j + 4], mem_in[:, 4 * j:4 * j + 4]).then_inc(s_mem[j], 16)
            sp.dma_start(pk[:], pk_in).then_inc(s_par, 16)
            load(dense_in[0, 0], 0, 0, DW)
            sp.dma_start(x[:], x_in).then_inc(s_x, 16)
            for l in range(DEPTH):
                L = LAYER0[l]
                used = CACHES * l
                first = 0 if l else RAWS
                for j in range(1, first):
                    load(dense_in[l, j], 0, L + j, DW)
                looped(lambda j: dense_in[l, j + first], L + first, O - first, DW)
                for i in range(2):
                    sp.wait_ge(lo_done, 2 * (L + Q + i) + 2)
                    cache(l, 2 + i)
                sp.wait_ge(pe_done, 2 * (L + K_C) + 2)
                for c in range(2):
                    sp.dma_start(spare[:, c], cache_in[l, c]).then_inc(spare_full[c], 16)
                for i in range(2, 4):
                    sp.wait_ge(lo_done, 2 * (L + Q + i) + 2)
                    cache(l, 2 + i)
                for c in range(2):
                    sp.wait_ge(cache_used, used + c + 1)
                    sp.dma_start(spare[:, c], cache_in[l, 8 + c]).then_inc(spare_full[c], 16)
                for c, held in ((6, 2), (7, 3), (10, 4), (11, 5), (12, 6), (13, 7), (14, 10), (15, 11)):
                    sp.wait_ge(cache_used, used + held + 1)
                    cache(l, c)
                for i in range(4):
                    sp.wait_ge(cache_used, used + 13 + i)
                    k = (L + O + i) % RAWS
                    sp.dma_start(raw[:, k, 0:DW], dense_in[l, O + i]).then_inc(raw_full[k], 16)
                if l == 0:
                    looped(lambda j: gu_in[j], GU0, 22, DW)
                    looped(lambda j: down_in[j], DOWN0, 8, CW)
            for u in range(RAWS):
                load(moe_in[u], 0, MOE0 + u, CW)
            sp.wait_ge(route, 1)
            rounds = sp.value_load(cnt_i[0:1, 0:1], min_val=1, max_val=3)
            with sp.Fori(0, rounds) as r:
                with sp.Fori(0, 3) as p:
                    for u in range(RAWS, RAWS + PAIR_CHUNKS):
                        load(moe_in[p * PAIR_CHUNKS + u], r * 96 + p * 24, MOE0 + u, CW)
                for u in range(72 + RAWS, 96 + RAWS):
                    load(moe_in[u % 96], r * 96, MOE0 + u, CW)
            for j in range(2):
                sp.wait_ge(n_h, nh_of("fin", 4 * j + 4))
                sp.dma_start(y_out[:, 4 * j:4 * j + 4], hf[:, 4 * j:4 * j + 4]).then_inc(s_y, 16)
            sp.wait_ge(s_y, 32)

        @block.gpsimd
        def _(pool):
            fold_chain = Chain(pool, pool_c)

            def fold(name, buf):
                for j in range(3):
                    pool.wait_ge(n_sq, sq_of(name, j + 1))
                    fold_chain(pool.tensor_tensor(buf[:, 2 * j], buf[:, 2 * j], buf[:, 2 * j + 1], ALU.add))
                    fold_chain.wait()
                    if j:
                        ins = pool.tensor_tensor(buf[:, 0], buf[:, 0], buf[:, 2 * j], ALU.add)
                        if j == 1:
                            fold_chain(ins)
                        else:
                            ins.then_inc(n_fold, 1)

            def fold_group(name, buf):
                pool.wait_ge(n_sq, sq_of(name, 1))
                fold_chain(pool.tensor_tensor(buf[:, 0:2], buf[:, 0:2], buf[:, 2:4], ALU.add))
                fold_chain.wait()
                pool.tensor_tensor(buf[:, 0], buf[:, 0], buf[:, 1], ALU.add).then_inc(n_fold, 1)

            pool.memset(ones[:], 1.0).then_inc(consts, 1)
            pool.memset(ident[:], 0.0).then_inc(consts, 1)
            pool.memset(epsb[:], EPS).then_inc(consts, 1)
            pool.wait_ge(consts, 3)
            pool.affine_select(out=ident[:], in_=ident[:], compare_op=ALU.not_equal, fill=1.0, base=0,
                               pattern=[[-1, 128]], channel_multiplier=1).then_inc(consts, 1)
            for l in range(DEPTH):
                L = LAYER0[l]
                if l:
                    pool.wait_ge(pe_done, 2 * L)
                pool.memset(lru_w[:], 0.0).then_inc(lruw_zero, 1)
                pool.wait_ge(lruw_zero, l + 1)
                for m in range(2):
                    for half in range(2):
                        q = slice(64 * half, 64 * half + 64)
                        pool.dma_start(lru_w[q, m, :, q], lru_in[l, m, half]).then_inc(s_lruw, 16)
                pool.wait_ge(evac, L + IN + 6)
                pool.tensor_tensor(z[:, ZC:ZC + G], z[:, ZC:ZC + G], z[:, ZX:ZX + G], ALU.mult).then_inc(cx_done, 1)
                pool.wait_ge(gates_act, 2 * G * (l + 1))
                pool.tensor_tensor(ig[:], ig[:], xc[:], ALU.mult).then_inc(iu_done, 1)
                pool.wait_ge(evac, L + V)
                pool.wait_ge(sc_done, l + 1)
                pool.tensor_tensor(z[:, ZX:ZX + G], z[:, ZX:ZX + G], z[:, ZB:ZB + G], ALU.mult).then_inc(ya_done, 1)
                fold_group(f"co{l}", xc)
                fold_group(f"lo{l}", ig)
                pool.wait_ge(evac, L + V + 4)
                pool.dma_start(v_out[l], vt[:]).then_inc(s_kv, 16)
                pool.wait_ge(sm_done, l + 1)
                pool.dma_start(small_out[l], sml[:]).then_inc(s_small, 16)
                fold(f"xattn{l}", sq)
                pool.wait_ge(evac, L + K_C + 1)
                pool.dma_start(k_out[l], kt[:]).then_inc(s_kv, 16)
                pool.wait_ge(n_lo, pair_of(f"xattn{l}", 4))
                pool.memset(qm[:], 0.0).then_inc(zeros, 1)
                pool.memset(ptm[:], 0.0).then_inc(zeros, 1)
                if l == DEPTH - 1:
                    pool.wait_ge(s_small, 16 * DEPTH)
                    pool.wait_ge(s_kv, 32 * DEPTH)
                    pool.wait_ge(at_lo, 6 * DEPTH)
                    pool.dma_start(rw[:], router_in).then_inc(s_rw, 16)
                    pool.memset(wr_hi[:].bitcast(f32), 0.0).then_inc(consts, 1)
                    pool.memset(wr_lo[:].bitcast(f32), 0.0).then_inc(consts, 1)
                    pool.iota(iot_i[:], pattern=[[1, 128]], base=0, channel_multiplier=0).then_inc(consts, 1)
                    pool.memset(one_b[:], 1.0).then_inc(consts, 1)
                    pool.memset(valid[:], 1.0).then_inc(consts, 1)
                    pool.memset(ht_hi[:, 2].bitcast(f32), 0.0).then_inc(consts, 1)
                    pool.memset(ht_lo[:, 2].bitcast(f32), 0.0).then_inc(consts, 1)
                    pool.wait_ge(consts, 11)
                    pool.affine_select(out=valid[:, 2], in_=valid[:, 2], compare_op=ALU.is_gt, fill=0.0, base=DEC,
                                       pattern=[[0, E]], channel_multiplier=-1).then_inc(consts, 1)
                    pool.affine_select(out=tri[:], in_=one_b[:], compare_op=ALU.is_gt, fill=0.0, base=0,
                                       pattern=[[1, 128]], channel_multiplier=-1).then_inc(consts, 1)
                fold(f"ffn{l}", sq)
                if l == 0:
                    fold("mix1", sq_d)

        @block.scalar
        def _(act):
            def hi(off, k, s):
                c, w = halves(k)[s]
                m = 2 * k + s
                if s == 0:
                    act.wait_ge(raw_full[k % RAWS], off * (16 // RAWS) + 16 * fills(k))
                if m >= 4:
                    act.wait_ge(pe_done, off * 2 + (m - 3))
                act.activation(whi[m % 4][:, 0:w], raw[:, k % RAWS, c:c + w], ACT.Copy).then_inc(hi_done, 1)

            def step(off, k, body=None, first=False):
                if not first:
                    hi(off, k + 2, 0)
                if body:
                    body()
                if first:
                    hi(off, k + 2, 0)
                hi(off, k + 2, 1)

            def load_table(function):
                act.activation(warm[:], epsb[:], function)

            def square(dst, src):
                act.activation(dst, src, ACT.Square).then_inc(n_sq, 1)

            def root(name, scale):
                w = MEM if name == "mem" else T
                act.wait_ge(n_ss, order[name] + 1)
                act.activation(rt[:, 0:w], ps[:, 4, 0:w], ACT.Sqrt, bias=epsb[:, 0:1], scale=scale).then_inc(n_rt, 1)

            def norm_hi(name, src, dst, ks=range(0, KT, 2)):
                for k in ks:
                    act.wait_ge(n_h, nh_of(name, k + 2))
                    act.activation(dst[:, k:k + 2], src(k), ACT.Copy).then_inc(n_hi, 1)

            def of(buf):
                return lambda k: buf[:, k:k + 2]

            def x_square(k, j, buf):
                def body():
                    act.wait_ge(evac, k + 1)
                    square(buf[:, 2 * j:2 * j + 2], x[:, 2 * j:2 * j + 2])
                return body

            def attn_hi(l, h):
                act.wait_ge(ov_mm, HEADS * l + h + 1)
                act.activation(a_hi[:, HT * h:HT * h + 2, 0:SEQ], ps[:, 2 + h % 2, :].rearrange(
                    "p (a t) -> p a t", a=2), ACT.Copy).then_inc(at_hi, 1)

            act.wait_ge(consts, 4)
            load_table(ACT.Sqrt)
            for j in range(4):
                act.wait_ge(s_mem[j // 2], 16)
                square(sq[:, 2 * j:2 * j + 2, 0:MEM], memn[:, 2 * j:2 * j + 2])
            hi(0, 0, 0)
            hi(0, 0, 1)
            root("mem", 1.0 / D)
            norm_hi("m0", lambda k: hf[:, k:k + 2, 0:MEM], m_hi)
            act.wait_ge(s_x, 16)
            for j in range(4):
                square(sq_x[:, 2 * j:2 * j + 2], x[:, 2 * j:2 * j + 2])
            hi(0, 1, 0)
            hi(0, 1, 1)
            for l in range(DEPTH):
                L = LAYER0[l]
                P = pk[:, l, :]
                step(0, L + K_A, lambda: root(f"mix{l}", 1.0 / D))
                norm_hi(f"mix{l}", of(hf), a_hi)
                step(0, L + K_A + 1)

                def sigmoids(t0):
                    def body():
                        for t in (t0, t0 + 1):
                            act.wait_ge(gates_mm, G * l + t + 1)
                            act.activation(rg[:, t], ps[:, 4 + 2 * (t % 2), 0:T], ACT.Sigmoid,
                                           bias=P[:, PK["b_a"] + t:PK["b_a"] + t + 1]).then_inc(gates_act, 1)
                            act.activation(ig[:, t], ps[:, 5 + 2 * (t % 2), 0:T], ACT.Sigmoid,
                                           bias=P[:, PK["b_x"] + t:PK["b_x"] + t + 1]).then_inc(gates_act, 1)
                    return body

                def decay():
                    act.wait_ge(gates_act, 2 * G * (l + 1))
                    act.wait_ge(sp_ready, 2)
                    for t in range(G):
                        act.activation(av[:, t], rg[:, t], ACT.Exp, scale=nsp[:, l, 0, t:t + 1])
                        act.activation(th[:, t], rg[:, t], ACT.Tanh, scale=nsp[:, l, 1, t:t + 1]).then_inc(gate_a, 1)

                def lru_root():
                    act.wait_ge(u_w, 2 * l + 1)
                    act.activation(th[:], th[:], ACT.Sqrt).then_inc(u_sq, 1)

                def gelu():
                    act.wait_ge(evac, L + IN + 8)
                    act.activation(z[:, ZG:ZG + G], z[:, ZG:ZG + G], ACT.Gelu_apprx_tanh).then_inc(gelu_done, 1)
                    load_table(ACT.Sqrt)

                def softplus_exp():
                    act.wait_ge(sp_in, 1)
                    act.activation(spt[:, 1], spt[:, 0], ACT.Exp, scale=-1.0).then_inc(sp_exp, 1)

                do = {2: softplus_exp if l == 0 else None, 5: sigmoids(0), 6: sigmoids(2), 7: decay, 8: gelu}
                for j in range(10):
                    step(0, L + IN + j, do.get(j))

                def ya_square():
                    act.wait_ge(ya_done, l + 1)
                    square(xc[:], z[:, ZX:ZX + G])

                def yb_square():
                    root(f"co{l}", 1.0 / 512)
                    act.wait_ge(u_w, 2 * l + 2)
                    square(ig[:], hs[:])

                def group_roots():
                    norm_hi(f"g{l}", lambda k: z[:, ZX + k:ZX + k + 2], a_hi, (0, 2))
                    root(f"lo{l}", 1.0 / 512)

                step(0, L + V, lru_root, True)
                step(0, L + V + 1, ya_square, True)
                step(0, L + V + 2, yb_square)
                step(0, L + V + 3, group_roots)
                norm_hi(f"g{l}", lambda k: hs[:, k - G:k - G + 2], a_hi, (4, 6))
                step(0, L + K_B)
                for j in range(4):
                    step(0, L + MIX + j, x_square(L + MIX + j, j, sq))
                root(f"xattn{l}", 1.0 / D)
                load_table(ACT.Exp)
                norm_hi(f"xattn{l}", of(hf), a_hi)
                step(0, L + K_C)
                step(0, L + Q)
                step(0, L + Q + 1)
                def exps(h):
                    act.wait_ge(sc_max, HEADS * l + h + 1)
                    for t in range(2):
                        act.activation(pr[h % 2][:, t], ps[:, 4 + h % 2, t * MEM:(t + 1) * MEM], ACT.Exp,
                                       bias=stat[:, 2 * h + t:2 * h + t + 1],
                                       accum_out=stat[:, 16 + 2 * h + t:17 + 2 * h + t]).then_inc(sc_exp, 1)

                exps(0)
                exps(1)
                attn_hi(l, 0)
                exps(2)
                attn_hi(l, 1)
                exps(3)
                act.wait_ge(ss_max, l + 1)
                act.activation(ps_s[:], ps[:, 0, 0:MEM], ACT.Exp, bias=stat[:, 32:33],
                               accum_out=stat[:, 34:35]).then_inc(ss_exp, 1)
                attn_hi(l, 2)
                hi(0, L + O, 0)
                hi(0, L + O, 1)
                attn_hi(l, 3)
                act.wait_ge(sot_mm, 2 * l + 2)
                for g in range(2):
                    act.activation(a_hi[:, :, SEQ + 4 * g:SEQ + 4 * g + 4], sample_out(g), ACT.Copy).then_inc(at_hi, 1)
                load_table(ACT.Sqrt)
                hi(0, L + O + 1, 0)
                hi(0, L + O + 1, 1)
                for j in range(4):
                    if j < 3 or l == 0:
                        step(0, L + O + j, x_square(L + O + j, j, sq))
                    else:
                        x_square(L + O + 3, 3, sq)()
                root(f"ffn{l}", 1.0 / D)
                norm_hi(f"ffn{l}", of(hf), a_hi)
                if l:
                    step(0, L + O + 3)
                if l == 0:
                    norm_hi("m1", lambda k: hf[:, k:k + 2, 0:MEM], m_hi)
                    act.wait_ge(n_lo, pair_of("m1", 4))

                    def silu(off, k):
                        def body():
                            act.wait_ge(pe_done, off * 2 + (2 * k + 2))
                            act.wait_ge(evac, off + (k - 1))
                            act.activation(sg[k % 2][:], ps[:, 2 * (k % 2), 0:T], ACT.Silu).then_inc(silu_done, 1)
                        return body

                    with act.Fori(0, 5) as i:
                        for u in range(RAWS):
                            step(i * RAWS, GU0 + u, silu(i * RAWS, GU0 + u))
                    for k in range(GU0 + 20, GU0 + 22):
                        step(0, k, silu(0, k))
                    for j in range(8):
                        step(0, DOWN0 + j, x_square(DOWN0 + j, j // 2, sq_d) if j % 2 else None)

            for i in range(6):
                t, half = i // 2, i % 2
                w = TT[t][1]
                for part, dst in enumerate((ht_hi, ht_lo)):
                    act.wait_ge(tk_mm, 2 * i + part + 1)
                    act.activation(dst[0:w, t, half * 512:half * 512 + 512], ps[0:w, 4 + 2 * (i % 2) + part, :],
                                   ACT.Copy).then_inc(tk_cp, 1)

            def gather_hi(n, gs=range(4)):
                for g in gs:
                    act.wait_ge(ga_mm, n * 8 + (2 * g + 1))
                    act.activation(xg_hi[:, 2 * g:2 * g + 2, :], ps[:, 4 + 2 * (g % 2), :].rearrange(
                        "p (a c) -> p a c", a=2), ACT.Copy).then_inc(ga_hi, 1)

            gather_hi(0)
            act.wait_ge(g_in, 1)
            act.activation(gt[:, :, 1], gt[:, :, 0], ACT.Exp).then_inc(g_exp, 1)
            load_table(ACT.Silu)
            act.wait_ge(route, 1)
            rounds = act.value_load(cnt_i[0:1, 0:1], min_val=1, max_val=3)
            with act.Fori(0, rounds) as r:
                with act.Fori(0, 4) as p:
                    it = r * 4 + p
                    off = r * 96 + p * 24

                    def hidden_hi(e):
                        for b in range(3):
                            w = 512 if b < 2 else 384
                            act.wait_ge(hx_mm, it * 6 + (3 * e + b + 1))
                            act.activation(hx_hi[e][:, 4 * b:4 * b + w // 128].rearrange("p a c -> p (a c)"),
                                           ps[:, 4 + b, 0:w], ACT.Copy).then_inc(hx_h, 1)

                    for e in range(2):
                        for q in range(4):
                            k = MOE0 + 8 * e + 2 * q

                            def silu_q():
                                act.wait_ge(pe_done, off * 2 + (2 * k + 2))
                                act.wait_ge(evac, off + (k - 2))
                                act.activation(sgm[:, q % 2], ps[:, k % 4, 0:GQ], ACT.Silu).then_inc(m_silu, 1)
                                if e and q == 0:
                                    hidden_hi(0)

                            step(off, k, silu_q)
                            step(off, k + 1)
                    for e in range(2):
                        for q in range(4):
                            k = MOE0 + 16 + 4 * e + q

                            def scaled_hi():
                                act.wait_ge(pe_done, off * 2 + (2 * k + 2))
                                if e == 0 and q == 0:
                                    act.wait_ge(gs_cp, it + 1)
                                act.activation(y_part(a_hi, e, q), ps[:, k % 4, 0:DQ], ACT.Copy,
                                               scale=gs[:, e:e + 1]).then_inc(y_h, 1)
                                if e == 0 and q == 0:
                                    hidden_hi(1)
                                if 2 <= 4 * e + q < 6:
                                    gather_hi(it + 1, (4 * e + q - 2,))

                            step(off, k, scaled_hi)
            load_table(ACT.Sqrt)
            act.wait_ge(scat_add, rounds * 32 + 1)
            for j in range(4):
                square(sq[:, 2 * j:2 * j + 2], x[:, 2 * j:2 * j + 2])
            root("fin", 1.0 / D)

        @block.vector
        def _(dve):
            chain = Chain(dve, dve_c)

            def col(l, name, i):
                c = PK[name] + i
                return pk[:, l, c:c + 1]

            def lo(off, k, s):
                c, w = halves(k)[s]
                m = 2 * k + s
                dve.wait_ge(hi_done, off * 2 + (m + 1))
                dve.tensor_tensor(wlo[m % 4][:, 0:w], raw[:, k % RAWS, c:c + w], whi[m % 4][:, 0:w].bitcast(f32),
                                  ALU.subtract).then_inc(lo_done, 1)

            def banks(k, w):
                b = 2 * (k % 2)
                return ps[:, b:b + 2, 0:w]

            def step(off, k, read, extra=None, first=None, split=True, late=False):
                if first:
                    first()
                if split and not late:
                    lo(off, k + 2, 0)
                dve.wait_ge(pe_done, off * 2 + (2 * k + 2))
                read().then_inc(evac, 1)
                if extra:
                    dve.wait_ge(evac, off + (k + 1))
                    extra()
                if late:
                    lo(off, k + 2, 0)
                if split:
                    lo(off, k + 2, 1)

            def root_reciprocal(name, w=T):
                dve.wait_ge(n_rt, order[name] + 1)
                chain.wait()
                chain(dve.reciprocal(rstd[:, 0:w], rt[:, 0:w]))
                chain.wait()

            def lo_pair(name, j, src, dst_hi, dst_lo):
                dve.wait_ge(n_hi, pair_of(name, j + 1))
                dve.tensor_tensor(dst_lo[:, 2 * j:2 * j + 2], src, dst_hi[:, 2 * j:2 * j + 2].bitcast(f32),
                                  ALU.subtract).then_inc(n_lo, 1)

            def norm(name, gain, l):
                root_reciprocal(name)
                if name != "fin":
                    dve.wait_ge(n_lo, pair_of(name, 0))
                for k in range(KT):
                    dve.scalar_tensor_tensor(out=hf[:, k], in0=x[:, k], scalar=col(l, gain, k), in1=rstd[:],
                                             op0=ALU.mult, op1=ALU.mult).then_inc(n_h, 1)
                    if k in (3, 5, 7) and name != "fin":
                        j = (k - 3) // 2
                        lo_pair(name, j, hf[:, 2 * j:2 * j + 2], a_hi, a_lo)
                if name != "fin":
                    lo_pair(name, 3, hf[:, 6:8], a_hi, a_lo)

            def mem_operand(l):
                if l:
                    dve.wait_ge(n_lo, pair_of("m1", 0))
                for k in range(KT):
                    dve.scalar_tensor_tensor(out=hf[:, k, 0:MEM], in0=memn[:, k], scalar=col(l, "g_mem", k),
                                             in1=rstm[:], op0=ALU.mult, op1=ALU.mult).then_inc(n_h, 1)
                    if k in (3, 5, 7):
                        j = (k - 3) // 2
                        lo_pair(f"m{l}", j, hf[:, 2 * j:2 * j + 2, 0:MEM], m_hi, m_lo)
                lo_pair(f"m{l}", 3, hf[:, 6:8, 0:MEM], m_hi, m_lo)

            dve.wait_ge(s_par, 16)
            lam = pk[:, :, PK["lam"]:PK["lam"] + G]
            dve.scalar_tensor_tensor(out=spt[:, 0], in0=lam, scalar=-1.0, in1=lam, op0=ALU.mult,
                                     op1=ALU.max).then_inc(sp_in, 1)

            lo(0, 0, 0)
            lo(0, 0, 1)
            dve.wait_ge(n_rt, order["mem"] + 1)
            chain(dve.reciprocal(rstm[:], rt[:, 0:MEM]))
            chain.wait()
            mem_operand(0)
            lo(0, 1, 0)
            lo(0, 1, 1)

            def softplus():
                dve.wait_ge(sp_exp, 1)
                chain(dve.tensor_scalar(spt[:, 2], spt[:, 1], 2.0, None, ALU.add))
                chain.wait()
                chain(dve.reciprocal(spt[:, 3], spt[:, 2]))
                chain.wait()
                chain(dve.tensor_tensor(spt[:, 0], spt[:, 1], spt[:, 3], ALU.mult))
                chain.wait()
                chain(dve.tensor_tensor(spt[:, 1], spt[:, 0], spt[:, 0], ALU.mult))
                chain.wait()
                chain(dve.tensor_scalar(spt[:, 2], spt[:, 1], 1.0 / 19, None, ALU.mult))
                for c in range(17, 1, -2):
                    chain.wait()
                    chain(dve.scalar_tensor_tensor(out=spt[:, 2], in0=spt[:, 2], scalar=1.0 / c, in1=spt[:, 1],
                                                   op0=ALU.add, op1=ALU.mult))
                chain.wait()
                chain(dve.scalar_tensor_tensor(out=spt[:, 2], in0=spt[:, 2], scalar=1.0, in1=spt[:, 0],
                                               op0=ALU.add, op1=ALU.mult))
                chain(dve.tensor_scalar(spt[:, 3], lam, -1.0, 0.0, ALU.mult, ALU.max))
                chain.wait()
                chain(dve.scalar_tensor_tensor(out=spt[:, 2], in0=spt[:, 2], scalar=2.0, in1=spt[:, 3],
                                               op0=ALU.mult, op1=ALU.add))
                chain.wait()
                for i, c in enumerate((-8.0, 8.0)):
                    dve.tensor_scalar(nsp[:, :, i, :], spt[:, 2], c, None, ALU.mult).then_inc(sp_ready, 1)

            for l in range(DEPTH):
                L = LAYER0[l]
                st_lc = pk[:, l, PK["st_lc"]:PK["st_lc"] + 96].rearrange("p (t k) -> p t k", t=G)
                st_sc = pk[:, l, PK["st_sc"]:PK["st_sc"] + 64].rearrange("p (t k) -> p t k", t=G)
                st_h = pk[:, l, PK["st_h"]:PK["st_h"] + 32].rearrange("p (t k) -> p t k", t=G)

                def keys(j, k, **kw):
                    step(0, k, lambda: dve.tensor_copy(kt[:, 2 * j:2 * j + 2], banks(k, MEM)), **kw)

                keys(0, L + K_A)
                norm(f"mix{l}", "g_mix", l)
                keys(1, L + K_A + 1)

                def small(name, w, src, shift=0):
                    c = OC[name] + shift
                    return dve.tensor_copy(sml[:, :, c:c + w], src)

                def conv_tap(dst, src, name, state, taps, tap):
                    chain.wait()
                    s = taps - 1 - tap
                    for t in range(G):
                        w = col(l, name, 4 * tap + t)
                        chain(dve.scalar_tensor_tensor(out=dst[:, t, s:SEQ], in0=src[:, t, 0:SEQ - s], scalar=w,
                                                       in1=dst[:, t, s:SEQ], op0=ALU.mult, op1=ALU.add))
                        c = 8 * tap
                        chain(dve.scalar_tensor_tensor(out=dst[:, t, SEQ:T], in0=state[:, t, c:c + 8], scalar=w,
                                                       in1=dst[:, t, SEQ:T], op0=ALU.mult, op1=ALU.add))

                xl, cx, sc = z[:, ZL:ZL + G], z[:, ZC:ZC + G], z[:, ZX:ZX + G]

                def lru_conv_base():
                    for t in range(G):
                        chain(dve.tensor_scalar(xc[:, t], xl[:, t], col(l, "w_lc", 12 + t), col(l, "b_lc", t),
                                                ALU.mult, ALU.add))
                    conv_tap(xc, xl, "w_lc", st_lc, 4, 2)

                def lru_conv_end():
                    conv_tap(xc, xl, "w_lc", st_lc, 4, 0)
                    chain.wait()
                    if l:
                        dve.wait_ge(s_small, 16)
                    small("p_lc", 3, z[:, ZL:ZL + G, SEQ - 3:SEQ]).then_inc(xc_done, 1)

                def lru_states():
                    chain(small("s_lc", 16, st_lc[:, :, 8:24]))
                    chain(small("s_lc", 8, z[:, ZL:ZL + G, SEQ:T], 16))
                    chain(small("s_sc", 8, st_sc[:, :, 8:16]))

                def lru_input():
                    dve.wait_ge(gate_a, G * (l + 1))
                    chain(dve.tensor_tensor(rg[:], av[:], av[:], ALU.mult))
                    chain.wait()
                    dve.scalar_tensor_tensor(out=th[:], in0=rg[:], scalar=1.0, in1=th[:], op0=ALU.add,
                                             op1=ALU.mult).then_inc(u_w, 1)

                def short_conv():
                    dve.wait_ge(cx_done, l + 1)
                    for t in range(G):
                        chain(dve.tensor_scalar(sc[:, t], cx[:, t], col(l, "w_sc", 8 + t), None, ALU.mult))
                    conv_tap(sc, cx, "w_sc", st_sc, 3, 1)

                def short_conv_end():
                    conv_tap(sc, cx, "w_sc", st_sc, 3, 0)
                    chain.wait()
                    chain(small("p_sc", 2, z[:, ZC:ZC + G, SEQ - 2:SEQ]))
                    small("s_sc", 8, z[:, ZC:ZC + G, SEQ:T], 8).then_inc(sc_done, 1)

                def recurrence():
                    dve.wait_ge(u_sq, l + 1)
                    dve.wait_ge(iu_done, l + 1)
                    dve.wait_ge(sc_done, l + 1)
                    chain(dve.tensor_tensor(ig[:], ig[:], th[:], ALU.mult))
                    chain(dve.tensor_tensor(hs[:, :, SEQ:T], av[:, :, SEQ:T], st_h, ALU.mult))
                    chain.wait()
                    for t in range(G):
                        chain(dve.tensor_tensor_scan(hs[:, t, 0:SEQ], av[:, t, 0:SEQ], ig[:, t, 0:SEQ], 0.0,
                                                     ALU.mult, ALU.add))
                    chain(dve.tensor_tensor(hs[:, :, SEQ:T], hs[:, :, SEQ:T], ig[:, :, SEQ:T], ALU.add))
                    chain.wait()
                    chain(small("p_h", 1, hs[:, :, SEQ - 1:SEQ]))
                    small("s_h", 8, hs[:, :, SEQ:T]).then_inc(sm_done, 1)
                    dve.wait_ge(gelu_done, l + 1)
                    dve.wait_ge(sm_done, l + 1)
                    chain.wait()
                    dve.tensor_tensor(hs[:], hs[:], z[:, ZG:ZG + G], ALU.mult).then_inc(u_w, 1)

                def group_norm(name, src, gain):
                    root_reciprocal(name)
                    for k in range(G):
                        dve.scalar_tensor_tensor(out=src[:, k], in0=src[:, k], scalar=col(l, gain, k), in1=rstd[:],
                                                 op0=ALU.mult, op1=ALU.mult).then_inc(n_h, 1)

                extras = {1: lru_conv_base, 2: lambda: conv_tap(xc, xl, "w_lc", st_lc, 4, 1), 3: lru_conv_end,
                          4: lru_states, 5: softplus if l == 0 else None, 7: short_conv,
                          8: short_conv_end, 9: lru_input}
                for j in range(10):
                    step(0, L + IN + j, lambda: dve.tensor_copy(z[:, 2 * j:2 * j + 2, :], banks(L + IN + j, T)),
                         extras.get(j))

                def value(j, **kw):
                    step(0, L + V + j, lambda: dve.tensor_copy(vt[:, :, j * 256:j * 256 + 256],
                                                                banks(L + V + j, 256)), **kw)

                def lru_norm():
                    for j in range(2):
                        lo_pair(f"g{l}", j, z[:, ZX + 2 * j:ZX + 2 * j + 2], a_hi, a_lo)
                    group_norm(f"lo{l}", hs, "g_lo")

                def lru_lo():
                    for j in range(2):
                        lo_pair(f"g{l}", 2 + j, hs[:, 2 * j:2 * j + 2], a_hi, a_lo)

                value(0, extra=recurrence)
                value(1)
                value(2)
                group_norm(f"co{l}", sc, "g_co")
                value(3, first=lru_norm)
                lru_lo()
                keys(2, L + K_B)

                def add_x(k, j):
                    return dve.tensor_tensor(x[:, 2 * j:2 * j + 2], x[:, 2 * j:2 * j + 2], banks(k, T), ALU.add)

                for j in range(4):
                    step(0, L + MIX + j, lambda: add_x(L + MIX + j, j))
                keys(3, L + K_C, first=lambda: norm(f"xattn{l}", "g_x", l))
                for j in range(4):
                    step(0, L + Q + j, lambda: dve.tensor_scalar(qt[:, 2 * j:2 * j + 2], banks(L + Q + j, T),
                                                                  1.0 / 16, None, ALU.mult), split=j < 2)

                dve.wait_ge(evac, L + O)
                dve.wait_ge(zeros, 2 * l + 1)
                for h in range(HEADS):
                    ins = dve.tensor_copy(
                        qm[:].rearrange("p j b c -> p j (b c)")[:, HT * h:HT * h + HT, 8 * h:8 * h + 232:33],
                        qt[:, HT * h:HT * h + HT, SEQ:T])
                    if h < HEADS - 1:
                        chain(ins)
                ins.then_inc(qm_ready, 1)

                def score_max(h):
                    dve.wait_ge(sc_mm, HEADS * l + h + 1)
                    chain(dve.tensor_reduce(stat[:, 8 + 2 * (h % 2):10 + 2 * (h % 2)],
                                            ps[:, 4 + h % 2, :].rearrange("p (t m) -> p t m", t=2), AX.X, ALU.max))
                    chain.wait()
                    dve.tensor_scalar(stat[:, 2 * h:2 * h + 2], stat[:, 8 + 2 * (h % 2):10 + 2 * (h % 2)], -1.0, None,
                                      ALU.mult).then_inc(sc_max, 1)

                def normalised(h):
                    dve.wait_ge(sc_exp, 2 * (HEADS * l + h) + 2)
                    chain(dve.reciprocal(stat[:, 24 + 2 * h:26 + 2 * h], stat[:, 16 + 2 * h:18 + 2 * h]))
                    chain.wait()
                    for t in range(2):
                        ins = dve.tensor_scalar(pr[h % 2][:, t], pr[h % 2][:, t], stat[:, 24 + 2 * h + t:25 + 2 * h + t],
                                                None, ALU.mult)
                    ins.then_inc(sc_nrm, 1)

                def turned(h):
                    dve.wait_ge(pt_mm, HEADS * l + h + 1)
                    dve.tensor_copy(ptr[h % 2][:], ps[:, 6 + h % 2, :].rearrange("p (m t) -> p m t", m=2))\
                       .then_inc(pt_cp, 1)

                def attn_lo(h):
                    dve.wait_ge(at_hi, 6 * l + h + 1)
                    dve.tensor_tensor(a_lo[:, HT * h:HT * h + 2, 0:SEQ],
                                      ps[:, 2 + h % 2, :].rearrange("p (a t) -> p a t", a=2),
                                      a_hi[:, HT * h:HT * h + 2, 0:SEQ].bitcast(f32), ALU.subtract).then_inc(at_lo, 1)

                score_max(0)
                score_max(1)
                for h in range(2):
                    normalised(h)
                    turned(h)
                    score_max(h + 2)
                    attn_lo(h)
                normalised(2)
                dve.wait_ge(cache_used, CACHES * l + 8)
                chain(dve.tensor_reduce(stat[:, 33:34], ps[:, 0, 0:MEM], AX.X, ALU.max))
                chain.wait()
                dve.tensor_scalar(stat[:, 32:33], stat[:, 33:34], -1.0, None, ALU.mult).then_inc(ss_max, 1)
                turned(2)
                normalised(3)
                dve.wait_ge(ss_exp, l + 1)
                chain(dve.reciprocal(stat[:, 35:36], stat[:, 34:35]))
                chain.wait()
                dve.tensor_scalar(ps_s[:], ps_s[:], stat[:, 35:36], None, ALU.mult).then_inc(ss_nrm, 1)
                dve.wait_ge(zeros, 2 * l + 2)
                dve.wait_ge(st_mm, l + 1)
                for r in range(4):
                    dve.tensor_copy(
                        ptm[:].rearrange("p m h b c -> p (m h) (b c)")[:, :, 33 * r:33 * r + 133:132],
                        ps[:, 1, 0:MEM].rearrange("p (m c) -> p m c", m=MT)[:, :, 33 * r:33 * r + 29:4]
                        .rearrange("p m (h q) -> p m h q", q=2)).then_inc(st_cp, 1)
                attn_lo(2)
                turned(3)
                dve.wait_ge(cache_used, CACHES * l + 16)
                dve.tensor_copy(o_s[:].rearrange("p (b d) -> p b d", b=2), ps[:, 0:2, :]).then_inc(so_cp, 1)
                lo(0, L + O, 0)
                attn_lo(3)
                dve.wait_ge(at_hi, 6 * l + 6)
                for g in range(2):
                    c = SEQ + 4 * g
                    dve.tensor_tensor(a_lo[:, :, c:c + 4], sample_out(g), a_hi[:, :, c:c + 4].bitcast(f32),
                                      ALU.subtract).then_inc(at_lo, 1)

                lo(0, L + O, 1)
                for s in range(2):
                    lo(0, L + O + 1, s)

                for j in range(4):
                    step(0, L + O + j, lambda: add_x(L + O + j, j),
                         (lambda: norm("ffn1", "g_ffn", l)) if l and j == 3 else None, late=bool(l) and j == 3)
                    if l and j == 1:
                        dve.wait_ge(consts, 13)
                        dve.wait_ge(s_rw, 16)
                        chain(dve.tensor_copy(wr_hi[:, :, 0:E], rw[:]))
                        chain(dve.tensor_copy(iot[:], iot_i[:]))
                        chain.wait()
                        dve.tensor_tensor(wr_lo[:, :, 0:E], rw[:], wr_hi[:, :, 0:E].bitcast(f32),
                                          ALU.subtract).then_inc(wr_ready, 1)
                        dve.memset(lt[:], 0.0).then_inc(scat_add, 1)
                if l == 0:
                    norm("ffn0", "g_ffn", 0)
                    mem_operand(1)
                    dve.wait_ge(s_kv, 32)
                    dve.wait_ge(n_lo, pair_of("m1", 4))

                    def gated(off, j, last=False):
                        k = GU0 + j
                        lo(off, k + 2, 0)
                        dve.wait_ge(silu_done, off + (j + 1))
                        dve.tensor_tensor(hff[k % 2][:], sg[k % 2][:], ps[:, 2 * (k % 2) + 1, 0:T],
                                          ALU.mult).then_inc(evac, 1)
                        lo(off, k + 2, 1)
                        dve.wait_ge(evac, off + (k + 1))
                        chain(dve.tensor_copy(h_hi[:, off + j, :], hff[k % 2][:]))
                        chain.wait()
                        ins = dve.tensor_tensor(h_lo[:, off + j, :], hff[k % 2][:], h_hi[:, off + j, :].bitcast(f32),
                                                ALU.subtract)
                        if last:
                            ins.then_inc(ff_h, 1)

                    with dve.Fori(0, 5) as i:
                        chain.off = i * RAWS
                        for u in range(RAWS):
                            gated(i * RAWS, u)
                    chain.off, chain.n = 0, chain.n + 4 * RAWS
                    gated(0, 20)
                    gated(0, 21, True)
                    for j in range(8):
                        k = DOWN0 + j
                        step(0, k, lambda: dve.tensor_tensor(x[:, j, :], x[:, j, :], ps[:, 2 * (k % 2), 0:T], ALU.add))

            dve.wait_ge(scat_add, 1)
            dve.wait_ge(lg_mm, 1)
            dve.tensor_copy(lg[0:E], ps[0:E, 0, 0:T]).then_inc(lg_cp, 1)
            dve.wait_ge(lt_mm, 1)
            chain.wait()
            for i, (c0, w) in enumerate(TT):
                chain(dve.tensor_copy(lt[0:w, i], ps[0:w, 1, i * E:(i + 1) * E]))
            chain.wait()
            for i in range(3):
                chain(dve.max(top[:, i], lt[:, i]))
            chain.wait()
            for i in range(3):
                chain(dve.max_index(topi[:, i], top[:, i], lt[:, i]))
            dve.tensor_tensor(gt[:, :, 0], top[:, :, 1], top[:, :, 0], ALU.subtract).then_inc(g_in, 1)
            chain.wait()
            chain(dve.tensor_copy(topf[:], topi[:]))
            chain.wait()
            numbers = iot[:, 0:E].unsqueeze(1).to_broadcast([128, 3, E])
            for c, m in ((0, m1), (1, m2)):
                chain(dve.tensor_tensor(m[:], numbers, topf[:, :, c:c + 1].to_broadcast([128, 3, E]), ALU.is_equal))
            chain.wait()
            for m in (m1, m2):
                chain(dve.tensor_tensor(m[:], m[:], valid[:], ALU.mult))
            chain.wait()
            dve.tensor_tensor(msk[:], m1[:], m2[:], ALU.add).then_inc(rk_in, 1)
            dve.wait_ge(rk_mm, 1)
            chain(dve.scalar_tensor_tensor(out=rk[:, :, 3], in0=ps[:, 2, 0:3 * E].rearrange("p (i e) -> p i e", i=3),
                                           scalar=1.0, in1=msk[:], op0=ALU.add, op1=ALU.mult))
            chain.wait()
            chain(dve.tensor_reduce(cnt[:, 0:1], ps[:, 3, 0:E], AX.X, ALU.max))
            for r in range(4):
                chain(dve.tensor_scalar(rk[:, :, r], rk[:, :, 3], -1.0 - 128 * r, None, ALU.add))
            chain.wait()
            rks = rk[:].rearrange("p i r e -> p i (r e)")

            def one_hots(n):
                for i in range(3):
                    for e in range(2):
                        c = slice(2 * n + e, 2 * n + e + 1) if isinstance(n, int) else bass.ds(n * 2 + e, 1)
                        ins = dve.tensor_scalar(oh[:, i, 128 * e:128 * e + 128], iot[:], rks[:, i, c], None,
                                                ALU.is_equal)
                ins.then_inc(oh_ready, 1)

            def gather_lo(n, gs=range(4)):
                for g in gs:
                    dve.wait_ge(ga_mm, n * 8 + (2 * g + 2))
                    dve.tensor_copy(xg_lo[:, 2 * g:2 * g + 2, :],
                                    ps[:, 5 + 2 * (g % 2), :].rearrange("p (a c) -> p a c", a=2)).then_inc(ga_lo, 1)

            one_hots(0)
            chain(dve.tensor_scalar(cnt[:, 1:2], cnt[:, 0:1], 128.5, 1.0, ALU.is_gt, ALU.add))
            chain(dve.tensor_scalar(cnt[:, 2:3], cnt[:, 0:1], 256.5, None, ALU.is_gt))
            chain.wait()
            dve.tensor_tensor(cnt_i[:, 0:1], cnt[:, 1:2], cnt[:, 2:3], ALU.add).then_inc(route, 1)
            gather_lo(0)
            dve.wait_ge(g_exp, 1)
            chain(dve.tensor_scalar(gt[:, :, 2], gt[:, :, 1], 1.0, None, ALU.add))
            chain.wait()
            chain(dve.reciprocal(gt[:, :, 3], gt[:, :, 2]))
            chain.wait()
            chain(dve.tensor_tensor(gt[:, :, 2], gt[:, :, 1], gt[:, :, 3], ALU.mult))
            chain.wait()
            chain(dve.tensor_tensor(m1[:], m1[:], gt[:, :, 3:4].to_broadcast([128, 3, E]), ALU.mult))
            chain(dve.tensor_tensor(m2[:], m2[:], gt[:, :, 2:3].to_broadcast([128, 3, E]), ALU.mult))
            chain.wait()
            chain(dve.tensor_tensor(comb[:, :, 0:E], m1[:], m2[:], ALU.add))
            chain.wait()
            dve.tensor_copy(comb[:, :, E:E + 2], comb[:, :, 0:2]).then_inc(comb_ready, 1)
            dve.wait_ge(route, 1)

            rounds = dve.value_load(cnt_i[0:1, 0:1], min_val=1, max_val=3)
            with dve.Fori(0, rounds) as r:
                with dve.Fori(0, 4) as p:
                    it = r * 4 + p
                    off = r * 96 + p * 24

                    def hidden_lo(e):
                        for b in range(3):
                            w = 512 if b < 2 else 384
                            dve.wait_ge(hx_h, it * 6 + (3 * e + b + 1))
                            dve.tensor_tensor(hx_lo[e][:, 4 * b:4 * b + w // 128].rearrange("p a c -> p (a c)"),
                                              ps[:, 4 + b, 0:w],
                                              hx_hi[e][:, 4 * b:4 * b + w // 128].rearrange("p a c -> p (a c)")
                                              .bitcast(f32), ALU.subtract).then_inc(hx_l, 1)

                    def scattered(f0, f1):
                        for f in range(f0, f1):
                            dve.wait_ge(scat_mm, it * 8 + (f + 1))
                            dve.tensor_tensor(x[:, f], x[:, f], ps[:, 4 + f % 4, 0:T], ALU.add).then_inc(scat_add, 1)

                    for e in range(2):
                        for q in range(4):
                            k = MOE0 + 8 * e + 2 * q
                            lo(off, k + 2, 0)
                            lo(off, k + 2, 1)
                            lo(off, k + 3, 0)
                            dve.wait_ge(m_silu, it * 8 + (4 * e + q + 1))
                            dve.wait_ge(pe_done, off * 2 + (2 * k + 4))
                            dve.tensor_tensor(hm[:, q * GQ:(q + 1) * GQ], sgm[:, q % 2], ps[:, (k + 1) % 4, 0:GQ],
                                              ALU.mult).then_inc(evac, 2)
                            lo(off, k + 3, 1)
                            if e == 0 and q == 0:
                                for u in range(2):
                                    dve.wait_ge(oht_mm, it * 2 + (u + 1))
                                    dve.tensor_copy(oht[:, u], ps[:, 6 + u, 0:T]).then_inc(oht_cp, 1)
                                dve.wait_ge(gs_mm, it + 1)
                                for u in range(2):
                                    ins = dve.tensor_copy(gs[:, u:u + 1],
                                                          ps[:, 4, bass.ds(p * 2 + ((E + 2) * u + u), 1)])
                                ins.then_inc(gs_cp, 1)
                                one_hots(it + 1)
                            if e and q == 0:
                                hidden_lo(0)
                    for e in range(2):
                        for q in range(4):
                            k = MOE0 + 16 + 4 * e + q
                            lo(off, k + 2, 0)
                            dve.wait_ge(y_h, it * 8 + (4 * e + q + 1))
                            dve.scalar_tensor_tensor(out=y_part(a_lo, e, q), in0=ps[:, k % 4, 0:DQ],
                                                     scalar=gs[:, e:e + 1], in1=y_part(a_hi, e, q).bitcast(f32),
                                                     op0=ALU.mult, op1=ALU.subtract).then_inc(evac, 1)
                            if 2 <= 4 * e + q < 6:
                                gather_lo(it + 1, (4 * e + q - 2,))
                            lo(off, k + 2, 1)
                            if e and q >= 2:
                                scattered(4 * (q - 2), 4 * (q - 1))
                            if e == 0 and q == 0:
                                hidden_lo(1)
            norm("fin", "g_fin", 0)

        @block.tensor
        def _(pe):
            def mm3(out, w_hi, w_lo, m_hi_, m_lo_, first, last):
                pe.matmul(out, w_hi, m_hi_, start=first, stop=False)
                pe.matmul(out, w_hi, m_lo_, start=False, stop=False)
                return pe.matmul(out, w_lo, m_hi_, start=False, stop=last)

            def chunk(off, k, body):
                if not isinstance(off, int) or k >= 2:
                    pe.wait_ge(evac, off + (k - 1))
                for s in range(2):
                    pe.wait_ge(lo_done, off * 2 + (2 * k + s + 1))
                    body(k, s).then_inc(pe_done, 1)

            def chunks(k0, count, body):
                with pe.Fori(0, count // 2) as i:
                    for u in range(2):
                        chunk(i * 2, k0 + u, body)

            def slab(k, s, i, m_h, m_l, w):
                h = (2 * k + s) % 4
                c = i * 128
                return mm3(ps[:, 2 * (k % 2) + s, 0:w], whi[h][:, c:c + 128], wlo[h][:, c:c + 128],
                           m_h[:, i, :], m_l[:, i, :], i == 0, i == KT - 1)

            def proj(m_h, m_l, w, beside=None):
                def body(k, s):
                    for i in range(KT):
                        if beside and s == 0 and i == 4:
                            beside()
                        last = slab(k, s, i, m_h, m_l, w)
                    return last
                return body

            def first_chunk(k, name, m_h, m_l, w):
                pe.wait_ge(lo_done, 2 * k + 2)
                if k >= 2:
                    pe.wait_ge(evac, k - 1)
                for p in range(4):
                    pe.wait_ge(n_lo, pair_of(name, p + 1))
                    for s in range(2):
                        for i in (2 * p, 2 * p + 1):
                            last = slab(k, s, i, m_h, m_l, w)
                        if p == 3:
                            last.then_inc(pe_done, 1)

            def values(k, s):
                h = (2 * k + s) % 4
                for t in range(MT):
                    for i in range(4 * s, 4 * s + 4):
                        m = slice(t * 128, t * 128 + 128)
                        w = slice((i - 4 * s) * 256, (i - 4 * s) * 256 + 256)
                        last = mm3(ps[:, 2 * (k % 2) + t, 0:256], m_hi[:, i, m], m_lo[:, i, m],
                                   whi[h][:, w], wlo[h][:, w], i == 0, i == KT - 1)
                return last

            def down(k, s):
                h = (2 * k + s) % 4
                for i in range(11 * s, 11 * s + 11):
                    if k == DOWN0 and i == FFT - 2:
                        pe.wait_ge(ff_h, 1)
                    c = (i - 11 * s) * 128
                    last = mm3(ps[:, 2 * (k % 2), 0:T], whi[h][:, c:c + 128], wlo[h][:, c:c + 128],
                               h_hi[:, i, :], h_lo[:, i, :], i == 0, i == FFT - 1)
                return last

            def sum_pair(name, src, j, pairs=4, w=T):
                pe.wait_ge(n_sq, sq_of(name, j + 1))
                if j == 0 and order[name]:
                    pe.wait_ge(n_rt, order[name])
                for i in (2 * j, 2 * j + 1):
                    last = pe.matmul(ps[:, 4, 0:w], ones[:], src[:, i, 0:w], start=i == 0, stop=i == 2 * pairs - 1)
                if j == pairs - 1:
                    last.then_inc(n_ss, 1)

            def folded_sum(name, src):
                pe.wait_ge(n_fold, FOLDED.index(name) + 1)
                pe.wait_ge(n_rt, order[name])
                pe.matmul(ps[:, 4, 0:T], ones[:], src[:, 0], start=True, stop=False)
                pe.wait_ge(n_sq, sq_of(name, 4))
                pe.matmul(ps[:, 4, 0:T], ones[:], src[:, 6], start=False, stop=False)
                pe.matmul(ps[:, 4, 0:T], ones[:], src[:, 7], start=False, stop=True).then_inc(n_ss, 1)

            def group_sum(name, src):
                pe.wait_ge(n_fold, FOLDED.index(name) + 1)
                pe.wait_ge(n_rt, order[name])
                pe.matmul(ps[:, 4, 0:T], ones[:], src[:, 0], start=True, stop=True).then_inc(n_ss, 1)

            pe.wait_ge(consts, 4)
            for j in range(4):
                sum_pair("mem", sq, j, w=MEM)
            for l in range(DEPTH):
                L = LAYER0[l]
                by_a = proj(a_hi, a_lo, T)
                by_m = proj(m_hi, m_lo, MEM)

                def gates(t):
                    if t >= 2:
                        pe.wait_ge(gates_act, 2 * G * l + 2 * t - 2)
                    for m in range(2):
                        last = pe.matmul(ps[:, 4 + 2 * (t % 2) + m, 0:T], lru_w[:, m, t], xc[:, t], start=True, stop=True)
                    last.then_inc(gates_mm, 1)

                def beside_v(fn):
                    def body(k, s):
                        if s == 1:
                            fn()
                        return values(k, s)
                    return body

                if l == 0:
                    first_chunk(L + K_A, "m0", m_hi, m_lo, MEM)
                    for j in range(4):
                        sum_pair("mix0", sq_x, j)
                else:
                    pe.wait_ge(n_lo, pair_of("m1", 4))
                    chunk(0, L + K_A, proj(m_hi, m_lo, MEM, lambda: folded_sum("mix1", sq_d)))
                chunk(0, L + K_A + 1, by_m)
                first_chunk(L + IN, f"mix{l}", a_hi, a_lo, T)
                chunks(L + IN + 1, 4, by_a)
                pe.wait_ge(s_lruw, 64 * (l + 1))
                pe.wait_ge(xc_done, l + 1)
                gates(0)
                gates(1)
                chunk(0, L + IN + 5, by_a)
                gates(2)
                gates(3)
                chunks(L + IN + 6, 4, by_a)
                chunk(0, L + V, values)
                chunk(0, L + V + 1, values)
                chunk(0, L + V + 2, beside_v(lambda: group_sum(f"co{l}", xc)))
                chunk(0, L + V + 3, beside_v(lambda: group_sum(f"lo{l}", ig)))
                chunk(0, L + K_B, by_m)
                first_chunk(L + MIX, f"g{l}", a_hi, a_lo, T)
                for j in range(1, 4):
                    chunk(0, L + MIX + j, by_a)
                chunk(0, L + K_C, proj(m_hi, m_lo, MEM, lambda: folded_sum(f"xattn{l}", sq)))
                first_chunk(L + Q, f"xattn{l}", a_hi, a_lo, T)
                for j in range(1, 4):
                    chunk(0, L + Q + j, by_a)

                def scores(h):
                    for t in range(2):
                        for d in range(HT):
                            last = pe.matmul(ps[:, 4 + h % 2, t * MEM:(t + 1) * MEM],
                                             qt[:, HT * h + d, t * 128:t * 128 + 128],
                                             kt[:, HT * h + d, :], start=d == 0, stop=d == HT - 1)
                    last.then_inc(sc_mm, 1)

                def cached(c):
                    if c % 8 < 2:
                        pe.wait_ge(spare_full[c % 8], 16 * (2 * l + c // 8 + 1))
                        return spare[:, c % 8]
                    n = cache_place(l, c)
                    pe.wait_ge(raw_full[n % RAWS], 16 * (n // RAWS + 1))
                    return raw[:, n % RAWS]

                def sample_scores(b0):
                    keys = [cached(b0), cached(b0 + 1)]
                    for j in range(KT):
                        for u in range(2):
                            b = b0 + u
                            g = 32 * (b % 4)
                            last = pe.matmul(ps[g:g + 32, 0, 0:MEM], qm[:, j, b, :],
                                             keys[u][:, j * MEM:(j + 1) * MEM],
                                             start=b < 4 and j == 0, stop=b >= 4 and j == KT - 1)
                            if j == KT - 1:
                                last.then_inc(cache_used, 1)

                def probs_t(h):
                    pe.wait_ge(sc_nrm, HEADS * l + h + 1)
                    for m in range(MT):
                        for t in range(2):
                            last = pe.transpose(ps[:, 6 + h % 2, m * SEQ + t * 128:m * SEQ + t * 128 + 128],
                                                pr[h % 2][:, t, m * 128:m * 128 + 128], ident[:])
                    last.then_inc(pt_mm, 1)

                def outputs(h):
                    pe.wait_ge(pt_cp, HEADS * l + h + 1)
                    if h >= 2:
                        pe.wait_ge(at_lo, 6 * l + h - 1)
                    for d in range(HT):
                        for m in range(MT):
                            last = pe.matmul(ps[:, 2 + h % 2, d * SEQ:(d + 1) * SEQ],
                                             vt[:, m, h * 256 + d * 128:h * 256 + d * 128 + 128], ptr[h % 2][:, m],
                                             start=m == 0, stop=m == MT - 1)
                    last.then_inc(ov_mm, 1)

                def sample_outputs(b0):
                    vals = [cached(DEC + b0), cached(DEC + b0 + 1)]
                    for h in range(HEADS):
                        for m in range(MT):
                            for u in range(2):
                                b = b0 + u
                                g = 32 * (b % 4)
                                o = m * D + h * 256
                                last = pe.matmul(ps[g:g + 32, h // 2, (h % 2) * 256:(h % 2) * 256 + 256],
                                                 ptm[:, m, h, b, :], vals[u][:, o:o + 256],
                                                 start=b < 4 and m == 0 and h % 2 == 0, stop=b >= 4 and m == MT - 1,
                                                 skip_group_check=True)
                                if h == HEADS - 1 and m == MT - 1:
                                    last.then_inc(cache_used, 1)

                pe.wait_ge(evac, L + O)
                scores(0)
                scores(1)
                pe.wait_ge(qm_ready, l + 1)
                sample_scores(0)
                sample_scores(2)
                probs_t(0)
                scores(2)
                outputs(0)
                sample_scores(4)
                probs_t(1)
                scores(3)
                outputs(1)
                sample_scores(6)
                probs_t(2)
                outputs(2)
                probs_t(3)
                pe.wait_ge(ss_nrm, l + 1)
                for m in range(MT):
                    last = pe.transpose(ps[:, 1, m * 128:m * 128 + 128], ps_s[:, m * 128:m * 128 + 128], ident[:])
                last.then_inc(st_mm, 1)
                pe.wait_ge(st_cp, 4 * l + 4)
                for b0 in range(0, DEC, 2):
                    sample_outputs(b0)
                outputs(3)
                pe.wait_ge(so_cp, l + 1)
                for j in range(KT):
                    last = pe.transpose(ps[:, j // 4, (j % 4) * 128:(j % 4) * 128 + 128],
                                        o_s[:, j * 128:j * 128 + 128], ident[:])
                    if j % 4 == 3:
                        last.then_inc(sot_mm, 1)
                pe.wait_ge(at_lo, 6 * l + 6)
                chunk(0, L + O, by_a)
                for j in range(1, 4):
                    chunk(0, L + O + j, by_a)
                folded_sum(f"ffn{l}", sq)
                if l == 0:
                    first_chunk(GU0, "ffn0", a_hi, a_lo, T)
                    chunks(GU0 + 1, 20, by_a)
                    chunk(0, GU0 + 21, by_a)
                    for j in range(8):
                        chunk(0, DOWN0 + j, down)

            pe.wait_ge(wr_ready, 1)
            pe.wait_ge(evac, MOE0)
            for i in range(KT):
                if i % 2 == 0:
                    pe.wait_ge(n_lo, pair_of("ffn1", i // 2 + 1))
                last = mm3(ps[:, 0, 0:T], wr_hi[:, i], wr_lo[:, i], a_hi[:, i], a_lo[:, i], i == 0, i == KT - 1)
            last.then_inc(lg_mm, 1)

            def token_major(i):
                t, half = i // 2, i % 2
                c0, w = TT[t]
                if i >= 2:
                    pe.wait_ge(tk_cp, 2 * i - 2)
                else:
                    pe.wait_ge(n_rt, order["ffn1"] + 1)
                for part, src in enumerate((a_hi, a_lo)):
                    for f in range(4):
                        last = pe.transpose(ps[0:w, 4 + 2 * (i % 2) + part, f * 128:f * 128 + 128],
                                            src[:, 4 * half + f, c0:c0 + w].bitcast(f32), ident[:])
                    last.then_inc(tk_mm, 1)

            token_major(0)
            pe.wait_ge(lg_cp, 1)
            for i, (c0, w) in enumerate(TT):
                last = pe.transpose(ps[0:w, 1, i * E:(i + 1) * E], lg[0:E, c0:c0 + w], ident[0:E, 0:E])
            last.then_inc(lt_mm, 1)
            for i in range(1, 4):
                token_major(i)
            pe.wait_ge(rk_in, 1)
            for i in range(3):
                for j in range(i + 1):
                    pe.matmul(ps[:, 2, i * E:(i + 1) * E], tri[:] if j == i else one_b[:], msk[:, j],
                              start=j == 0, stop=j == i)
            for j in range(3):
                last = pe.matmul(ps[:, 3, 0:E], one_b[:], msk[:, j], start=j == 0, stop=j == 2)
            last.then_inc(rk_mm, 1)
            token_major(4)
            token_major(5)

            pe.wait_ge(tk_cp, 12)
            ohf = oh[:].bitcast(f32)

            def gather(n, gs=range(4)):
                for g in gs:
                    if g == 0:
                        pe.wait_ge(oh_ready, n + 1)
                    if g >= 2:
                        pe.wait_ge(ga_hi, n * 4 + (g - 1))
                        pe.wait_ge(ga_lo, n * 4 + (g - 1))
                    for part, src in enumerate((ht_hi, ht_lo)):
                        for a in range(2):
                            f = 2 * g + a
                            for i in range(3):
                                last = pe.matmul(ps[:, 4 + 2 * (g % 2) + part, a * 256:a * 256 + 256],
                                                 src[:, i, f * 128:f * 128 + 128], oh[:, i, :],
                                                 start=i == 0, stop=i == 2)
                        last.then_inc(ga_mm, 1)

            gather(0)
            pe.wait_ge(route, 1)
            rounds = pe.value_load(cnt_i[0:1, 0:1], min_val=1, max_val=3)
            with pe.Fori(0, rounds) as r:
                with pe.Fori(0, 4) as p:
                    it = r * 4 + p
                    off = r * 96 + p * 24

                    def expert_chunk(k, body, e):
                        pe.wait_ge(evac, off + (k - 3))
                        for s in range(2):
                            pe.wait_ge(lo_done, off * 2 + (2 * k + s + 1))
                            body(k, s, e).then_inc(pe_done, 1)

                    def gate_up(k, s, e):
                        h = (2 * k + s) % 4
                        t = slice(128 * e, 128 * e + 128)
                        for i in range(4 * s, 4 * s + 4):
                            w = slice((i - 4 * s) * GQ, (i - 4 * s + 1) * GQ)
                            last = mm3(ps[:, k % 4, 0:GQ], xg_hi[:, i, t], xg_lo[:, i, t], whi[h][:, w],
                                       wlo[h][:, w], i == 0, i == KT - 1)
                        return last

                    def down_q(k, s, e):
                        h = (2 * k + s) % 4
                        for i in range(6 * s, 6 + 5 * s):
                            w = slice((i - 6 * s) * DQ, (i - 6 * s + 1) * DQ)
                            last = mm3(ps[:, k % 4, 0:DQ], hx_hi[e][:, i], hx_lo[e][:, i], whi[h][:, w],
                                       wlo[h][:, w], i == 0, i == FET - 1)
                        return last

                    def turn(e):
                        if e:
                            pe.wait_ge(hx_l, it * 6 + 3)
                        else:
                            pe.wait_ge(gs_cp, it + 1)
                            pe.wait_ge(oht_cp, it * 2 + 2)
                        pe.wait_ge(evac, off + (MOE0 + 8 * e + 8))
                        for b in range(3):
                            for a in range(4 if b < 2 else 3):
                                f = 4 * b + a
                                last = pe.transpose(ps[:, 4 + b, a * 128:a * 128 + 128], hm[:, f * 128:f * 128 + 128],
                                                    ident[:])
                            last.then_inc(hx_mm, 1)

                    def scatter(f0, f1):
                        for f in range(f0, f1):
                            if f % 2 == 0:
                                pe.wait_ge(evac, off + (MOE0 + 21 + f // 2))
                            if f >= 4:
                                pe.wait_ge(scat_add, it * 8 + (f - 2))
                            w = slice((f % 2) * 128, (f % 2) * 128 + 128)
                            for e in range(2):
                                for part, y in enumerate((a_hi, a_lo)):
                                    last = pe.matmul(ps[:, 4 + f % 4, 0:T], y_part(y, e, f // 2)[:, w], oht[:, e],
                                                     start=e == 0 and part == 0, stop=e == 1 and part == 1)
                            last.then_inc(scat_mm, 1)

                    pe.wait_ge(ga_hi, it * 4 + 4)
                    pe.wait_ge(ga_lo, it * 4 + 4)
                    for e in range(2):
                        for c in range(8):
                            expert_chunk(MOE0 + 8 * e + c, gate_up, e)
                            if e == 0 and c == 0:
                                pe.wait_ge(comb_ready, 1)
                                pe.wait_ge(scat_add, it * 8 + 1)
                                for u in range(2):
                                    for i in range(3):
                                        last = pe.transpose(ps[:, 6 + u, i * 128:i * 128 + 128],
                                                            ohf[:, i, 128 * u:128 * u + 128], ident[:])
                                    last.then_inc(oht_mm, 1)
                                for u in range(2):
                                    for i in range(3):
                                        last = pe.matmul(ps[:, 4, (E + 2) * u:(E + 2) * u + E + 2],
                                                         ohf[:, i, 128 * u:128 * u + 128], comb[:, i],
                                                         start=i == 0, stop=i == 2)
                                last.then_inc(gs_mm, 1)
                            if e and c == 0:
                                turn(0)
                    for e in range(2):
                        pe.wait_ge(hx_l, it * 6 + (3 * e + 3))
                        for c in range(4):
                            expert_chunk(MOE0 + 16 + 4 * e + c, down_q, e)
                            if e == 0 and c == 0:
                                turn(1)
                            if 2 <= 4 * e + c < 6:
                                if 4 * e + c == 2:
                                    pe.wait_ge(hx_l, it * 6 + 6)
                                gather(it + 1, (4 * e + c - 2,))
                            if e and c == 2:
                                pe.wait_ge(ga_hi, it * 4 + 8)
                                pe.wait_ge(ga_lo, it * 4 + 8)
                                scatter(0, 4)
                    scatter(4, 8)
            for j in range(4):
                sum_pair("fin", sq, j)


def kernel(**inputs):
    import concourse.bacc as bacc
    from concourse.bass_utils import run_bass_kernel_spmd as run

    a = {k: np.asarray(v) for k, v in inputs.items()}
    c = np.ascontiguousarray

    def rows(w, k):
        return w.reshape(*w.shape[:-2], k, 128, w.shape[-1]).swapaxes(-3, -2)

    def dense(w):
        n = w.shape[1] // 256
        return rows(w, KT).reshape(128, KT, n, 256).transpose(2, 0, 1, 3).reshape(n, 128, DW)

    def slabs(w):
        return dense(w).reshape(-1, 128, KT, 2, 128).swapaxes(2, 3).reshape(-1, 128, DW)

    def vec(v):
        v = v.reshape(*v.shape[:-1], v.shape[-1] // 128, 128)
        return np.moveaxis(v, -1, 0)

    x = np.concatenate([a["x_prompt"][0], a["x_sample"][:, 0]], axis=0)
    x_in = c(rows(x.T, KT))
    mem_in = c(rows(a["mem_prompt"][0].T, KT))
    layers, packs = [], []
    for l in range(DEPTH):
        B, C, X, XL, GA = np.split(a["w_in"][l], 5, axis=1)
        w_in = np.concatenate([XL, C, X, GA, B], axis=1)
        w_k = slabs(a["w_k"][l])
        layers.append(np.concatenate([w_k[0:2], slabs(w_in), dense(a["w_v"][l]), w_k[2:3], slabs(a["w_mix_out"][l]),
                                      w_k[3:4], slabs(a["w_q"][l]), slabs(a["w_o"][l])]))
        p = [vec(a["norm_mix"][l]), vec(a["norm_xattn"][l]), vec(a["norm_mem"][l]), vec(a["norm_ffn"][l]),
             vec(a["norm_final"]), vec(a["w_short_conv"][l]), vec(a["w_lru_conv"][l]), vec(a["b_lru_conv"][l]),
             vec(a["b_lru_a"][l]), vec(a["b_lru_x"][l]), vec(a["lru_lambda"][l]), vec(a["norm_conv_out"][l]),
             vec(a["norm_lru_out"][l]),
             vec(a["state_shortconv"][l]).transpose(0, 3, 2, 1), vec(a["state_lru_conv"][l]).transpose(0, 3, 2, 1),
             vec(a["state_lru_h"][l]).transpose(0, 2, 1)]
        packs.append(np.concatenate([q.reshape(128, -1) for q in p], axis=1))
    gate, up = (rows(a[k][0], KT).reshape(128, KT, FFT, 128) for k in ("w_ff_gate", "w_ff_up"))
    gu = np.stack([gate, up], axis=0).transpose(3, 1, 0, 2, 4).reshape(FFT, 128, DW)
    down = rows(a["w_ff_down"][0], FFT).reshape(128, FFT, KT, 128).transpose(2, 0, 1, 3).reshape(KT, 128, CW)
    mg, mu = (rows(a[k][0], KT).reshape(E, 128, KT, 4, GQ).transpose(0, 3, 1, 2, 4).reshape(E, 4, 1, 128, CW)
              for k in ("w_moe_gate", "w_moe_up"))
    md = rows(a["w_moe_down"][0], FET).reshape(E, 128, FET, 4, DQ).transpose(0, 3, 1, 2, 4).reshape(E, 4, 128, CW)
    moe = np.concatenate([np.concatenate([mg, mu], axis=2).reshape(E // 2, 16, 128, CW),
                          md.reshape(E // 2, 8, 128, CW)], axis=1).reshape(E * 12, 128, CW)
    lru = np.stack([a["w_lru_a"], a["w_lru_x"]], axis=1).reshape(DEPTH, 2, G, 2, 64, 64).transpose(0, 1, 3, 4, 2, 5)
    router = rows(a["w_router"][0], KT)
    kc = a["cache_mem_k"].reshape(DEPTH, DEC, MEM, KT, 128).transpose(0, 1, 4, 3, 2).reshape(DEPTH, DEC, 128, DW)
    vc = a["cache_mem_v"].reshape(DEPTH, DEC, MT, 128, D).transpose(0, 1, 3, 2, 4).reshape(DEPTH, DEC, 128, DW)

    ins = dict(x_in=x_in, mem_in=mem_in, pk_in=np.stack(packs, axis=1), dense_in=np.stack(layers), gu_in=gu,
               down_in=down, moe_in=moe, lru_in=lru, router_in=router, cache_in=np.concatenate([kc, vc], axis=1))
    outs = dict(y_out=(128, KT, T), k_out=(DEPTH, 128, KT, MEM), v_out=(DEPTH, 128, MT, D),
                small_out=(DEPTH, 128, G, NOC))
    nc = bacc.Bacc("TRN2", target_bir_lowering=False, num_devices=1)
    ins = {f"{k}_dram": c(v) for k, v in ins.items()}
    aps = [nc.dram_tensor(k, v.shape, mybir.dt.from_np(v.dtype), kind="ExternalInput").ap() for k, v in ins.items()]
    aps += [nc.dram_tensor(k, s, mybir.dt.float32, kind="ExternalOutput").ap() for k, s in outs.items()]
    build(nc, *aps)
    r = run(nc, [ins], core_ids=[0]).results[0]
    y = r["y_out"].transpose(1, 0, 2).reshape(D, T).T
    k_mem = r["k_out"].transpose(0, 3, 2, 1).reshape(DEPTH, 1, MEM, HEADS, 256)
    v_mem = r["v_out"].transpose(0, 2, 1, 3).reshape(DEPTH, 1, MEM, HEADS, 256)
    s = r["small_out"].transpose(0, 3, 2, 1).reshape(DEPTH, NOC, 512)

    def part(name, n):
        return s[:, OC[name]:OC[name] + n]

    return (c(y[None, 0:SEQ]), c(y[SEQ:T, None]), c(part("p_sc", 2)[:, None]), c(part("p_lc", 3)[:, None]),
            c(part("p_h", 1)), c(k_mem), c(v_mem),
            c(part("s_sc", 16).reshape(DEPTH, 2, DEC, 512).swapaxes(1, 2)),
            c(part("s_lc", 24).reshape(DEPTH, 3, DEC, 512).swapaxes(1, 2)), c(part("s_h", 8)))
```
